# Optimizing a Trainium2 kernel written in Bass

```python
import math
import jax, jax.numpy as jnp
from jax import lax
import numpy as np

D_MODEL = 1024
BATCH = 1
SEQ = 512
DEPTH = 2

HEAD_DIM = 64
N_GROUPS = D_MODEL // HEAD_DIM
N_MEM_HEADS = 4
N_MIX_HEADS = N_GROUPS - N_MEM_HEADS
D_MIX = N_MIX_HEADS * HEAD_DIM
D_MEM = N_MEM_HEADS * HEAD_DIM
CHUNK = 128
Q_BLOCK = 128
N_MEM_TOKENS = 256
D_FF = 4 * D_MODEL
N_A_LAYERS = DEPTH - DEPTH // 2
N_B_LAYERS = DEPTH // 2
DN_ALPHA = (2 * DEPTH) ** 0.25
DN_BETA = (8 * DEPTH) ** -0.25
LN_EPS = 1e-5

kernel_name = "yoco_gmlp_fox_memory_hybrid"

def layer_norm(x, g, b):
    xf = x.astype(jnp.float32)
    mu = jnp.mean(xf, axis=-1, keepdims=True)
    var = jnp.mean(jnp.square(xf - mu), axis=-1, keepdims=True)
    y = (xf - mu) * lax.rsqrt(var + LN_EPS)
    return (y * g.astype(jnp.float32) + b.astype(jnp.float32)).astype(x.dtype)

def chunked_sgu(u, v, w_s, b_s):
    bsz, s, g, dh = v.shape
    n_chunks = s // CHUNK
    causal = jnp.tril(jnp.ones((CHUNK, CHUNK), dtype=bool))
    w = jnp.where(causal[None], w_s, jnp.zeros_like(w_s))
    vc = v.reshape(bsz, n_chunks, CHUNK, g, dh)
    mixed = jnp.einsum('gts,bnsgd->bntgd', w, vc) + b_s.T[None, None, :, :, None]
    return u * mixed.reshape(bsz, s, g, dh)

def fox_attention(q, k, v, logcum):
    bsz, s, h, dh = q.shape
    n_blk = s // Q_BLOCK
    scale = 1.0 / math.sqrt(dh)
    qb = q.reshape(bsz, n_blk, Q_BLOCK, h, dh).transpose(1, 0, 2, 3, 4)
    cb = logcum.reshape(bsz, h, n_blk, Q_BLOCK).transpose(2, 0, 1, 3)
    kpos = jnp.arange(s)

    def one_block(args):
        qi, ci, i = args
        sc = jnp.einsum('bqhd,bkhd->bhqk', qi, k).astype(jnp.float32) * scale
        sc = sc + ci[..., None] - logcum[:, :, None, :]
        qpos = i * Q_BLOCK + jnp.arange(Q_BLOCK)
        mask = kpos[None, :] <= qpos[:, None]
        sc = jnp.where(mask[None, None], sc, -jnp.inf)
        p = jax.nn.softmax(sc, axis=-1)
        return jnp.einsum('bhqk,bkhd->bqhd', p.astype(v.dtype), v)

    out = lax.map(one_block, (qb, cb, jnp.arange(n_blk)))
    return out.transpose(1, 0, 2, 3, 4).reshape(bsz, s, h, dh)

def memory_attention(qm, mk, mv):
    scale = 1.0 / math.sqrt(qm.shape[-1])
    sc = jnp.einsum('bshd,bmhd->bhsm', qm, mk).astype(jnp.float32) * scale
    p = jax.nn.softmax(sc, axis=-1)
    out = jnp.einsum('bhsm,bmhd->bshd', p.astype(mv.dtype), mv)
    return out.reshape(qm.shape[0], qm.shape[1], D_MEM)

def sq_relu_mlp(x, w_up, w_down):
    h = jnp.square(jax.nn.relu(x @ w_up))
    return h @ w_down

def setup_inputs(seed: int = 0) -> dict:
    key = jax.random.key(seed)
    ks = jax.random.split(key, 20)
    f32 = jnp.float32
    d = D_MODEL
    nrm = lambda k, shp: jax.random.normal(k, shp, f32)
    x = nrm(ks[0], (BATCH, SEQ, d))
    mem = nrm(ks[1], (BATCH, N_MEM_TOKENS, d))
    a_w_in = nrm(ks[2], (N_A_LAYERS, d, 2 * D_MIX + D_MEM)) * d ** -0.5
    a_sgu_ln_g = 1.0 + 0.02 * nrm(ks[3], (N_A_LAYERS, D_MIX))
    a_sgu_ln_b = 0.02 * nrm(ks[4], (N_A_LAYERS, D_MIX))
    a_w_s = nrm(ks[5], (N_A_LAYERS, N_MIX_HEADS, CHUNK, CHUNK)) * (0.5 * CHUNK ** -0.5)
    a_b_s = 1.0 + 0.02 * nrm(ks[6], (N_A_LAYERS, N_MIX_HEADS, CHUNK))
    kv_wk = nrm(ks[7], (d, D_MIX)) * d ** -0.5
    kv_wv = nrm(ks[8], (d, D_MIX)) * d ** -0.5 * DN_BETA
    kv_wf = nrm(ks[9], (d, N_MIX_HEADS)) * d ** -0.5
    kv_w = jnp.concatenate([kv_wk, kv_wv, kv_wf], axis=-1)
    kv_b_f = jnp.linspace(1.0, 6.0, N_MIX_HEADS, dtype=f32) + 0.01 * nrm(ks[10], (N_MIX_HEADS,))
    b_w_q = nrm(ks[11], (N_B_LAYERS, d, D_MIX + D_MEM)) * d ** -0.5
    mk = nrm(ks[12], (DEPTH, d, D_MEM)) * d ** -0.5
    mv = nrm(ks[13], (DEPTH, d, D_MEM)) * d ** -0.5 * DN_BETA
    mem_w_kv = jnp.concatenate([mk, mv], axis=-1)
    w_o = nrm(ks[14], (DEPTH, D_MIX + D_MEM, d)) * (D_MIX + D_MEM) ** -0.5 * DN_BETA
    ln_g = 1.0 + 0.02 * nrm(ks[15], (DEPTH, 2, d))
    ln_b = 0.02 * nrm(ks[16], (DEPTH, 2, d))
    w_up = nrm(ks[17], (DEPTH, d, D_FF)) * d ** -0.5
    w_down = nrm(ks[18], (DEPTH, D_FF, d)) * D_FF ** -0.5 * DN_BETA
    return {"x": x, "mem": mem, "a_w_in": a_w_in, "a_sgu_ln_g": a_sgu_ln_g,
            "a_sgu_ln_b": a_sgu_ln_b, "a_w_s": a_w_s, "a_b_s": a_b_s,
            "kv_w": kv_w, "kv_b_f": kv_b_f, "b_w_q": b_w_q, "mem_w_kv": mem_w_kv,
            "w_o": w_o, "ln_g": ln_g, "ln_b": ln_b, "w_up": w_up, "w_down": w_down}

def reference(x, mem, a_w_in, a_sgu_ln_g, a_sgu_ln_b, a_w_s, a_b_s, kv_w, kv_b_f,
              b_w_q, mem_w_kv, w_o, ln_g, ln_b, w_up, w_down):
    bsz, s, _ = x.shape
    m = mem.shape[1]
    k_sh = v_sh = logcum = None
    for layer in range(DEPTH):
        if layer < N_A_LAYERS:
            z = x @ a_w_in[layer]
            zu = jax.nn.gelu(z[..., :D_MIX])
            zv = layer_norm(jax.nn.gelu(z[..., D_MIX:2 * D_MIX]), a_sgu_ln_g[layer], a_sgu_ln_b[layer])
            qm = z[..., 2 * D_MIX:]
            mix = chunked_sgu(zu.reshape(bsz, s, N_MIX_HEADS, HEAD_DIM),
                              zv.reshape(bsz, s, N_MIX_HEADS, HEAD_DIM),
                              a_w_s[layer], a_b_s[layer]).reshape(bsz, s, D_MIX)
        else:
            if layer == N_A_LAYERS:
                kvf = x @ kv_w
                k_sh = kvf[..., :D_MIX].reshape(bsz, s, N_MIX_HEADS, HEAD_DIM)
                v_sh = kvf[..., D_MIX:2 * D_MIX].reshape(bsz, s, N_MIX_HEADS, HEAD_DIM)
                f_logit = kvf[..., 2 * D_MIX:].astype(jnp.float32) + kv_b_f.astype(jnp.float32)
                logcum = jnp.cumsum(jax.nn.log_sigmoid(f_logit), axis=1).transpose(0, 2, 1)
            j = layer - N_A_LAYERS
            z = x @ b_w_q[j]
            q = z[..., :D_MIX].reshape(bsz, s, N_MIX_HEADS, HEAD_DIM)
            qm = z[..., D_MIX:]
            mix = fox_attention(q, k_sh, v_sh, logcum).reshape(bsz, s, D_MIX)
        mkv = mem @ mem_w_kv[layer]
        mk = mkv[..., :D_MEM].reshape(bsz, m, N_MEM_HEADS, HEAD_DIM)
        mv = mkv[..., D_MEM:].reshape(bsz, m, N_MEM_HEADS, HEAD_DIM)
        mo = memory_attention(qm.reshape(bsz, s, N_MEM_HEADS, HEAD_DIM), mk, mv)
        y = jnp.concatenate([mix, mo], axis=-1) @ w_o[layer]
        x = layer_norm(DN_ALPHA * x + y, ln_g[layer, 0], ln_b[layer, 0])
        x = layer_norm(DN_ALPHA * x + sq_relu_mlp(x, w_up[layer], w_down[layer]),
                       ln_g[layer, 1], ln_b[layer, 1])
    return x


_drawn_inputs = setup_inputs


def setup_inputs(seed=0):
    import zlib

    import numpy as np

    out = dict(_drawn_inputs(seed))
    spreads = {}
    factors = {'mem': 4.469, 'a_sgu_ln_g': 28.711, 'a_sgu_ln_b': 29.714, 'a_b_s': 8.0, 'mem_w_kv': 3.627}
    for name, (base, spread) in spreads.items():
        noise = np.random.default_rng([zlib.crc32(name.encode()), seed]).standard_normal(out[name].shape)
        drawn = base * np.exp(spread * noise) if base else spread * noise
        out[name] = __import__('jax').numpy.asarray(drawn.astype(out[name].dtype))
    for name, factor in factors.items():
        out[name] = (out[name] * factor).astype(out[name].dtype)
    return out
```

```python
from contextlib import ExitStack

import concourse.bass as bass
from concourse import mybir
from concourse.alu_op_type import AluOpType as ALU

ACT = mybir.ActivationFunctionType
AX = mybir.AxisListType
F32 = mybir.dt.float32
F32R = mybir.dt.float32r

P = 128
HALF = P // 2
MASKED = -1.0e37
LN_EPS = 1e-5


class Pos:

    def __init__(self, base, trip=None, step=0):
        self.base, self.trip, self.step = base, trip, step

    def at(self, off=0, mul=1):
        n = self.base * mul + off
        return n if self.trip is None else self.trip * (self.step * mul) + n

    def half(self, off=0):
        n = (self.base + off) // 2
        return n if self.trip is None else self.trip * (self.step // 2) + n

    def plus(self, off):
        return Pos(self.base + off, self.trip, self.step)

    def times(self, mul, off=0):
        return Pos(self.base * mul + off, self.trip, self.step * mul)

    @property
    def slot(self):
        return self.base % 2


def wait(engine, semaphore, value):
    if not (isinstance(value, int) and value <= 0):
        engine.wait_ge(semaphore, value)


def trunk_kernel(nc, x, mem, a_w_in, a_sgu_ln_g, a_sgu_ln_b, a_w_s, a_b_s, kv_w, kv_b_f, b_w_q,
                 mem_w_kv, w_o, ln_g, ln_b, w_up, w_down, out):
    _, T, D = x.shape
    M = mem.shape[1]
    KT = D // P
    TT = T // P
    MT = M // P
    HEADS = a_w_s.shape[1]
    PAIRS = HEADS // 2
    DMIX = HEADS * HALF
    MEMPAIRS = (D - DMIX) // P
    FF = w_up.shape[2]
    FT = FF // P // 2
    SCALE = float(HALF) ** -0.5
    ALPHA = float(2 * w_up.shape[0]) ** 0.25
    assert (T, D, M, HEADS, FF) == (512, 1024, 256, 12, 4096) and a_w_s.shape[2] == P

    B_MEM = [0, 26]
    G_MEM = [0, 26]
    B_AV = G_AV = 4
    B_AQ = G_AQ = 10
    B_AU = G_AU = 12
    B_WO, G_WO = [18, 114], [18, 98]
    B_UP = [[30, 62], [122, 154]]
    G_UP = [[30, 54], [106, 130]]
    B_DN = [[46, 78], [138, 170]]
    G_DN = [[46, 70], [122, 146]]
    B_BQ, G_BQ = 94, 78
    B_FOX, G_FOX = 96, 80

    STEP_A, STEP_B, STEP_FOX, STEP_LAST = 0, 2, 3, 9
    T_MEM, T_MV, T_PAR, T_WS, T_X, T_AV = [0, 39], [4, 43], 5, 6, 9, 17
    T_STEP = [23, 28]
    T_OUT = 108
    H_MEM, H_MV, H_WS = [0, 24], [4, 28], 5
    H_STEP = [8, 13]
    Q_MEM, Q_AQ, Q_BQ, Q_FOX = [0, 4], 2, 6, 8

    ctx = ExitStack()
    with ctx:
        def psum(name):
            return ctx.enter_context(nc.psum_tensor(name, [P, 512], F32))

        def sem(name):
            return ctx.enter_context(nc.semaphore(name))

        base = [(nc.sbuf_base + 63) // 64 * 64]

        def put(name, shape, dtype, offset=None):
            size = 4
            for n in shape[1:]:
                size *= n
            if offset is None:
                offset = base[0]
                base[0] += (size + 63) // 64 * 64
            assert offset + size <= nc.sbuf_usable_end, (name, offset + size)
            return nc.alloc_sbuf_tensor_at(name, shape, dtype, offset=offset)

        K1 = 1024
        x_hi = put("x_hi", [P, KT, T], F32R)
        x_lo = put("x_lo", [P, KT, T], F32R)
        w_hi = put("w_hi", [P, 2, KT, P], F32R)
        w_lo = put("w_lo", [P, 2, KT, P], F32R)
        x32 = put("x32", [P, KT, T], F32)
        w_raw = put("w_raw", [P, 2, KT, P], F32)
        mk_hi = put("mk_hi", [P, MEMPAIRS, M], F32R)
        mk_lo = put("mk_lo", [P, MEMPAIRS, M], F32R)
        mv_hi = put("mv_hi", [P, MT, MEMPAIRS * P], F32R)
        mv_lo = put("mv_lo", [P, MT, MEMPAIRS * P], F32R)
        ident = put("ident", [P, P], F32)
        ident_r = put("ident_r", [P, P], F32R)
        ones_r = put("ones_r", [P, P], F32R)
        causal = put("causal", [P, P], F32)
        causal_r = put("causal_r", [P, P], F32R)
        tri_r = put("tri_r", [P, T], F32R)
        head_rows = put("head_rows", [P, PAIRS], F32)
        eps = put("eps", [P, 1], F32)
        par_raw = put("par_raw", [64, P], F32)
        par = put("par", [P, 64], F32)
        neg_max = put("neg_max", [P, 8], F32)
        row_sum = put("row_sum", [P, 8], F32)
        inv_sum = put("inv_sum", [P, 8], F32)
        sgu_stats = put("sgu_stats", [P, TT, 2, 6], F32)
        sgu_mv = put("sgu_mv", [P, TT, 2], F32)
        sgu_root = put("sgu_root", [P, TT], F32)
        sgu_rstd = put("sgu_rstd", [P, TT], F32)
        wf_raw = put("wf_raw", [P, KT, HEADS], F32)
        wf_hi = put("wf_hi", [P, KT, HEADS], F32R)
        wf_lo = put("wf_lo", [P, KT, HEADS], F32R)
        bf_row = put("bf_row", [P, HEADS], F32)
        v_tmp = put("v_tmp", [P, 2, T], F32)
        probs = put("probs", [P, 2, T], F32)
        top = base[0]

        mix_hi = put("mix_hi", [P, KT, T], F32R, top)
        mix_lo = put("mix_lo", [P, KT, T], F32R, top + 16 * K1)
        qm_hi = put("qm_hi", [P, MEMPAIRS, T], F32R, top + 32 * K1)
        qm_lo = put("qm_lo", [P, MEMPAIRS, T], F32R, top + 36 * K1)
        A0 = top + 40 * K1
        u_t = put("u_t", [P, PAIRS, T], F32, A0)
        z_nat = put("z_nat", [P, TT, DMIX], F32, A0 + 12 * K1)
        pa_hi = put("pa_hi", [P, 2, MT, T], F32R, A0 + 24 * K1)
        pa_lo = put("pa_lo", [P, 2, MT, T], F32R, A0 + 32 * K1)
        z_hi = put("z_hi", [P, 2, TT, P], F32R, A0 + 40 * K1)
        z_lo = put("z_lo", [P, 2, TT, P], F32R, A0 + 44 * K1)
        gated = put("gated", [P, 2, 2 * P], F32, A0 + 48 * K1)
        ws_hi = put("ws_hi", [P, HEADS, P], F32R, A0 + 50 * K1)
        ws_lo = put("ws_lo", [P, HEADS, P], F32R, A0 + 56 * K1)
        bs_all = put("bs_all", [P, PAIRS, P], F32, A0 + 62 * K1)
        g_all = put("g_all", [P, DMIX], F32, A0 + 65 * K1)
        b_all = put("b_all", [P, DMIX], F32, A0 + 68 * K1)
        memt_hi = put("memt_hi", [P, KT, M], F32R, top)
        memt_lo = put("memt_lo", [P, KT, M], F32R, top + 8 * K1)
        mem_nat = put("mem_nat", [P, MT, D], F32, top + 16 * K1)
        ws_raw = put("ws_raw", [P, HEADS, P], F32, top + 24 * K1)
        x_nat = put("x_nat", [P, TT, D], F32, top + 30 * K1)
        tri_f = put("tri_f", [P, T], F32, A0 + 12 * K1)
        q_hi = put("q_hi", [P, 2, T], F32R, A0)
        q_lo = put("q_lo", [P, 2, T], F32R, A0 + 4 * K1)
        k_hi = put("k_hi", [P, 2, T], F32R, A0 + 8 * K1)
        k_lo = put("k_lo", [P, 2, T], F32R, A0 + 12 * K1)
        v_hi = put("v_hi", [P, 2, TT, P], F32R, A0 + 16 * K1)
        v_lo = put("v_lo", [P, 2, TT, P], F32R, A0 + 20 * K1)
        pb_hi = put("pb_hi", [P, 2, TT, T], F32R, A0 + 24 * K1)
        pb_lo = put("pb_lo", [P, 2, TT, T], F32R, A0 + 40 * K1)
        cum = put("cum", [P, T], F32R, A0 + 56 * K1)
        cum_row = put("cum_row", [P, T], F32R, A0 + 58 * K1)
        lf_hi = put("lf_hi", [P, TT, P], F32R, A0 + 62 * K1)
        lf_lo = put("lf_lo", [P, TT, P], F32R, A0 + 64 * K1)
        f_log = put("f_log", [P, TT, HEADS], F32, A0 + 66 * K1)
        f_abs = put("f_abs", [P, TT, HEADS], F32, A0 + 66 * K1 + 256)
        f_neg = put("f_neg", [P, TT, HEADS], F32, A0 + 66 * K1 + 512)
        f_exp = put("f_exp", [P, TT, HEADS], F32, A0 + 66 * K1 + 768)
        f_ln = put("f_ln", [P, TT, HEADS], F32, A0 + 67 * K1)
        f_sp = put("f_sp", [P, TT, HEADS], F32, A0 + 67 * K1 + 256)
        h_hi = put("h_hi", [P, FT, T], F32R, top)
        h_lo = put("h_lo", [P, FT, T], F32R, top + 32 * K1)
        L0 = top + 64 * K1
        shift = put("shift", [P, T], F32, L0)
        shift_in = put("shift_in", [P, T], F32R, L0 + 2 * K1)
        total = put("total", [P, T], F32, L0 + 4 * K1)
        total_sq = put("total_sq", [P, T], F32, L0 + 6 * K1)
        square = put("square", [P, 2, T], F32, L0 + 8 * K1)
        stat_hi = put("stat_hi", [P, 2, T], F32R, L0 + 12 * K1)
        stat_lo = put("stat_lo", [P, 2, T], F32R, L0 + 16 * K1)
        rstd = put("rstd", [P, T], F32, L0 + 20 * K1)
        mean = put("mean", [P, T], F32, L0 + 22 * K1)
        relu = put("relu", [P, 2, T], F32, L0 + 24 * K1)
        h_raw = put("h_raw", [P, 2, T], F32, L0 + 28 * K1)
        mem2_nat = put("mem2_nat", [P, MT, D], F32, L0 + 24 * K1)
        memt2_hi = put("memt2_hi", [P, KT, M], F32R, L0 + 32 * K1)
        memt2_lo = put("memt2_lo", [P, KT, M], F32R, L0 + 40 * K1)
        y_nat = put("y_nat", [P, TT, D], F32, top)
        mem_in = [mem_nat, mem2_nat]
        mem_hi, mem_lo = [memt_hi, memt2_hi], [memt_lo, memt2_lo]

        proj = [psum("proj0"), psum("proj1")]
        sc = [psum("sc0"), psum("sc1")]
        tr = [psum("tr0"), psum("tr1")]
        pv = [psum("pv0"), psum("pv1")]

        w_landed = [sem("w_landed0"), sem("w_landed1")]
        w_hi_ready, w_split = sem("w_hi_ready"), sem("w_split")
        w_used = sem("w_used")
        proj_free = [sem("proj_free0"), sem("proj_free1")]
        qk_hi = sem("qk_hi")
        tr_done, tr_hi, tr_free = sem("tr_done"), sem("tr_hi"), sem("tr_free")
        x_split, x_hi_ready, x_ready = sem("x_split"), sem("x_hi_ready"), sem("x_ready")
        mem_landed, x_landed, ws_landed = sem("mem_landed"), sem("x_landed"), sem("ws_landed")
        par_landed, sgu_landed, wf_landed = sem("par_landed"), sem("sgu_landed"), sem("wf_landed")
        const_ready, const_r, ws_masked = sem("const_ready"), sem("const_r"), sem("ws_masked")
        pool_step = sem("pool_step")
        bn_step, zn_ready, zg_ready = sem("bn_step"), sem("zn_ready"), sem("zg_ready")
        zg_step = sem("zg_step")
        z_hi_ready, z_ready = sem("z_hi_ready"), sem("z_ready")
        sgu_done, sgu_added, sgu_gated = sem("sgu_done"), sem("sgu_added"), sem("sgu_gated")
        sgu_hi, sgu_ready = sem("sgu_hi"), sem("sgu_ready")
        sc_done, max_done, exp_done = sem("sc_done"), sem("max_done"), sem("exp_done")
        inv_done, probs_ready = sem("inv_done"), sem("probs_ready")
        pv_done, mix_hi_ready, mix_ready = sem("pv_done"), sem("mix_hi_ready"), sem("mix_ready")
        vt_done, vt_hi, vt_ready = sem("vt_done"), sem("vt_hi"), sem("vt_ready")
        row_ready = sem("row_ready")
        wf_hi_ready, wf_ready = sem("wf_hi_ready"), sem("wf_ready")
        f_done, f_step, f_act, cum_done = sem("f_done"), sem("f_step"), sem("f_act"), sem("cum_done")
        relu_sq, h_hi_ready, h_ready = sem("relu_sq"), sem("h_hi_ready"), sem("h_ready")
        shift_ready, shift_done, shifted = sem("shift_ready"), sem("shift_done"), sem("shifted")
        shift_out = sem("shift_out")
        sq_ready, sum_added, sq_added = sem("sq_ready"), sem("sum_added"), sem("sq_added")
        stat_hi_ready, stat_ready, stat_done = sem("stat_hi_ready"), sem("stat_ready"), sem("stat_done")
        ln_step, ln_root = sem("ln_step"), sem("ln_root")
        bn_root, u_ready = sem("bn_root"), sem("u_ready")
        fin_scaled, fin_moved, fin_ready = sem("fin_scaled"), sem("fin_moved"), sem("fin_ready")
        y_stored = sem("y_stored")

        block = ctx.enter_context(nc.Block())

        def x32_tile(j):
            if j.trip is None:
                return x32[:, j.base, :]
            return x32[:, bass.ds(j.at(), 1), :].rearrange("p a t -> p (a t)")

        def tr_index(s, u):
            return s.times(8, T_STEP[s.base >= STEP_B] + u)

        def hi_index(s, u):
            return s.times(8, H_STEP[s.base >= STEP_B] + u)

        def fox(s):
            return STEP_FOX <= s.base < STEP_LAST

        def step_kind(s):
            return s.plus(-STEP_FOX) if fox(s) else Pos({0: 0, 1: 1, STEP_B: 0, STEP_LAST: 1}[s.base])

        def step_tile(s):
            return step_kind(s).at() if fox(s) else PAIRS + step_kind(s).at()

        def keys(s, u):
            return u % TT + 1 if fox(s) else MT

        def p_buffers(s):
            return (pb_hi, pb_lo) if s.base >= STEP_B else (pa_hi, pa_lo)

        @block.sync
        def _(sp):
            def load(b, source):
                wait(sp, w_split, b.at(-1))
                sp.dma_start(w_raw[:, b.slot], source).then_inc(w_landed[b.slot], 16)

            def cols(w, c, r=0):
                return w[r:r + D, bass.ds(c, P)].rearrange("(k p) n -> p k n", p=P)

            def memory_weights(layer):
                for c in range(4):
                    load(Pos(B_MEM[layer] + c), cols(mem_w_kv[layer], c * P))

            def feed_forward(layer):
                for half in range(2):
                    with sp.Fori(0, FT // 2) as i:
                        for c in range(2):
                            load(Pos(B_UP[layer][half] + c, i, 2),
                                 cols(w_up[layer], i * (2 * P) + (half * FT + c) * P))
                    with sp.Fori(0, KT) as i:
                        for c in range(2):
                            load(Pos(B_DN[layer][half] + c, i, 2),
                                 cols(w_down[layer], i * P, (half * 2 + c) * D))

            memory_weights(0)
            with sp.Fori(0, PAIRS // 2) as i:
                for c in range(2):
                    load(Pos(B_AV + c, i, 2), cols(a_w_in[0], i * (2 * P) + DMIX + c * P))
            for c in range(MEMPAIRS):
                load(Pos(B_AQ + c), cols(a_w_in[0], 2 * DMIX + c * P))
            with sp.Fori(0, PAIRS // 2) as i:
                for c in range(2):
                    load(Pos(B_AU + c, i, 2), cols(a_w_in[0], i * (2 * P) + c * P))
            with sp.Fori(0, KT // 2) as i:
                for c in range(2):
                    load(Pos(B_WO[0] + c, i, 2), cols(w_o[0], i * (2 * P) + c * P))
            memory_weights(1)
            feed_forward(0)
            for c in range(MEMPAIRS):
                load(Pos(B_BQ + c), cols(b_w_q[0], DMIX + c * P))
            with sp.Fori(0, PAIRS // 2) as i:
                for j in range(2):
                    load(Pos(B_FOX + 3 * j, i, 6), cols(b_w_q[0], i * (2 * P) + j * P))
                    load(Pos(B_FOX + 3 * j + 1, i, 6), cols(kv_w, i * (2 * P) + j * P))
                    load(Pos(B_FOX + 3 * j + 2, i, 6), cols(kv_w, i * (2 * P) + DMIX + j * P))
            with sp.Fori(0, KT // 2) as i:
                for c in range(2):
                    load(Pos(B_WO[1] + c, i, 2), cols(w_o[1], i * (2 * P) + c * P))
            feed_forward(1)
            rows = out[0].rearrange("(t p) d -> p t d", p=P)
            for k in range(KT):
                sp.wait_ge(tr_free, T_OUT + k + 1)
                sp.dma_start(rows[:, :, k * P:(k + 1) * P], y_nat[:, :, k * P:(k + 1) * P]).then_inc(y_stored, 16)
            sp.wait_ge(y_stored, 16 * KT)

        @block.tensor
        def _(pe):
            def products(target, terms, start=True, stop=True):
                for n, (lhs, rhs) in enumerate(terms):
                    last = pe.matmul(target, lhs, rhs, start=start and n == 0,
                                     stop=stop and n == len(terms) - 1)
                return last

            def block_terms(b, k, hi, lo):
                return [(w_hi[:, b.slot, k], hi), (w_hi[:, b.slot, k], lo), (w_lo[:, b.slot, k], hi)]

            def project(b, g, hi, lo, columns=T, order=range(KT), ready=None, parts=(0, KT),
                        start=True, stop=True):
                bank = proj[g.slot]
                for n in range(*parts):
                    k = order[n]
                    if n == 0:
                        pe.wait_ge(w_split, b.at(1))
                        if start:
                            wait(pe, proj_free[g.slot], g.half())
                    if ready:
                        ready(n)
                    last = products(bank[:, 0:columns], block_terms(b, k, hi[:, k], lo[:, k]),
                                    start and n == 0, stop and n == KT - 1)
                if parts[1] == KT:
                    last.then_inc(w_used, 1)

            def transposes(t, pieces):
                wait(pe, tr_free, t.at(-1))
                at = 0
                for piece in pieces:
                    rows, n = piece.shape[0], piece.shape[-1]
                    last = pe.transpose(tr[t.slot][0:n, at:at + rows], piece, ident[0:rows, 0:rows])
                    at += rows
                last.then_inc(tr_done, 1)

            def memory_transposes(layer):
                pe.wait_ge(mem_landed, 16 * (layer + 1))
                for n in range(4):
                    transposes(Pos(T_MEM[layer] + n), [mem_in[layer][:, m, k * P:(k + 1) * P]
                                                       for k in (2 * n, 2 * n + 1) for m in range(MT)])

            def memory_projection(layer, c):
                if c == 0:
                    pe.wait_ge(tr_free, T_MEM[layer] + 4)
                project(Pos(B_MEM[layer] + c), Pos(G_MEM[layer] + c), mem_hi[layer], mem_lo[layer], M)

            def memory_values(layer):
                for c in range(2, 4):
                    g = Pos(G_MEM[layer] + c)
                    pe.wait_ge(proj_free[g.slot], g.half(2))
                transposes(Pos(T_MV[layer]), [v_tmp[:, c, m * P:(m + 1) * P] for m in range(MT) for c in range(2)])

            def scores(s, u):
                head, i, n = u // TT, u % TT, keys(s, u) * P
                rows = slice(head * HALF, (head + 1) * HALF)
                here = slice(i * P, (i + 1) * P)
                wait(pe, exp_done, s.at(u - 1, 8))
                bank = sc[u % 2]
                if fox(s):
                    c = step_kind(s).slot
                    if u == 0:
                        g = step_kind(s).times(3, G_FOX)
                        for q in (g, g.plus(1)):
                            pe.wait_ge(proj_free[q.slot], Pos(q.base, q.trip, q.step).half(2))
                        pe.wait_ge(row_ready, step_kind(s).at(1))
                    products(bank[:, 0:n], [(ones_r[rows, :], cum_row[rows, 0:n])], stop=False)
                    products(bank[:, here], [(ident_r[:, :], causal_r[:, :])], start=False, stop=False)
                    qh, ql, kh, kl = q_hi[rows, c, here], q_lo[rows, c, here], k_hi[rows, c, 0:n], k_lo[rows, c, 0:n]
                else:
                    c = step_kind(s).at()
                    qh, ql, kh, kl = qm_hi[rows, c, here], qm_lo[rows, c, here], mk_hi[rows, c, :], mk_lo[rows, c, :]
                products(bank[:, 0:n], [(qh, kl), (ql, kh), (qh, kh)], start=not fox(s)).then_inc(sc_done, 1)

            def turn(s, u):
                pe.wait_ge(probs_ready, s.at(u + 1, 8))
                transposes(tr_index(s, u), [probs[:, u % 2, j * P:(j + 1) * P] for j in range(keys(s, u))])

            def attend(s, head):
                pe.wait_ge(tr_free, tr_index(s, head * TT + TT - 1).at(1))
                wait(pe, mix_ready, s.at(head - 1, 2))
                if s.base == STEP_B and head == 1:
                    pe.wait_ge(f_step, 1)
                hi, lo = p_buffers(s)
                c = step_kind(s).slot
                if fox(s) and head == 0:
                    pe.wait_ge(vt_ready, step_kind(s).at(1))
                tiles = TT if fox(s) else MT
                for j in range(tiles):
                    seen = slice(j * P if fox(s) else 0, T)
                    if fox(s):
                        vh, vl = v_hi[:, c, j], v_lo[:, c, j]
                    else:
                        vh, vl = mv_hi[:, j, c * P:(c + 1) * P], mv_lo[:, j, c * P:(c + 1) * P]
                    ph, pl = hi[:, head, j, seen], lo[:, head, j, seen]
                    last = products(pv[head][:, seen], [(vh, ph), (vh, pl), (vl, ph)], j == 0, j == tiles - 1)
                last.then_inc(pv_done, 1)

            def turn_values(s, j):
                g = j.times(3, G_FOX + 2)
                pe.wait_ge(proj_free[g.slot], g.half(2))
                if s is not None:
                    pe.wait_ge(mix_ready, s.at(1, 2))
                for t in range(TT):
                    last = pe.transpose(pv[0][:, t * P:(t + 1) * P], v_tmp[:, g.slot, t * P:(t + 1) * P], ident[:, :])
                last.then_inc(vt_done, 1)

            def pair_step(s, b=None, g=None, values=None):
                def filler(n):
                    if b is not None:
                        c = n // 3
                        project(b.plus(c), g.plus(c), x_hi, x_lo, parts=[(0, 3), (3, 6), (6, KT)][n % 3])
                for u in range(8):
                    filler(u)
                    if u >= 2:
                        turn(s, u - 2)
                    scores(s, u)
                    if u == 6:
                        attend(s, 0)
                filler(8)
                turn(s, 6)
                turn(s, 7)
                attend(s, 1)
                if values is not None:
                    turn_values(s, values)

            def out_projection(layer, ready):
                for j in range(KT):
                    order = [6, 7, 0, 1, 2, 3, 4, 5] if layer == 0 else [6, 0, 1, 2, 3, 4, 5, 7]
                    project(Pos(B_WO[layer] + j), Pos(G_WO[layer] + j), mix_hi, mix_lo, order=order,
                            ready=ready if j == 0 else None)
                    if j == 1:
                        shift_sum(2 * layer)

            def shift_sum(n):
                pe.wait_ge(shift_ready, n + 1)
                products(sc[0][:, :], [(ones_r[:, :], shift_in[:, :])]).then_inc(shift_done, 1)

            def layer_sums(n):
                for q in range(2):
                    pe.wait_ge(stat_ready, 2 * n + q + 1)
                    products(sc[q][:, :], [(ones_r[:, :], stat_hi[:, q]), (ones_r[:, :], stat_lo[:, q])])\
                        .then_inc(stat_done, 1)

            def feed_forward(layer):
                for half in range(2):
                    b, g = B_UP[layer][half], G_UP[layer][half]
                    first = 2
                    for c in range(first):
                        project(Pos(b + c), Pos(g + c), x_hi, x_lo,
                                ready=(lambda n: pe.wait_ge(x_ready, KT * (2 * layer + 1) + n + 1)) if half == c == 0 else None)
                    with pe.Fori(0, (FT - first) // 2) as i:
                        for c in range(2):
                            project(Pos(b + first + c, i, 2), Pos(g + first + c, i, 2), x_hi, x_lo)
                    b, g = B_DN[layer][half], G_DN[layer][half]
                    h0 = (2 * layer + half) * FT

                    def down(b, g, ready=False):
                        for c in range(2):
                            project(b.plus(c), g, h_hi[:, c * KT:(c + 1) * KT], h_lo[:, c * KT:(c + 1) * KT],
                                    ready=(lambda n: pe.wait_ge(h_ready, h0 + c * KT + n + 1)) if ready else None,
                                    start=c == 0, stop=c == 1)
                    for j in range(2):
                        down(Pos(b + 2 * j), Pos(g + j), j == 0)
                    if half:
                        shift_sum(2 * layer + 1)
                    with pe.Fori(0, KT // 2 - 1) as i:
                        for j in range(2):
                            down(Pos(b + 4 + 2 * j, i, 4), Pos(g + 2 + j, i, 2))


            def spatial_gate():
                pe.wait_ge(exp_done, 16)
                for j in range(PAIRS):
                    pe.wait_ge(z_ready, j + 1)
                    both = slice(2 * j, 2 * j + 2)
                    for c in range(2):
                        wait(pe, sgu_added, 2 * (j - 1) + c + 1)
                        for n in range(2):
                            zh, zl = z_hi[:, j % 2, 2 * c + n], z_lo[:, j % 2, 2 * c + n]
                            last = products(sc[c][:, n * 2 * P:(n + 1) * 2 * P],
                                            [(zh, ws_hi[:, both]), (zh, ws_lo[:, both]), (zl, ws_hi[:, both])])
                        last.then_inc(sgu_done, 1)

            def forget_gate():
                pe.wait_ge(wf_ready, 1)
                for t in range(TT):
                    here = slice(t * P, (t + 1) * P)
                    terms = []
                    for k in range(KT):
                        terms += [(x_hi[:, k, here], wf_hi[:, k]), (x_hi[:, k, here], wf_lo[:, k]),
                                  (x_lo[:, k, here], wf_hi[:, k])]
                    last = products(pv[1][:, t * HEADS:(t + 1) * HEADS], terms)
                last.then_inc(f_done, 1)

            def cumulate():
                pe.wait_ge(f_act, 3)
                pe.wait_ge(f_step, 7)
                pe.wait_ge(mix_ready, 2 * STEP_B + 2)
                for t in range(TT):
                    span = tri_r[:, 0:T - t * P]
                    last = products(pv[1][:, t * P:T], [(lf_hi[:, t], span), (lf_lo[:, t], span)],
                                    t == 0, t == TT - 1)
                last.then_inc(cum_done, 1)

            pe.wait_ge(const_ready, 1)
            memory_transposes(0)
            for c in range(4):
                memory_projection(0, c)
            memory_values(0)
            pe.wait_ge(par_landed, 32)
            transposes(Pos(T_PAR), [par_raw[:, :]])
            pe.wait_ge(ws_masked, 1)
            for n in range(3):
                transposes(Pos(T_WS + n), [ws_raw[:, h] for h in range(4 * n, 4 * n + 4)])
            pe.wait_ge(x_landed, 16)
            for k in range(KT):
                transposes(Pos(T_X + k), [x_nat[:, t, k * P:(k + 1) * P] for t in range(TT)])
            pe.wait_ge(x_ready, KT)
            with pe.Fori(0, PAIRS // 2) as i:
                for c in range(2):
                    project(Pos(B_AV + c, i, 2), Pos(G_AV + c, i, 2), x_hi, x_lo)
                for c in range(2):
                    g = Pos(G_AV + c, i, 2)
                    pe.wait_ge(proj_free[g.slot], g.half(2))
                    transposes(Pos(T_AV + c, i, 2), [v_tmp[:, g.slot, t * P:(t + 1) * P] for t in range(TT)])
            for c in range(MEMPAIRS):
                project(Pos(B_AQ + c), Pos(G_AQ + c), x_hi, x_lo)
            for c in range(MEMPAIRS):
                pe.wait_ge(proj_free[c], (G_AQ + c) // 2 + 1)
            for s in range(2):
                pair_step(Pos(STEP_A + s), Pos(B_AU + 3 * s), Pos(G_AU + 3 * s))
            spatial_gate()
            out_projection(0, lambda n: pe.wait_ge(mix_ready, 2 * n + 2) if n < 2 else pe.wait_ge(sgu_ready, 2 * (n - 1)))
            memory_transposes(1)
            for c in range(2):
                memory_projection(1, c)
            layer_sums(0)
            for c in range(2, 4):
                memory_projection(1, c)
            memory_values(1)
            feed_forward(0)
            layer_sums(1)

            for c in range(MEMPAIRS):
                project(Pos(B_BQ + c), Pos(G_BQ + c), x_hi, x_lo,
                        ready=(lambda n: pe.wait_ge(x_ready, 2 * KT + n + 1)) if c == 0 else None)
            forget_gate()
            for c in range(MEMPAIRS):
                pe.wait_ge(proj_free[c], (G_BQ + c) // 2 + 1)
            pair_step(Pos(STEP_B), Pos(B_FOX), Pos(G_FOX), values=Pos(0))
            cumulate()
            with pe.Fori(0, 2) as i:
                for j in range(2):
                    pair_step(Pos(STEP_FOX + j, i, 2), Pos(B_FOX + 3 * (j + 1), i, 6),
                              Pos(G_FOX + 3 * (j + 1), i, 6), values=Pos(j + 1, i, 2))
            pair_step(Pos(7), Pos(B_FOX + 15), Pos(G_FOX + 15), values=Pos(5))
            pair_step(Pos(8))
            pair_step(Pos(STEP_LAST))
            out_projection(1, lambda n: pe.wait_ge(mix_ready, 2 * (STEP_B + n) + 2))
            layer_sums(2)
            feed_forward(1)
            layer_sums(3)
            for k in range(KT):
                pe.wait_ge(fin_ready, 3 * KT + k + 1)
                transposes(Pos(T_OUT + k), [x32[:, k, t * P:(t + 1) * P] for t in range(TT)])

        @block.scalar
        def _(act):
            def prepare(b):
                if b.trip is None and b.base >= B_DN[1][1] + 2 * KT:
                    return
                act.wait_ge(w_landed[b.slot], b.half(2) * 16)
                wait(act, w_used, b.at(-1))
                act.copy(w_hi[:, b.slot], w_raw[:, b.slot]).then_inc(w_hi_ready, 1)

            def turned_hi(t, target, source=None):
                act.wait_ge(tr_done, t.at(1))
                act.copy(target, tr[t.slot][:, :] if source is None else source).then_inc(tr_hi, 1)

            def projected(b, g, target, scale=1.0):
                act.wait_ge(w_used, b.at(1))
                act.activation(target, proj[g.slot][:, 0:target.shape[-1]], ACT.Copy, scale=scale).then_inc(qk_hi, 1)

            def plain(b, g, target, function=ACT.Copy):
                act.wait_ge(w_used, b.at(1))
                act.activation(target, proj[g.slot][:, 0:target.shape[-1]], function).then_inc(proj_free[g.slot], 1)

            def memory_hi(layer):
                for n in range(4):
                    turned_hi(Pos(T_MEM[layer] + n), mem_hi[layer][:, 2 * n:2 * n + 2],
                              tr[(T_MEM[layer] + n) % 2][:, :].rearrange("p (k m) -> p k m", k=2))

            def memory_projection(layer, c):
                b, g = Pos(B_MEM[layer] + c), Pos(G_MEM[layer] + c)
                if c < 2:
                    projected(b, g, mk_hi[:, c, :])
                else:
                    plain(b, g, v_tmp[:, c - 2, 0:M])

            def memory_values(layer):
                turned_hi(Pos(T_MV[layer]), mv_hi[:, :, :], tr[T_MV[layer] % 2][:, :].rearrange("p (m c) -> p m c", m=MT))

            def exponentials(s, u):
                n = keys(s, u) * P
                act.wait_ge(max_done, s.at(u + 1, 8))
                act.activation(probs[:, u % 2, 0:n], sc[u % 2][:, 0:n], ACT.Exp, bias=neg_max[:, u:u + 1],
                               accum_out=row_sum[:, u:u + 1]).then_inc(exp_done, 1)

            def turned_probs(s, u):
                n, here, t = keys(s, u), slice(u % TT * P, (u % TT + 1) * P), tr_index(s, u)
                turned_hi(t, p_buffers(s)[0][:, u // TT, 0:n, here],
                          tr[t.slot][:, 0:n * P].rearrange("p (j t) -> p j t", j=n))

            def attended(s, head):
                rows = slice(head * HALF, (head + 1) * HALF)
                act.wait_ge(pv_done, s.at(head + 1, 2))
                act.copy(mix_hi[rows, bass.ds(step_tile(s), 1), :], pv[head][rows, :].rearrange("p (a t) -> p a t", a=1))\
                    .then_inc(mix_hi_ready, 1)

            def step_projection(s, b, g, c):
                if s.base < STEP_B:
                    plain(b, g, u_t[:, g.base - G_AU, :])
                elif c < 2:
                    j = (g.base - G_FOX) // 3 % 2
                    projected(b, g, (q_hi, k_hi)[c][:, j, :], SCALE if c == 0 else 1.0)
                else:
                    plain(b, g, v_tmp[:, g.slot, :])

            def pair_step(s, b=None, g=None, values=None):
                for u in range(8):
                    if b is not None and u in (0, 3, 6):
                        prepare(b.plus(u // 3 + 1))
                    if u >= 2:
                        turned_probs(s, u - 2)
                    exponentials(s, u)
                    if b is not None and u in (2, 5):
                        step_projection(s, b.plus(u // 3), g.plus(u // 3), u // 3)
                attended(s, 0)
                if b is not None:
                    step_projection(s, b.plus(2), g.plus(2), 2)
                turned_probs(s, 6)
                turned_probs(s, 7)
                attended(s, 1)
                if values is not None:
                    act.wait_ge(vt_done, values.at(1))
                    act.copy(v_hi[:, values.slot], pv[0][:, :].rearrange("p (t c) -> p t c", t=TT)).then_inc(vt_hi, 1)

            def squares(n, j):
                act.wait_ge(shifted, j.at(KT * n + 1))
                wait(act, sq_added, j.at(KT * n - 1))
                act.activation(square[:, j.slot, :], x32_tile(j), ACT.Square).then_inc(sq_ready, 1)

            def shift_source(n, g):
                act.wait_ge(proj_free[g % 2], g // 2 + 1)
                act.copy(shift_in[:, :], x32[:, 0]).then_inc(shift_ready, 1)

            def stats(n):
                for q, (added, source) in enumerate([(sum_added, total), (sq_added, total_sq)]):
                    act.wait_ge(added, KT * (n + 1))
                    act.copy(stat_hi[:, q], source[:, :]).then_inc(stat_hi_ready, 1)

            def root(n):
                act.wait_ge(ln_step, 5 * n + 3)
                act.activation(rstd[:, :], rstd[:, :], ACT.Sqrt, bias=eps[:, 0:1]).then_inc(ln_root, 1)

            def finish(n, tiles):
                for k in tiles:
                    act.wait_ge(fin_moved, KT * n + k + 1)
                    act.activation(x32[:, k], x32[:, k], ACT.Identity, bias=par[:, 32 + KT * n + k:33 + KT * n + k],
                                   scale=par[:, KT * n + k:KT * n + k + 1]).then_inc(fin_ready, 1)
                    if n < 3:
                        act.wait_ge(fin_ready, KT * n + k + 1)
                        act.copy(x_hi[:, k], x32[:, k]).then_inc(x_hi_ready, 1)

            def feed_forward(layer):
                for half in range(2):
                    def up(tile):
                        b, g = tile.plus(B_UP[layer][half]), tile.plus(G_UP[layer][half])
                        h = tile.plus((2 * layer + half) * FT)
                        prepare(b.plus(1))
                        wait(act, relu_sq, h.at(-1))
                        plain(b, g, relu[:, tile.slot, :], ACT.Relu)
                        act.wait_ge(proj_free[g.slot], g.half(2))
                        act.activation(h_hi[:, bass.ds(tile.at(), 1), :], relu[:, tile.slot:tile.slot + 1, :],
                                       ACT.Square).then_inc(h_hi_ready, 1)
                    up(Pos(0))
                    up(Pos(1))
                    with act.Fori(0, FT // 2 - 1) as i:
                        up(Pos(2, i, 2))
                        up(Pos(3, i, 2))
                    b, n = B_DN[layer][half], 2 * layer + 1
                    if not half:
                        with act.Fori(0, KT) as i:
                            for c in range(2):
                                prepare(Pos(b + c + 1, i, 2))
                        continue
                    for c in range(4):
                        prepare(Pos(b + c + 1))
                    shift_source(n, G_DN[layer][half])
                    for j in range(2):
                        squares(n, Pos(j))
                    with act.Fori(0, 2) as i:
                        for j in range(2):
                            for c in range(2):
                                prepare(Pos(b + 4 + 2 * j + c + 1, i, 4))
                            squares(n, Pos(2 + j, i, 2))
                    for j in range(6, KT):
                        for c in range(2):
                            prepare(Pos(b + 2 * j + c + 1))
                        squares(n, Pos(j))
                    stats(n)
                    root(n)
                    finish(n, range(KT))

            def out_projection(layer):
                for j in range(KT):
                    prepare(Pos(B_WO[layer] + j + 1))
                    if j == 1:
                        shift_source(2 * layer, G_WO[layer])
                        squares(2 * layer, Pos(0))
                    if j > 0:
                        squares(2 * layer, Pos(j))

            act.dma_start(mem_nat[:, :, :], mem[0].rearrange("(m p) d -> p m d", p=P)).then_inc(mem_landed, 16)
            act.dma_start(x_nat[:, :, :], x[0].rearrange("(t p) d -> p t d", p=P)).then_inc(x_landed, 16)
            act.dma_start(par_raw[0:32, :], ln_g.rearrange("l i (k p) -> (l i k) p", p=P)).then_inc(par_landed, 16)
            act.dma_start(par_raw[32:64, :], ln_b.rearrange("l i (k p) -> (l i k) p", p=P)).then_inc(par_landed, 16)
            act.dma_start(ws_raw[:, :, :], a_w_s[0].rearrange("h t s -> t h s")).then_inc(ws_landed, 16)
            act.dma_start(g_all[:, :], a_sgu_ln_g.broadcast_to([P, DMIX])).then_inc(sgu_landed, 16)
            act.dma_start(b_all[:, :], a_sgu_ln_b.broadcast_to([P, DMIX])).then_inc(sgu_landed, 16)
            for head in range(2):
                own = a_b_s.rearrange("a (j e) t -> a e j t", e=2)[:, head].broadcast_to([HALF, PAIRS, P])
                act.dma_start(bs_all[head * HALF:(head + 1) * HALF, :, :], own).then_inc(sgu_landed, 16)
            act.dma_start(wf_raw[:, :, :], kv_w[:, 2 * DMIX:].rearrange("(k p) n -> p k n", p=P)).then_inc(wf_landed, 16)
            act.dma_start(bf_row[:, :], kv_b_f.rearrange("(a n) -> a n", a=1).broadcast_to([P, HEADS])).then_inc(wf_landed, 16)

            act.wait_ge(const_ready, 3)
            act.copy(ident_r[:, :], ident[:, :])
            act.copy(causal_r[:, :], causal[:, :])
            act.copy(tri_r[:, :], tri_f[:, :]).then_inc(const_r, 1)
            prepare(Pos(0))
            memory_hi(0)
            for c in range(4):
                prepare(Pos(c + 1))
                memory_projection(0, c)
            memory_values(0)
            for n in range(3):
                turned_hi(Pos(T_WS + n), ws_hi[:, 4 * n:4 * n + 4], tr[(T_WS + n) % 2][:, :].rearrange("p (h t) -> p h t", h=4))
            for k in range(KT):
                act.wait_ge(tr_free, T_X + k + 1)
                act.copy(x_hi[:, k], x32[:, k]).then_inc(x_hi_ready, 1)
            with act.Fori(0, PAIRS // 2) as i:
                for c in range(2):
                    b, g = Pos(B_AV + c, i, 2), Pos(G_AV + c, i, 2)
                    prepare(b.plus(1))
                    plain(b, g, v_tmp[:, g.slot, :], ACT.Gelu_apprx_tanh)
            for c in range(MEMPAIRS):
                prepare(Pos(B_AQ + c + 1))
                projected(Pos(B_AQ + c), Pos(G_AQ + c), qm_hi[:, c, :], SCALE)
            act.wait_ge(bn_step, 3 * TT)
            act.activation(sgu_root[:, :], sgu_mv[:, :, 1], ACT.Sqrt, bias=eps[:, 0:1]).then_inc(bn_root, 1)
            for s in range(2):
                pair_step(Pos(STEP_A + s), Pos(B_AU + 3 * s), Pos(G_AU + 3 * s))
            act.wait_ge(zg_ready, TT)
            for j in range(PAIRS + 1):
                if j < PAIRS:
                    wait(act, sgu_done, 2 * (j - 1))
                    act.copy(z_hi[:, j % 2], z_nat[:, :, j * P:(j + 1) * P]).then_inc(z_hi_ready, 1)
                    if j == 0:
                        for g in (G_WO[0] - 2, G_WO[0] - 1):
                            act.wait_ge(proj_free[g % 2], g // 2 + 1)
                    act.activation(u_t[:, j, :], u_t[:, j, :], ACT.Gelu_apprx_tanh).then_inc(u_ready, 1)
                for c in range(2):
                    if j:
                        act.wait_ge(sgu_gated, 2 * (j - 1) + c + 1)
                        act.copy(mix_hi[:, j - 1, c * 2 * P:(c + 1) * 2 * P], gated[:, c]).then_inc(sgu_hi, 1)
            act.wait_ge(sgu_ready, 2 * PAIRS)
            act.dma_start(mem2_nat[:, :, :], mem[0].rearrange("(m p) d -> p m d", p=P)).then_inc(mem_landed, 16)
            out_projection(0)
            memory_hi(1)
            prepare(Pos(27))
            stats(0)
            memory_projection(1, 0)
            prepare(Pos(28))
            root(0)
            memory_projection(1, 1)
            prepare(Pos(29))
            memory_projection(1, 2)
            finish(0, range(4))
            prepare(Pos(30))
            memory_projection(1, 3)
            finish(0, range(4, KT))
            memory_values(1)
            feed_forward(0)

            for c in range(MEMPAIRS):
                prepare(Pos(B_BQ + c + 1))
                projected(Pos(B_BQ + c), Pos(G_BQ + c), qm_hi[:, c, :], SCALE)
            act.wait_ge(f_step, 2)
            act.activation(f_exp[:, :, :], f_abs[:, :, :], ACT.Exp).then_inc(f_act, 1)
            act.wait_ge(f_act, 1)
            act.activation(f_ln[:, :, :], f_exp[:, :, :], ACT.Ln, bias=1.0).then_inc(f_act, 1)
            act.wait_ge(f_step, 6)
            for r in range(0, P, 32):
                last = act.copy(lf_hi[:, :, r:r + HEADS], f_sp[:, :, :])
            last.then_inc(f_act, 1)
            pair_step(Pos(STEP_B), Pos(B_FOX), Pos(G_FOX), values=Pos(0))
            act.wait_ge(cum_done, 1)
            act.copy(cum[:, :], pv[1][:, :]).then_inc(f_act, 1)
            with act.Fori(0, 2) as i:
                for j in range(2):
                    pair_step(Pos(STEP_FOX + j, i, 2), Pos(B_FOX + 3 * (j + 1), i, 6),
                              Pos(G_FOX + 3 * (j + 1), i, 6), values=Pos(j + 1, i, 2))
            pair_step(Pos(7), Pos(B_FOX + 15), Pos(G_FOX + 15), values=Pos(5))
            pair_step(Pos(8))
            pair_step(Pos(STEP_LAST))
            out_projection(1)
            stats(2)
            root(2)
            finish(2, range(KT))
            feed_forward(1)

        @block.vector
        def _(dve):
            def rest(target, whole, hi):
                return dve.tensor_tensor(target, whole, hi.bitcast(F32), ALU.subtract)

            def prepare(b):
                if b.trip is None and b.base >= B_DN[1][1] + 2 * KT:
                    return
                dve.wait_ge(w_hi_ready, b.at(1))
                rest(w_lo[:, b.slot], w_raw[:, b.slot], w_hi[:, b.slot]).then_inc(w_split, 1)

            def turned_lo(t, h, target, hi, source=None):
                dve.wait_ge(tr_hi, h.at(1))
                rest(target, tr[t.slot][:, :] if source is None else source, hi).then_inc(tr_free, 1)

            def projected(g, q, target, hi, scale=1.0):
                dve.wait_ge(qk_hi, q.at(1))
                source = proj[g.slot][:, 0:target.shape[-1]]
                if scale == 1.0:
                    rest(target, source, hi).then_inc(proj_free[g.slot], 1)
                else:
                    dve.scalar_tensor_tensor(out=target, in0=source, scalar=scale, in1=hi.bitcast(F32),
                                             op0=ALU.mult, op1=ALU.subtract).then_inc(proj_free[g.slot], 1)

            def memory_lo(layer):
                for n in range(4):
                    pair = slice(2 * n, 2 * n + 2)
                    turned_lo(Pos(T_MEM[layer] + n), Pos(H_MEM[layer] + n), mem_lo[layer][:, pair], mem_hi[layer][:, pair],
                              tr[(T_MEM[layer] + n) % 2][:, :].rearrange("p (k m) -> p k m", k=2))

            def memory_keys(layer, c):
                projected(Pos(G_MEM[layer] + c), Pos(Q_MEM[layer] + c), mk_lo[:, c, :], mk_hi[:, c, :])

            def memory_values(layer):
                turned_lo(Pos(T_MV[layer]), Pos(H_MV[layer]), mv_lo[:, :, :], mv_hi[:, :, :],
                          tr[T_MV[layer] % 2][:, :].rearrange("p (m c) -> p m c", m=MT))

            def row_max(s, u):
                dve.wait_ge(sc_done, s.at(u + 1, 8))
                dve.tensor_reduce(neg_max[:, u:u + 1], sc[u % 2][:, 0:keys(s, u) * P], AX.X, ALU.max,
                                  negate=True).then_inc(max_done, 1)

            def normalize(s, u):
                own = probs[:, u % 2, 0:keys(s, u) * P]
                dve.wait_ge(exp_done, s.at(u + 1, 8))
                dve.reciprocal(inv_sum[:, u:u + 1], row_sum[:, u:u + 1]).then_inc(inv_done, 1)
                dve.wait_ge(inv_done, s.at(u + 1, 8))
                dve.tensor_scalar(own, own, inv_sum[:, u:u + 1], None, ALU.mult).then_inc(probs_ready, 1)

            def turned_probs(s, u):
                n, here, t = keys(s, u), slice(u % TT * P, (u % TT + 1) * P), tr_index(s, u)
                hi, lo = p_buffers(s)
                turned_lo(t, hi_index(s, u), lo[:, u // TT, 0:n, here], hi[:, u // TT, 0:n, here],
                          tr[t.slot][:, 0:n * P].rearrange("p (j t) -> p j t", j=n))

            def attended(s, head):
                rows = slice(head * HALF, (head + 1) * HALF)
                tile = bass.ds(step_tile(s), 1)
                dve.wait_ge(mix_hi_ready, s.at(head + 1, 2))
                rest(mix_lo[rows, tile, :], pv[head][rows, :].rearrange("p (a t) -> p a t", a=1),
                     mix_hi[rows, tile, :]).then_inc(mix_ready, 1)

            def gate_stats(n):
                if n == 0:
                    dve.wait_ge(tr_free, T_AV + PAIRS)
                for c in range(2):
                    dve.bn_stats(sgu_stats[:, n, c], z_nat[:, n, c * (DMIX // 2):(c + 1) * (DMIX // 2)]).then_inc(bn_step, 1)
                dve.wait_ge(bn_step, 3 * n + 2)
                dve.bn_aggr(sgu_mv[:, n], sgu_stats[:, n]).then_inc(bn_step, 1)

            def gate_norm(n):
                if n == 0:
                    dve.wait_ge(bn_root, 1)
                    dve.reciprocal(sgu_rstd[:, :], sgu_root[:, :]).then_inc(bn_step, 1)
                    dve.wait_ge(bn_step, 3 * TT + 1)
                dve.tensor_scalar(z_nat[:, n], z_nat[:, n], sgu_mv[:, n, 0:1], sgu_rstd[:, n:n + 1],
                                  ALU.subtract, ALU.mult).then_inc(zn_ready, 1)

            def step_projection(s, g, c, q):
                if s.base < STEP_B:
                    if s.base == STEP_A and c < 2:
                        gate_norm(2 * c)
                        gate_norm(2 * c + 1)
                elif c < 2:
                    j = (g.base - G_FOX) // 3 % 2
                    projected(g, q.plus(c), (q_lo, k_lo)[c][:, j, :], (q_hi, k_hi)[c][:, j, :], SCALE if c == 0 else 1.0)

            def pair_step(s, b=None, g=None, q=None, values=None):
                if fox(s):
                    dve.wait_ge(f_step, 8)
                    dve.tensor_scalar(cum_row[:, :], cum[:, :].bitcast(F32), head_rows[:, bass.ds(step_kind(s).at(), 1)],
                                      None, ALU.mult).then_inc(row_ready, 1)
                for u in range(8):
                    if b is not None and u in (0, 3, 6):
                        prepare(b.plus(u // 3 + 1))
                    row_max(s, u)
                    if u >= 2:
                        turned_probs(s, u - 2)
                    normalize(s, u)
                    if b is not None and u in (2, 5):
                        step_projection(s, g.plus(u // 3), u // 3, q)
                attended(s, 0)
                turned_probs(s, 6)
                turned_probs(s, 7)
                attended(s, 1)
                if values is not None:
                    dve.wait_ge(vt_hi, values.at(1))
                    rest(v_lo[:, values.slot], pv[0][:, :].rearrange("p (t c) -> p t c", t=TT),
                         v_hi[:, values.slot]).then_inc(vt_ready, 1)

            def residual(n, b, g, j, first=True):
                tile = x32_tile(j)
                dve.wait_ge(w_used, b.at(1))
                dve.scalar_tensor_tensor(out=tile, in0=tile, scalar=ALPHA if first else 1.0, in1=proj[g.slot][:, :],
                                         op0=ALU.mult, op1=ALU.add).then_inc(proj_free[g.slot], 1)

            def shift_tile(n, g, j):
                tile = x32_tile(j)
                dve.wait_ge(proj_free[g.slot], g.half(2))
                dve.tensor_tensor(tile, tile, shift[:, :], ALU.subtract).then_inc(shifted, 1)

            def take_shift(n):
                dve.wait_ge(shift_done, n + 1)
                dve.tensor_scalar(shift[:, :], sc[0][:, :], 1.0 / P, None, ALU.mult).then_inc(shift_out, 1)
                dve.wait_ge(shift_out, n + 1)

            def stats(n):
                for q, source in enumerate([total, total_sq]):
                    dve.wait_ge(stat_hi_ready, 2 * n + q + 1)
                    rest(stat_lo[:, q], source[:, :], stat_hi[:, q]).then_inc(stat_ready, 1)

            def moments(n):
                dve.wait_ge(stat_done, 2 * n + 1)
                dve.tensor_scalar(mean[:, :], sc[0][:, :], 1.0 / D, None, ALU.mult).then_inc(ln_step, 1)
                dve.wait_ge(ln_step, 5 * n + 1)
                dve.tensor_tensor(rstd[:, :], mean[:, :], mean[:, :], ALU.mult).then_inc(ln_step, 1)
                dve.wait_ge(ln_step, 5 * n + 2)
                dve.wait_ge(stat_done, 2 * n + 2)
                dve.scalar_tensor_tensor(out=rstd[:, :], in0=sc[1][:, :], scalar=1.0 / D, in1=rstd[:, :],
                                         op0=ALU.mult, op1=ALU.subtract).then_inc(ln_step, 1)
                dve.wait_ge(ln_step, 5 * n + 3)
                dve.wait_ge(ln_root, n + 1)
                dve.reciprocal(rstd[:, :], rstd[:, :]).then_inc(ln_step, 1)
                dve.wait_ge(ln_step, 5 * n + 4)
                dve.tensor_tensor(mean[:, :], mean[:, :], rstd[:, :], ALU.mult).then_inc(ln_step, 1)
                dve.wait_ge(ln_step, 5 * n + 5)

            def finish(n, tiles):
                def lo(k):
                    if n < 3:
                        dve.wait_ge(x_hi_ready, KT * (n + 1) + k + 1)
                        rest(x_lo[:, k], x32[:, k], x_hi[:, k]).then_inc(x_ready, 1)
                tiles = list(tiles)
                for k in tiles:
                    dve.tensor_tensor(x32[:, k], x32[:, k], rstd[:, :], ALU.mult).then_inc(fin_scaled, 1)
                    if k - 2 >= tiles[0]:
                        lo(k - 2)
                for k in tiles[-2:]:
                    lo(k)

            def feed_forward(layer):
                for half in range(2):
                    with dve.Fori(0, FT // 2) as i:
                        for c in range(2):
                            b, g = Pos(B_UP[layer][half] + c, i, 2), Pos(G_UP[layer][half] + c, i, 2)
                            h = Pos((2 * layer + half) * FT + c, i, 2)
                            prepare(b.plus(1))
                            dve.wait_ge(proj_free[g.slot], g.half(2))
                            dve.tensor_tensor(h_raw[:, c], relu[:, c], relu[:, c], ALU.mult).then_inc(relu_sq, 1)
                            dve.wait_ge(relu_sq, h.at(1))
                            dve.wait_ge(h_hi_ready, h.at(1))
                            tile = bass.ds(i * 2 + c, 1)
                            rest(h_lo[:, tile, :], h_raw[:, c:c + 1, :], h_hi[:, tile, :]).then_inc(h_ready, 1)
                    b, g, n = B_DN[layer][half], G_DN[layer][half], 2 * layer + 1
                    if not half:
                        with dve.Fori(0, KT // 2) as i:
                            for j in range(2):
                                for c in range(2):
                                    prepare(Pos(b + 2 * j + c + 1, i, 4))
                                residual(n, Pos(b + 2 * j + 1, i, 4), Pos(g + j, i, 2), Pos(j, i, 2))
                        continue
                    for j in range(2):
                        for c in range(2):
                            prepare(Pos(b + 2 * j + c + 1))
                        residual(n, Pos(b + 2 * j + 1), Pos(g + j), Pos(j), False)
                    take_shift(n)
                    for j in range(2):
                        shift_tile(n, Pos(g + j), Pos(j))
                    with dve.Fori(0, 2) as i:
                        for j in range(2):
                            for c in range(2):
                                prepare(Pos(b + 4 + 2 * j + c + 1, i, 4))
                            residual(n, Pos(b + 4 + 2 * j + 1, i, 4), Pos(g + 2 + j, i, 2), Pos(2 + j, i, 2), False)
                            shift_tile(n, Pos(g + 2 + j, i, 2), Pos(2 + j, i, 2))
                    for j in range(6, KT):
                        for c in range(2):
                            prepare(Pos(b + 2 * j + c + 1))
                        residual(n, Pos(b + 2 * j + 1), Pos(g + j), Pos(j), False)
                        shift_tile(n, Pos(g + j), Pos(j))
                    stats(n)
                    moments(n)
                    finish(n, range(KT))

            def out_projection(layer):
                b, g, n = B_WO[layer], G_WO[layer], 2 * layer
                for j in range(KT):
                    prepare(Pos(b + j + 1))
                    residual(n, Pos(b + j), Pos(g + j), Pos(j))
                    if j == 1:
                        take_shift(n)
                        shift_tile(n, Pos(g), Pos(0))
                    if j > 0:
                        shift_tile(n, Pos(g + j), Pos(j))

            dve.memset(ones_r[:, :].bitcast(F32), 1.0).then_inc(const_r, 1)
            prepare(Pos(0))
            memory_lo(0)
            for c in range(4):
                prepare(Pos(c + 1))
                if c < 2:
                    memory_keys(0, c)
            memory_values(0)
            dve.wait_ge(tr_done, T_PAR + 1)
            dve.tensor_copy(par[:, :], tr[T_PAR % 2][:, 0:64]).then_inc(tr_free, 1)
            for n in range(3):
                four = slice(4 * n, 4 * n + 4)
                turned_lo(Pos(T_WS + n), Pos(H_WS + n), ws_lo[:, four], ws_hi[:, four],
                          tr[(T_WS + n) % 2][:, :].rearrange("p (h t) -> p h t", h=4))
            for k in range(KT + 1):
                if k < KT:
                    dve.wait_ge(tr_done, T_X + k + 1)
                    dve.tensor_copy(x32[:, k], tr[(T_X + k) % 2][:, :]).then_inc(tr_free, 1)
                if k:
                    dve.wait_ge(x_hi_ready, k)
                    rest(x_lo[:, k - 1], x32[:, k - 1], x_hi[:, k - 1]).then_inc(x_ready, 1)
            with dve.Fori(0, PAIRS // 2) as i:
                for c in range(2):
                    prepare(Pos(B_AV + c + 1, i, 2))
                for c in range(2):
                    t = Pos(T_AV + c, i, 2)
                    dve.wait_ge(tr_done, t.at(1))
                    dve.tensor_copy(z_nat[:, :, bass.ds(i * (2 * P) + c * P, P)],
                                    tr[t.slot][:, :].rearrange("p (t c) -> p t c", t=TT)).then_inc(tr_free, 1)
            for c in range(MEMPAIRS):
                prepare(Pos(B_AQ + c + 1))
                projected(Pos(G_AQ + c), Pos(Q_AQ + c), qm_lo[:, c, :], qm_hi[:, c, :], SCALE)
                gate_stats(2 * c)
                gate_stats(2 * c + 1)
            for s in range(2):
                pair_step(Pos(STEP_A + s), Pos(B_AU + 3 * s), Pos(G_AU + 3 * s))
            dve.wait_ge(sgu_landed, 64)
            for j in range(PAIRS + 1):
                if j < PAIRS:
                    dve.wait_ge(z_hi_ready, j + 1)
                    rest(z_lo[:, j % 2], z_nat[:, :, j * P:(j + 1) * P], z_hi[:, j % 2]).then_inc(z_ready, 1)
                for c in range(2):
                    if j:
                        cols = slice(c * 2 * P, (c + 1) * 2 * P)
                        dve.wait_ge(sgu_hi, 2 * (j - 1) + c + 1)
                        rest(mix_lo[:, j - 1, cols], gated[:, c], mix_hi[:, j - 1, cols]).then_inc(sgu_ready, 1)
                for c in range(2):
                    if j == PAIRS:
                        break
                    dve.wait_ge(sgu_done, 2 * j + c + 1)
                    wait(dve, sgu_ready, 2 * (j - 1) + c + 1)
                    mixed = sc[c][:, :].rearrange("p (n h t) -> p n h t", n=2, h=2)
                    for head in range(2):
                        rows = slice(head * HALF, (head + 1) * HALF)
                        last = dve.tensor_tensor(gated[rows, c].rearrange("p (n t) -> p n t", n=2), mixed[rows, :, head],
                                                 bs_all[rows, j:j + 1, :].broadcast_to([HALF, 2, P]), ALU.add)
                    last.then_inc(sgu_added, 1)
            out_projection(0)
            memory_lo(1)
            prepare(Pos(27))
            stats(0)
            memory_keys(1, 0)
            prepare(Pos(28))
            moments(0)
            memory_keys(1, 1)
            prepare(Pos(29))
            finish(0, range(4))
            prepare(Pos(30))
            finish(0, range(4, KT))
            memory_values(1)
            feed_forward(0)

            for c in range(MEMPAIRS):
                prepare(Pos(B_BQ + c + 1))
                projected(Pos(G_BQ + c), Pos(Q_BQ + c), qm_lo[:, c, :], qm_hi[:, c, :], SCALE)
            dve.wait_ge(f_done, 1)
            dve.tensor_tensor(f_log[:, :, :], pv[1][:, 0:TT * HEADS].rearrange("p (t h) -> p t h", t=TT),
                              bf_row[:, :].rearrange("p (a h) -> p a h", a=1).broadcast_to([P, TT, HEADS]), ALU.add).then_inc(f_step, 1)
            dve.wait_ge(f_step, 1)
            dve.scalar_tensor_tensor(out=f_abs[:, :, :], in0=f_log[:, :, :], scalar=-1.0, in1=f_log[:, :, :],
                                     op0=ALU.mult, op1=ALU.min).then_inc(f_step, 1)
            dve.tensor_scalar(f_neg[:, :, :], f_log[:, :, :], -1.0, 0.0, ALU.mult, ALU.max).then_inc(f_step, 1)
            dve.memset(lf_hi[:, :, :].bitcast(F32), 0.0).then_inc(f_step, 1)
            dve.memset(lf_lo[:, :, :].bitcast(F32), 0.0).then_inc(f_step, 1)
            dve.wait_ge(f_step, 3)
            dve.wait_ge(f_act, 2)
            dve.tensor_tensor(f_sp[:, :, :], f_ln[:, :, :], f_neg[:, :, :], ALU.add).then_inc(f_step, 1)
            dve.wait_ge(f_step, 6)
            dve.wait_ge(f_act, 3)
            for r in range(0, P, 32):
                last = rest(lf_lo[:, :, r:r + HEADS], f_sp[:, :, :], lf_hi[:, :, r:r + HEADS])
            last.then_inc(f_step, 1)
            pair_step(Pos(STEP_B), Pos(B_FOX), Pos(G_FOX), Pos(Q_FOX), values=Pos(0))
            dve.wait_ge(f_act, 4)
            for r in (32, 96):
                last = rest(cum[r:r + 32, :], pv[1][r:r + 32, :], cum[r:r + 32, :])
            last.then_inc(f_step, 1)
            with dve.Fori(0, 2) as i:
                for j in range(2):
                    pair_step(Pos(STEP_FOX + j, i, 2), Pos(B_FOX + 3 * (j + 1), i, 6), Pos(G_FOX + 3 * (j + 1), i, 6),
                              Pos(Q_FOX + 2 * (j + 1), i, 4), values=Pos(j + 1, i, 2))
            pair_step(Pos(7), Pos(B_FOX + 15), Pos(G_FOX + 15), Pos(Q_FOX + 10), values=Pos(5))
            pair_step(Pos(8))
            pair_step(Pos(STEP_LAST))
            out_projection(1)
            stats(2)
            moments(2)
            finish(2, range(KT))
            feed_forward(1)
            for k in range(KT):
                dve.wait_ge(tr_done, T_OUT + k + 1)
                dve.tensor_copy(y_nat[:, :, k * P:(k + 1) * P], tr[(T_OUT + k) % 2][:, :].rearrange("p (t c) -> p t c", t=TT))\
                    .then_inc(tr_free, 1)

        @block.gpsimd
        def _(pool):
            steps = [0]

            def behind(instruction):
                steps[0] += 1
                instruction.then_inc(pool_step, 1)
                pool.wait_ge(pool_step, steps[0])

            pool.memset(eps[:, :], LN_EPS)
            behind(pool.memset(ident[:, :], 0.0))
            pool.affine_select(out=ident[:, :], in_=ident[:, :], compare_op=ALU.not_equal, fill=1.0, base=0,
                               pattern=[[-1, P]], channel_multiplier=1).then_inc(const_ready, 1)
            behind(pool.memset(causal[:, :], 0.0))
            pool.affine_select(out=causal[:, :], in_=causal[:, :], compare_op=ALU.is_ge, fill=MASKED, base=0,
                               pattern=[[-1, P]], channel_multiplier=1).then_inc(const_ready, 1)
            behind(pool.memset(tri_f[:, :], 1.0))
            pool.affine_select(out=tri_f[:, :], in_=tri_f[:, :], compare_op=ALU.is_ge, fill=0.0, base=0,
                               pattern=[[1, T]], channel_multiplier=-1).then_inc(const_ready, 1)
            pool.wait_ge(ws_landed, 16)
            pool.affine_select(out=ws_raw[:, :, :], in_=ws_raw[:, :, :], compare_op=ALU.is_ge, fill=0.0, base=0,
                               pattern=[[0, HEADS], [-1, P]], channel_multiplier=1).then_inc(ws_masked, 1)
            behind(pool.memset(head_rows[:, :], 0.0))
            for n, row in enumerate((0, 32, 65, 97)):
                last = pool.affine_select(out=head_rows[:, :], in_=head_rows[:, :], compare_op=ALU.not_equal, fill=1.0,
                                          base=-row, pattern=[[-2, PAIRS]], channel_multiplier=1)
                if n < 3:
                    behind(last)
            last.then_inc(const_ready, 1)
            pool.wait_ge(wf_landed, 32)
            pool.tensor_copy(wf_hi[:, :, :], wf_raw[:, :, :]).then_inc(wf_hi_ready, 1)
            pool.wait_ge(wf_hi_ready, 1)
            pool.tensor_tensor(wf_lo[:, :, :], wf_raw[:, :, :], wf_hi[:, :, :].bitcast(F32), ALU.subtract).then_inc(wf_ready, 1)

            pool.wait_ge(sgu_landed, 64)
            for n in range(TT):
                pool.wait_ge(zn_ready, n + 1)
                pool.tensor_tensor(z_nat[:, n], z_nat[:, n], g_all[:, :], ALU.mult).then_inc(zg_step, 1)
                pool.wait_ge(zg_step, n + 1)
                pool.tensor_tensor(z_nat[:, n], z_nat[:, n], b_all[:, :], ALU.add).then_inc(zg_ready, 1)
            for j in range(PAIRS):
                for c in range(2):
                    pool.wait_ge(sgu_added, 2 * j + c + 1)
                    pool.wait_ge(u_ready, j + 1)
                    pool.tensor_tensor(gated[:, c], gated[:, c], u_t[:, j, c * 2 * P:(c + 1) * 2 * P], ALU.mult)\
                        .then_inc(sgu_gated, 1)

            def add_tile(n, j, first=False):
                for source, done, added, sums in ((x32_tile(j), shifted, sum_added, total),
                                                  (square[:, j.slot, :], sq_ready, sq_added, total_sq)):
                    pool.wait_ge(done, j.at(KT * n + 1))
                    if first:
                        pool.tensor_copy(sums[:, :], source).then_inc(added, 1)
                    else:
                        pool.wait_ge(added, j.at(KT * n))
                        pool.tensor_tensor(sums[:, :], sums[:, :], source, ALU.add).then_inc(added, 1)

            def layer_norm(n):
                add_tile(n, Pos(0), True)
                add_tile(n, Pos(1))
                with pool.Fori(0, KT // 2 - 1) as i:
                    for j in range(2):
                        add_tile(n, Pos(2 + j, i, 2))
                pool.wait_ge(ln_step, 5 * (n + 1))
                for k in range(KT):
                    pool.wait_ge(fin_scaled, KT * n + k + 1)
                    pool.tensor_tensor(x32[:, k], x32[:, k], mean[:, :], ALU.subtract).then_inc(fin_moved, 1)

            for n in range(4):
                layer_norm(n)


_INS = ["x", "mem", "a_w_in", "a_sgu_ln_g", "a_sgu_ln_b", "a_w_s", "a_b_s", "kv_w", "kv_b_f", "b_w_q",
        "mem_w_kv", "w_o", "ln_g", "ln_b", "w_up", "w_down"]


def kernel(**inputs):
    import numpy as np
    import concourse.bacc as bacc
    from concourse.bass_utils import run_bass_kernel_spmd

    nc = bacc.Bacc("TRN2", target_bir_lowering=False, num_devices=1)
    arrays, args = {}, []
    for name in _INS:
        a = np.ascontiguousarray(inputs[name])
        arrays[f"in_{name}"] = a
        args.append(nc.dram_tensor(f"in_{name}", a.shape, mybir.dt.from_np(a.dtype), kind="ExternalInput").ap())
    out = nc.dram_tensor("out_y", inputs["x"].shape, F32, kind="ExternalOutput").ap()
    trunk_kernel(nc, *args, out)
    result = run_bass_kernel_spmd(nc, [arrays], core_ids=[0])
    return result.results[0]["out_y"]
```

```python
from contextlib import ExitStack

import concourse.bass as bass
from concourse import mybir
from concourse.alu_op_type import AluOpType as ALU

ACT = mybir.ActivationFunctionType
AX = mybir.AxisListType
F32 = mybir.dt.float32
F32R = mybir.dt.float32r

P = 128
HALF = P // 2
MASKED = -1.0e37
LN_EPS = 1e-5


class Pos:

    def __init__(self, base, trip=None, step=0):
        self.base, self.trip, self.step = base, trip, step

    def at(self, off=0, mul=1):
        n = self.base * mul + off
        return n if self.trip is None else self.trip * (self.step * mul) + n

    def half(self, off=0):
        n = (self.base + off) // 2
        return n if self.trip is None else self.trip * (self.step // 2) + n

    def plus(self, off):
        return Pos(self.base + off, self.trip, self.step)

    def times(self, mul, off=0):
        return Pos(self.base * mul + off, self.trip, self.step * mul)

    @property
    def slot(self):
        return self.base % 2


def wait(engine, semaphore, value):
    if not (isinstance(value, int) and value <= 0):
        engine.wait_ge(semaphore, value)


def trunk_kernel(nc, x, mem, a_w_in, a_sgu_ln_g, a_sgu_ln_b, a_w_s, a_b_s, kv_w, kv_b_f, b_w_q,
                 mem_w_kv, w_o, ln_g, ln_b, w_up, w_down, out):
    _, T, D = x.shape
    M = mem.shape[1]
    KT = D // P
    TT = T // P
    MT = M // P
    HEADS = a_w_s.shape[1]
    PAIRS = HEADS // 2
    DMIX = HEADS * HALF
    MEMPAIRS = (D - DMIX) // P
    FF = w_up.shape[2]
    FT = FF // P // 2
    SCALE = float(HALF) ** -0.5
    ALPHA = float(2 * w_up.shape[0]) ** 0.25
    assert (T, D, M, HEADS, FF) == (512, 1024, 256, 12, 4096) and a_w_s.shape[2] == P

    B_MEM = [[0, 1, 2, 3], [26, 27, 92, 93]]
    G_MEM = [[0, 1, 2, 3], [26, 27, 76, 77]]
    B_AV = G_AV = 4
    B_AQ = G_AQ = 10
    B_AU = G_AU = 12
    B_WO, G_WO = [18, 114], [18, 98]
    B_UP = [[28, 60], [122, 154]]
    G_UP = [[28, 52], [106, 130]]
    B_DN = [[44, 76], [138, 170]]
    G_DN = [[44, 68], [122, 146]]
    B_BQ, G_BQ = 94, 78
    B_FOX, G_FOX = 96, 80

    STEP_A, STEP_B, STEP_FOX, STEP_LAST = 0, 2, 3, 9
    T_MEM, T_MV, T_PAR, T_WS, T_X, T_AV = [0, 39], [4, 43], 5, 6, 9, 17
    T_STEP = [23, 28]
    T_OUT = 108
    H_MEM, H_MV, H_WS = [0, 24], [4, 28], 5
    H_STEP = [8, 13]
    Q_MEM, Q_AQ, Q_BQ, Q_FOX = [0, 4], 2, 6, 8

    ctx = ExitStack()
    with ctx:
        def psum(name):
            return ctx.enter_context(nc.psum_tensor(name, [P, 512], F32))

        def sem(name):
            return ctx.enter_context(nc.semaphore(name))

        base = [(nc.sbuf_base + 63) // 64 * 64]

        def put(name, shape, dtype, offset=None):
            size = 4
            for n in shape[1:]:
                size *= n
            if offset is None:
                offset = base[0]
                base[0] += (size + 63) // 64 * 64
            assert offset + size <= nc.sbuf_usable_end, (name, offset + size)
            return nc.alloc_sbuf_tensor_at(name, shape, dtype, offset=offset)

        K1 = 1024
        X0 = base[0]
        x_hi = put("x_hi", [P, KT, T], F32R)
        x_lo = put("x_lo", [P, KT, T], F32R)
        w_hi = put("w_hi", [P, 2, KT, P], F32R)
        w_lo = put("w_lo", [P, 2, KT, P], F32R)
        x32 = put("x32", [P, KT, T], F32)
        w_raw = put("w_raw", [P, 2, KT, P], F32)
        mk_hi = put("mk_hi", [P, MEMPAIRS, M], F32R)
        mk_lo = put("mk_lo", [P, MEMPAIRS, M], F32R)
        mv_hi = put("mv_hi", [P, MT, MEMPAIRS * P], F32R)
        mv_lo = put("mv_lo", [P, MT, MEMPAIRS * P], F32R)
        ident = put("ident", [P, P], F32)
        ident_r = put("ident_r", [P, P], F32R)
        ones_r = put("ones_r", [P, P], F32R)
        ones_f = put("ones_f", [P, P], F32)
        causal = put("causal", [P, P], F32)
        causal_r = put("causal_r", [P, P], F32R)
        tri_r = put("tri_r", [P, T], F32R)
        head_rows = put("head_rows", [P, PAIRS], F32)
        eps = put("eps", [P, 1], F32)
        par_raw = put("par_raw", [64, P], F32)
        par = put("par", [P, 64], F32)
        neg_max = put("neg_max", [P, 8], F32)
        row_sum = put("row_sum", [P, 8], F32)
        inv_sum = put("inv_sum", [P, 8], F32)
        sgu_stats = put("sgu_stats", [P, TT, 2, 6], F32)
        sgu_mv = put("sgu_mv", [P, TT, 2], F32)
        sgu_root = put("sgu_root", [P, TT], F32)
        sgu_rstd = put("sgu_rstd", [P, TT], F32)
        wf_raw = put("wf_raw", [P, KT, HEADS], F32)
        wf_hi = put("wf_hi", [P, KT, HEADS], F32R)
        wf_lo = put("wf_lo", [P, KT, HEADS], F32R)
        bf_row = put("bf_row", [P, HEADS], F32)
        v_tmp = put("v_tmp", [P, 2, T], F32)
        probs = put("probs", [P, 2, T], F32)
        top = base[0]

        mix_hi = put("mix_hi", [P, KT, T], F32R, top)
        mix_lo = put("mix_lo", [P, KT, T], F32R, top + 16 * K1)
        qm_hi = put("qm_hi", [P, MEMPAIRS, T], F32R, top + 32 * K1)
        qm_lo = put("qm_lo", [P, MEMPAIRS, T], F32R, top + 36 * K1)
        A0 = top + 40 * K1
        u_t = put("u_t", [P, PAIRS, T], F32, A0)
        z_nat = put("z_nat", [P, TT, DMIX], F32, A0 + 12 * K1)
        pa_hi = put("pa_hi", [P, 2, MT, T], F32R, A0 + 24 * K1)
        pa_lo = put("pa_lo", [P, 2, MT, T], F32R, A0 + 32 * K1)
        z_hi = put("z_hi", [P, 2, TT, P], F32R, A0 + 40 * K1)
        z_lo = put("z_lo", [P, 2, TT, P], F32R, A0 + 44 * K1)
        gated = put("gated", [P, 2, 2 * P], F32, A0 + 48 * K1)
        ws_hi = put("ws_hi", [P, HEADS, P], F32R, A0 + 50 * K1)
        ws_lo = put("ws_lo", [P, HEADS, P], F32R, A0 + 56 * K1)
        bs_all = put("bs_all", [P, PAIRS, P], F32, A0 + 62 * K1)
        g_all = put("g_all", [P, DMIX], F32, A0 + 65 * K1)
        b_all = put("b_all", [P, DMIX], F32, A0 + 68 * K1)
        memt_hi = put("memt_hi", [P, KT, M], F32R, top)
        memt_lo = put("memt_lo", [P, KT, M], F32R, top + 8 * K1)
        mem_nat = put("mem_nat", [P, MT, D], F32, top + 16 * K1)
        ws_raw = put("ws_raw", [P, HEADS, P], F32, top + 24 * K1)
        x_nat = put("x_nat", [P, TT, D], F32, top + 30 * K1)
        tri_f = put("tri_f", [P, T], F32, A0 + 12 * K1)
        q_hi = put("q_hi", [P, 2, T], F32R, A0)
        q_lo = put("q_lo", [P, 2, T], F32R, A0 + 4 * K1)
        k_hi = put("k_hi", [P, 2, T], F32R, A0 + 8 * K1)
        k_lo = put("k_lo", [P, 2, T], F32R, A0 + 12 * K1)
        v_hi = put("v_hi", [P, 2, TT, P], F32R, A0 + 16 * K1)
        v_lo = put("v_lo", [P, 2, TT, P], F32R, A0 + 20 * K1)
        pb_hi = put("pb_hi", [P, 2, TT, T], F32R, A0 + 24 * K1)
        pb_lo = put("pb_lo", [P, 2, TT, T], F32R, A0 + 40 * K1)
        cum = put("cum", [P, T], F32R, A0 + 56 * K1)
        cum_row = put("cum_row", [P, T], F32R, A0 + 58 * K1)
        f_turned = put("f_turned", [P, T], F32, A0 + 58 * K1)
        lf_hi = put("lf_hi", [P, TT, P], F32R, A0 + 62 * K1)
        lf_lo = put("lf_lo", [P, TT, P], F32R, A0 + 64 * K1)
        f_log = put("f_log", [P, TT, HEADS], F32, A0 + 66 * K1)
        f_abs = put("f_abs", [P, TT, HEADS], F32, A0 + 66 * K1 + 256)
        f_neg = put("f_neg", [P, TT, HEADS], F32, A0 + 66 * K1 + 512)
        f_exp = put("f_exp", [P, TT, HEADS], F32, A0 + 66 * K1 + 768)
        f_ln = put("f_ln", [P, TT, HEADS], F32, A0 + 67 * K1)
        f_sp = put("f_sp", [P, TT, HEADS], F32, A0 + 67 * K1 + 256)
        h_hi = put("h_hi", [P, FT, T], F32R, top)
        h_lo = put("h_lo", [P, FT, T], F32R, top + 32 * K1)
        L0 = top + 64 * K1
        shift = put("shift", [P, T], F32, L0)
        shift_in = put("shift_in", [P, T], F32R, L0 + 2 * K1)
        total = put("total", [P, T], F32, L0 + 4 * K1)
        total_sq = put("total_sq", [P, T], F32, L0 + 6 * K1)
        square = put("square", [P, 2, T], F32, L0 + 8 * K1)
        spread = put("spread", [P, 2, TT, P], F32, L0 + 12 * K1)
        ln_mean = put("ln_mean", [P, TT], F32, L0 + 16 * K1)
        ln_var = put("ln_var", [P, TT], F32, L0 + 16 * K1 + 64)
        ln_sqrt = put("ln_sqrt", [P, TT], F32, L0 + 16 * K1 + 128)
        ln_rstd = put("ln_rstd", [P, TT], F32, L0 + 16 * K1 + 192)
        ln_move = put("ln_move", [P, TT], F32, L0 + 16 * K1 + 256)
        relu = put("relu", [P, 2, T], F32, L0 + 24 * K1)
        h_raw = put("h_raw", [P, 2, T], F32, L0 + 28 * K1)
        mem2_nat = put("mem2_nat", [P, MT, D], F32, L0 + 24 * K1)
        memt2_hi = put("memt2_hi", [P, KT, M], F32R, L0 + 32 * K1)
        memt2_lo = put("memt2_lo", [P, KT, M], F32R, L0 + 40 * K1)
        y_nat = put("y_nat", [P, TT, D], F32, X0)
        g_out = put("g_out", [P, D], F32, L0 + 32 * K1)
        b_out = put("b_out", [P, D], F32, L0 + 36 * K1)
        y_stats = put("y_stats", [P, TT, KT, 6], F32, L0 + 40 * K1)
        y_in = put("y_in", [P, 2, T], F32, L0 + 44 * K1)
        y_mv = put("y_mv", [P, TT, 2], F32, L0 + 41 * K1)
        y_root = put("y_root", [P, TT], F32, L0 + 41 * K1 + 64)
        y_rstd = put("y_rstd", [P, TT], F32, L0 + 41 * K1 + 128)
        y_move = put("y_move", [P, TT], F32, L0 + 41 * K1 + 192)
        mem_in = [mem_nat, mem2_nat]
        mem_hi, mem_lo = [memt_hi, memt2_hi], [memt_lo, memt2_lo]

        proj = [psum("proj0"), psum("proj1")]
        sc = [psum("sc0"), psum("sc1")]
        tr = [psum("tr0"), psum("tr1")]
        pv = [psum("pv0"), psum("pv1")]

        w_landed = [sem("w_landed0"), sem("w_landed1")]
        w_hi_ready, w_split = sem("w_hi_ready"), sem("w_split")
        w_used = sem("w_used")
        proj_free = [sem("proj_free0"), sem("proj_free1")]
        qk_hi = sem("qk_hi")
        tr_done, tr_hi, tr_free = sem("tr_done"), sem("tr_hi"), sem("tr_free")
        x_split, x_hi_ready, x_ready = sem("x_split"), sem("x_hi_ready"), sem("x_ready")
        mem_landed, x_landed, ws_landed = sem("mem_landed"), sem("x_landed"), sem("ws_landed")
        par_landed, sgu_landed, wf_landed = sem("par_landed"), sem("sgu_landed"), sem("wf_landed")
        const_ready, const_r, ws_masked = sem("const_ready"), sem("const_r"), sem("ws_masked")
        pool_step = sem("pool_step")
        bn_step, zn_ready, zg_ready = sem("bn_step"), sem("zn_ready"), sem("zg_ready")
        zg_step = sem("zg_step")
        z_hi_ready, z_ready = sem("z_hi_ready"), sem("z_ready")
        sgu_done, sgu_added, sgu_gated = sem("sgu_done"), sem("sgu_added"), sem("sgu_gated")
        sgu_hi, sgu_ready = sem("sgu_hi"), sem("sgu_ready")
        sc_done, max_done, exp_done = sem("sc_done"), sem("max_done"), sem("exp_done")
        inv_done, probs_ready = sem("inv_done"), sem("probs_ready")
        pv_done, mix_hi_ready, mix_ready = sem("pv_done"), sem("mix_hi_ready"), sem("mix_ready")
        vt_done, vt_hi, vt_ready = sem("vt_done"), sem("vt_hi"), sem("vt_ready")
        row_ready = sem("row_ready")
        wf_hi_ready, wf_ready = sem("wf_hi_ready"), sem("wf_ready")
        f_done, f_out, f_step, f_act, cum_done = sem("f_done"), sem("f_out"), sem("f_step"), sem("f_act"), sem("cum_done")
        relu_sq, h_hi_ready, h_ready = sem("relu_sq"), sem("h_hi_ready"), sem("h_ready")
        shift_ready, shift_done, shifted = sem("shift_ready"), sem("shift_done"), sem("shifted")
        shift_out, pre_shifted = sem("shift_out"), sem("pre_shifted")
        sq_ready, sum_added, sq_added = sem("sq_ready"), sem("sum_added"), sem("sq_added")
        stat_done, spread_ready, spread_done = sem("stat_done"), sem("spread_ready"), sem("spread_done")
        ln_step, ln_root = sem("ln_step"), sem("ln_root")
        bn_root, u_ready = sem("bn_root"), sem("u_ready")
        fin_scaled, fin_moved, fin_ready = sem("fin_scaled"), sem("fin_moved"), sem("fin_ready")
        y_counted, y_step, y_rooted = sem("y_counted"), sem("y_step"), sem("y_rooted")
        y_centred, y_scaled, y_gained = sem("y_centred"), sem("y_scaled"), sem("y_gained")
        y_done, y_last, y_stored = sem("y_done"), sem("y_last"), sem("y_stored")
        out_landed = sem("out_landed")

        block = ctx.enter_context(nc.Block())

        def x32_tile(j):
            if j.trip is None:
                return x32[:, j.base, :]
            return x32[:, bass.ds(j.at(), 1), :].rearrange("p a t -> p (a t)")

        def tr_index(s, u):
            return s.times(8, T_STEP[s.base >= STEP_B] + u)

        def hi_index(s, u):
            return s.times(8, H_STEP[s.base >= STEP_B] + u)

        def fox(s):
            return STEP_FOX <= s.base < STEP_LAST

        def step_kind(s):
            return s.plus(-STEP_FOX) if fox(s) else Pos({0: 0, 1: 1, STEP_B: 0, STEP_LAST: 1}[s.base])

        def step_tile(s):
            return step_kind(s).at() if fox(s) else PAIRS + step_kind(s).at()

        def keys(s, u):
            return u % TT + 1 if fox(s) else MT

        def p_buffers(s):
            return (pb_hi, pb_lo) if s.base >= STEP_B else (pa_hi, pa_lo)

        @block.sync
        def _(sp):
            def load(b, source):
                wait(sp, w_split, b.at(-1))
                sp.dma_start(w_raw[:, b.slot], source).then_inc(w_landed[b.slot], 16)

            def cols(w, c, r=0):
                return w[r:r + D, bass.ds(c, P)].rearrange("(k p) n -> p k n", p=P)

            def memory_weights(layer, parts):
                for c in parts:
                    load(Pos(B_MEM[layer][c]), cols(mem_w_kv[layer], c * P))

            def feed_forward(layer):
                for half in range(2):
                    with sp.Fori(0, FT // 2) as i:
                        for c in range(2):
                            load(Pos(B_UP[layer][half] + c, i, 2),
                                 cols(w_up[layer], i * (2 * P) + (half * FT + c) * P))
                    with sp.Fori(0, KT) as i:
                        for c in range(2):
                            load(Pos(B_DN[layer][half] + c, i, 2),
                                 cols(w_down[layer], i * P, (half * 2 + c) * D))

            memory_weights(0, range(4))
            with sp.Fori(0, PAIRS // 2) as i:
                for c in range(2):
                    load(Pos(B_AV + c, i, 2), cols(a_w_in[0], i * (2 * P) + DMIX + c * P))
            for c in range(MEMPAIRS):
                load(Pos(B_AQ + c), cols(a_w_in[0], 2 * DMIX + c * P))
            with sp.Fori(0, PAIRS // 2) as i:
                for c in range(2):
                    load(Pos(B_AU + c, i, 2), cols(a_w_in[0], i * (2 * P) + c * P))
            with sp.Fori(0, KT // 2) as i:
                for c in range(2):
                    load(Pos(B_WO[0] + c, i, 2), cols(w_o[0], i * (2 * P) + c * P))
            memory_weights(1, range(2))
            feed_forward(0)
            memory_weights(1, range(2, 4))
            for c in range(MEMPAIRS):
                load(Pos(B_BQ + c), cols(b_w_q[0], DMIX + c * P))
            with sp.Fori(0, PAIRS // 2) as i:
                for j in range(2):
                    load(Pos(B_FOX + 3 * j, i, 6), cols(b_w_q[0], i * (2 * P) + j * P))
                    load(Pos(B_FOX + 3 * j + 1, i, 6), cols(kv_w, i * (2 * P) + j * P))
                    load(Pos(B_FOX + 3 * j + 2, i, 6), cols(kv_w, i * (2 * P) + DMIX + j * P))
            with sp.Fori(0, KT // 2) as i:
                for c in range(2):
                    load(Pos(B_WO[1] + c, i, 2), cols(w_o[1], i * (2 * P) + c * P))
            feed_forward(1)
            rows = out[0].rearrange("(t p) d -> p t d", p=P)
            for t in range(TT):
                for c in range(2):
                    half = slice(c * D // 2, (c + 1) * D // 2)
                    if t < TT - 1:
                        sp.wait_ge(y_done, 2 * t + c + 1)
                    else:
                        sp.wait_ge(y_last, c + 1)
                    sp.dma_start(rows[:, t, half], y_nat[:, t, half]).then_inc(y_stored, 16)
            sp.wait_ge(y_stored, 32 * TT)

        @block.tensor
        def _(pe):
            def products(target, terms, start=True, stop=True):
                for n, (lhs, rhs) in enumerate(terms):
                    last = pe.matmul(target, lhs, rhs, start=start and n == 0,
                                     stop=stop and n == len(terms) - 1)
                return last

            def block_terms(b, k, hi, lo):
                return [(w_hi[:, b.slot, k], hi), (w_hi[:, b.slot, k], lo), (w_lo[:, b.slot, k], hi)]

            def project(b, g, hi, lo, columns=T, order=range(KT), ready=None, parts=(0, KT),
                        start=True, stop=True):
                bank = proj[g.slot]
                for n in range(*parts):
                    k = order[n]
                    if n == 0:
                        pe.wait_ge(w_split, b.at(1))
                        if start:
                            wait(pe, proj_free[g.slot], g.half())
                    if ready:
                        ready(n)
                    last = products(bank[:, 0:columns], block_terms(b, k, hi[:, k], lo[:, k]),
                                    start and n == 0, stop and n == KT - 1)
                if parts[1] == KT:
                    last.then_inc(w_used, 1)

            def transposes(t, pieces):
                wait(pe, tr_free, t.at(-1))
                at = 0
                for piece in pieces:
                    rows, n = piece.shape[0], piece.shape[-1]
                    last = pe.transpose(tr[t.slot][0:n, at:at + rows], piece, ident[0:rows, 0:rows])
                    at += rows
                last.then_inc(tr_done, 1)

            def memory_transposes(layer, n):
                pe.wait_ge(mem_landed, 16 * (layer + 1))
                transposes(Pos(T_MEM[layer] + n), [mem_in[layer][:, m, k * P:(k + 1) * P]
                                                   for k in (2 * n, 2 * n + 1) for m in range(MT)])

            def memory_projection(layer, c, parts=(0, KT)):
                if c == 0:
                    pe.wait_ge(tr_free, T_MEM[layer] + 4)
                project(Pos(B_MEM[layer][c]), Pos(G_MEM[layer][c]), mem_hi[layer], mem_lo[layer], M, parts=parts)

            def memory_values(layer):
                for c in range(2, 4):
                    g = Pos(G_MEM[layer][c])
                    pe.wait_ge(proj_free[g.slot], g.half(2))
                transposes(Pos(T_MV[layer]), [v_tmp[:, c, m * P:(m + 1) * P] for m in range(MT) for c in range(2)])

            def scores(s, u):
                head, i, n = u // TT, u % TT, keys(s, u) * P
                rows = slice(head * HALF, (head + 1) * HALF)
                here = slice(i * P, (i + 1) * P)
                wait(pe, exp_done, s.at(u - 1, 8))
                bank = sc[u % 2]
                if fox(s):
                    c = step_kind(s).slot
                    if u == 0:
                        g = step_kind(s).times(3, G_FOX)
                        for q in (g, g.plus(1)):
                            pe.wait_ge(proj_free[q.slot], Pos(q.base, q.trip, q.step).half(2))
                        pe.wait_ge(row_ready, step_kind(s).at(1))
                    products(bank[:, 0:n], [(ones_r[rows, :], cum_row[rows, 0:n])], stop=False)
                    products(bank[:, here], [(ident_r[:, :], causal_r[:, :])], start=False, stop=False)
                    qh, ql, kh, kl = q_hi[rows, c, here], q_lo[rows, c, here], k_hi[rows, c, 0:n], k_lo[rows, c, 0:n]
                else:
                    c = step_kind(s).at()
                    qh, ql, kh, kl = qm_hi[rows, c, here], qm_lo[rows, c, here], mk_hi[rows, c, :], mk_lo[rows, c, :]
                products(bank[:, 0:n], [(qh, kl), (ql, kh), (qh, kh)], start=not fox(s)).then_inc(sc_done, 1)

            def turn(s, u):
                pe.wait_ge(probs_ready, s.at(u + 1, 8))
                transposes(tr_index(s, u), [probs[:, u % 2, j * P:(j + 1) * P] for j in range(keys(s, u))])

            def attend(s, head):
                pe.wait_ge(tr_free, tr_index(s, head * TT + TT - 1).at(1))
                wait(pe, mix_ready, s.at(head - 1, 2))
                if s.base == STEP_B and head == 1:
                    pe.wait_ge(f_step, 1)
                hi, lo = p_buffers(s)
                c = step_kind(s).slot
                if fox(s) and head == 0:
                    pe.wait_ge(vt_ready, step_kind(s).at(1))
                tiles = TT if fox(s) else MT
                for j in range(tiles):
                    seen = slice(j * P if fox(s) else 0, T)
                    if fox(s):
                        vh, vl = v_hi[:, c, j], v_lo[:, c, j]
                    else:
                        vh, vl = mv_hi[:, j, c * P:(c + 1) * P], mv_lo[:, j, c * P:(c + 1) * P]
                    ph, pl = hi[:, head, j, seen], lo[:, head, j, seen]
                    last = products(pv[head][:, seen], [(vh, ph), (vh, pl), (vl, ph)], j == 0, j == tiles - 1)
                last.then_inc(pv_done, 1)

            def turn_values(s, j):
                g = j.times(3, G_FOX + 2)
                pe.wait_ge(proj_free[g.slot], g.half(2))
                if s is not None:
                    pe.wait_ge(mix_ready, s.at(1, 2))
                for t in range(TT):
                    last = pe.transpose(pv[0][:, t * P:(t + 1) * P], v_tmp[:, g.slot, t * P:(t + 1) * P], ident[:, :])
                last.then_inc(vt_done, 1)

            def pair_step(s, b=None, g=None, values=None, extra=None):
                at = [0, 3, 6, 8, 11, 14, 16, 18, 19, 21, 24]

                def filler(n):
                    if b is not None:
                        c = at[n] // KT
                        project(b.plus(c), g.plus(c), x_hi, x_lo, parts=(at[n] - c * KT, at[n + 1] - c * KT))
                    elif extra and n in extra:
                        out_start(1, *extra[n])
                for u in range(8):
                    filler(u)
                    if u >= 2:
                        turn(s, u - 2)
                    scores(s, u)
                attend(s, 0)
                turn(s, 6)
                filler(8)
                turn(s, 7)
                filler(9)
                attend(s, 1)
                if values is not None:
                    turn_values(s, values)

            def project_two(b, g, hi, lo, ready):
                for n in range(KT + 3):
                    if n < KT:
                        project(b, g, hi, lo, ready=ready, parts=(n, n + 1))
                    if n >= 3:
                        project(b.plus(1), g.plus(1), hi, lo, parts=(n - 3, n - 2))

            out_order = [[6, 7, 0, 1, 2, 3, 4, 5], [6, 0, 1, 2, 3, 4, 5, 7]]

            def out_start(layer, c, n):
                def ready(n):
                    if layer:
                        pe.wait_ge(mix_ready, 2 * (STEP_B + n) + 2)
                    elif n < 2:
                        pe.wait_ge(mix_ready, 2 * n + 2)
                    else:
                        pe.wait_ge(sgu_ready, 2 * (n - 1))
                project(Pos(B_WO[layer] + c), Pos(G_WO[layer] + c), mix_hi, mix_lo, order=out_order[layer],
                        ready=ready, parts=(n, n + 1))

            def out_projection(layer):
                for j in range(2, KT):
                    project(Pos(B_WO[layer] + j), Pos(G_WO[layer] + j), mix_hi, mix_lo, order=out_order[layer])
                    if j == 2:
                        shift_sum(2 * layer)
                    if layer == 0 and j < 6:
                        memory_transposes(1, j - 2)

            def shift_sum(n):
                pe.wait_ge(shift_ready, n + 1)
                products(sc[0][:, :], [(ones_r[:, :], shift_in[:, :])]).then_inc(shift_done, 1)

            def layer_sums(n, g):
                for bank, added, sums, done, count, last_tile in (
                        (sc[0], sum_added, total, proj_free[g % 2], g // 2 + 1, x32[:, KT - 1]),
                        (sc[1], sq_added, total_sq, sq_ready, KT * (n + 1), square[:, 1])):
                    for part in (sums, last_tile):
                        if part is sums:
                            pe.wait_ge(added, (KT - 1) * (n + 1))
                        else:
                            pe.wait_ge(done, count)
                        for t in range(TT):
                            last = pe.matmul(bank[:, t:t + 1], part[:, t * P:(t + 1) * P], ones_f[:, 0:1],
                                             start=part is sums and t == 0, stop=part is last_tile,
                                             skip_group_check=True)
                    last.then_inc(stat_done, 1)

            def layer_spread(n):
                for q in range(2):
                    pe.wait_ge(spread_ready, 2 * n + q + 1)
                    products(sc[q][:, :], [(ones_f[:, :], spread[:, q])]).then_inc(spread_done, 1)

            def turn_result(j, g):
                pe.wait_ge(proj_free[g.slot], g.half(2))
                transposes(j.plus(T_OUT), [y_in[:, j.slot, t * P:(t + 1) * P] for t in range(TT)])

            def feed_forward(layer):
                for half in range(2):
                    b, g = Pos(B_UP[layer][half]), Pos(G_UP[layer][half])
                    first = KT * (2 * layer + 1)
                    if half:
                        for c in range(2):
                            project(b.plus(c), g.plus(c), x_hi, x_lo)
                    else:
                        project_two(b, g, x_hi, x_lo, ready=lambda n: pe.wait_ge(x_ready, first + n + 1))
                    with pe.Fori(0, FT // 2 - 1) as i:
                        for c in range(2, 4):
                            project(Pos(b.base + c, i, 2), Pos(g.base + c, i, 2), x_hi, x_lo)
                    b, g = B_DN[layer][half], G_DN[layer][half]
                    h0 = (2 * layer + half) * FT

                    def down(b, g, ready=False):
                        for c in range(2):
                            project(b.plus(c), g, h_hi[:, c * KT:(c + 1) * KT], h_lo[:, c * KT:(c + 1) * KT],
                                    ready=(lambda n: pe.wait_ge(h_ready, h0 + c * KT + n + 1)) if ready else None,
                                    start=c == 0, stop=c == 1)
                    if half and layer:
                        down(Pos(b), Pos(g), True)
                        down(Pos(b + 2), Pos(g + 1))
                        turn_result(Pos(0), Pos(g))
                        with pe.Fori(0, KT // 2 - 1) as i:
                            for j in range(2, 4):
                                down(Pos(b + 2 * j, i, 4), Pos(g + j, i, 2))
                                turn_result(Pos(j - 1, i, 2), Pos(g + j - 1, i, 2))
                        turn_result(Pos(KT - 1), Pos(g + KT - 1))
                        continue
                    for j in range(2):
                        down(Pos(b + 2 * j), Pos(g + j), j == 0)
                    if half:
                        shift_sum(2 * layer + 1)
                    with pe.Fori(0, KT // 2 - 1) as i:
                        for j in range(2):
                            down(Pos(b + 4 + 2 * j, i, 4), Pos(g + 2 + j, i, 2))

            def spatial_gate():
                pe.wait_ge(exp_done, 16)
                for j in range(PAIRS):
                    pe.wait_ge(z_ready, j + 1)
                    both = slice(2 * j, 2 * j + 2)
                    for c in range(2):
                        wait(pe, sgu_added, 2 * (j - 1) + c + 1)
                        for n in range(2):
                            zh, zl = z_hi[:, j % 2, 2 * c + n], z_lo[:, j % 2, 2 * c + n]
                            last = products(sc[c][:, n * 2 * P:(n + 1) * 2 * P],
                                            [(zh, ws_hi[:, both]), (zh, ws_lo[:, both]), (zl, ws_hi[:, both])])
                        last.then_inc(sgu_done, 1)
                    out_start(0, 0, j)
                    if j >= 2:
                        out_start(0, 1, j - 2)

            def forget_gate():
                pe.wait_ge(wf_ready, 1)
                terms = []
                for k in range(KT):
                    terms += [(wf_hi[:, k], x_hi[:, k]), (wf_hi[:, k], x_lo[:, k]), (wf_lo[:, k], x_hi[:, k])]
                products(pv[1][0:HEADS, :], terms).then_inc(f_done, 1)

            def turn_forget_gate():
                pe.wait_ge(f_out, 1)
                for t in range(TT):
                    last = pe.transpose(pv[1][:, t * HEADS:(t + 1) * HEADS], f_turned[0:HEADS, t * P:(t + 1) * P],
                                        ident[0:HEADS, 0:HEADS])
                last.then_inc(f_done, 1)

            def cumulate():
                pe.wait_ge(f_act, 3)
                pe.wait_ge(f_step, 7)
                pe.wait_ge(mix_ready, 2 * STEP_B + 2)
                for t in range(TT):
                    span = tri_r[:, 0:T - t * P]
                    last = products(pv[1][:, t * P:T], [(lf_hi[:, t], span), (lf_lo[:, t], span)],
                                    t == 0, t == TT - 1)
                last.then_inc(cum_done, 1)

            pe.wait_ge(const_ready, 1)
            for n in range(4):
                memory_transposes(0, n)
            for c in range(4):
                memory_projection(0, c)
            memory_values(0)
            pe.wait_ge(par_landed, 32)
            transposes(Pos(T_PAR), [par_raw[:, :]])
            pe.wait_ge(ws_masked, 1)
            for n in range(3):
                transposes(Pos(T_WS + n), [ws_raw[:, h] for h in range(4 * n, 4 * n + 4)])
            pe.wait_ge(x_landed, 16)
            for k in range(KT):
                transposes(Pos(T_X + k), [x_nat[:, t, k * P:(k + 1) * P] for t in range(TT)])
            pe.wait_ge(x_ready, KT)
            with pe.Fori(0, PAIRS // 2) as i:
                for c in range(2):
                    project(Pos(B_AV + c, i, 2), Pos(G_AV + c, i, 2), x_hi, x_lo)
                for c in range(2):
                    g = Pos(G_AV + c, i, 2)
                    pe.wait_ge(proj_free[g.slot], g.half(2))
                    transposes(Pos(T_AV + c, i, 2), [v_tmp[:, g.slot, t * P:(t + 1) * P] for t in range(TT)])
            for c in range(MEMPAIRS):
                project(Pos(B_AQ + c), Pos(G_AQ + c), x_hi, x_lo)
            for c in range(MEMPAIRS):
                pe.wait_ge(proj_free[c], (G_AQ + c) // 2 + 1)
            for s in range(2):
                pair_step(Pos(STEP_A + s), Pos(B_AU + 3 * s), Pos(G_AU + 3 * s))
            spatial_gate()
            for c, n in ((0, 6), (1, 4), (0, 7), (1, 5), (1, 6), (1, 7)):
                out_start(0, c, n)
            out_projection(0)
            layer_sums(0, G_WO[0] + KT - 1)
            memory_projection(1, 0)
            layer_spread(0)
            memory_projection(1, 1)
            feed_forward(0)
            memory_projection(1, 2, (0, 4))
            layer_sums(1, G_DN[0][1] + KT - 1)
            memory_projection(1, 2, (4, KT))
            layer_spread(1)
            memory_projection(1, 3)
            memory_values(1)

            project_two(Pos(B_BQ), Pos(G_BQ), x_hi, x_lo, ready=lambda n: pe.wait_ge(x_ready, 2 * KT + n + 1))
            forget_gate()
            for c in range(MEMPAIRS):
                pe.wait_ge(proj_free[c], (G_BQ + c) // 2 + 1)
            turn_forget_gate()
            pair_step(Pos(STEP_B), Pos(B_FOX), Pos(G_FOX), values=Pos(0))
            cumulate()
            with pe.Fori(0, 2) as i:
                for j in range(2):
                    pair_step(Pos(STEP_FOX + j, i, 2), Pos(B_FOX + 3 * (j + 1), i, 6),
                              Pos(G_FOX + 3 * (j + 1), i, 6), values=Pos(j + 1, i, 2))
            pair_step(Pos(7), Pos(B_FOX + 15), Pos(G_FOX + 15), values=Pos(5))
            pair_step(Pos(8), extra={3: (0, 0), 5: (1, 0), 6: (0, 1), 8: (1, 1), 9: (0, 2)})
            pair_step(Pos(STEP_LAST), extra={0: (1, 2), 2: (0, 3), 4: (1, 3), 6: (0, 4), 8: (0, 5)})
            for c, n in ((0, 6), (0, 7), (1, 4), (1, 5), (1, 6), (1, 7)):
                out_start(1, c, n)
            out_projection(1)
            layer_sums(2, G_WO[1] + KT - 1)
            layer_spread(2)
            feed_forward(1)

        @block.scalar
        def _(act):
            def prepare(b):
                if b.trip is None and b.base >= B_DN[1][1] + 2 * KT:
                    return
                act.wait_ge(w_landed[b.slot], b.half(2) * 16)
                wait(act, w_used, b.at(-1))
                act.copy(w_hi[:, b.slot], w_raw[:, b.slot]).then_inc(w_hi_ready, 1)

            def turned_hi(t, target, source=None):
                act.wait_ge(tr_done, t.at(1))
                act.copy(target, tr[t.slot][:, :] if source is None else source).then_inc(tr_hi, 1)

            def projected(b, g, target, scale=1.0):
                act.wait_ge(w_used, b.at(1))
                act.activation(target, proj[g.slot][:, 0:target.shape[-1]], ACT.Copy, scale=scale).then_inc(qk_hi, 1)

            def plain(b, g, target, function=ACT.Copy):
                act.wait_ge(w_used, b.at(1))
                act.activation(target, proj[g.slot][:, 0:target.shape[-1]], function).then_inc(proj_free[g.slot], 1)

            def memory_hi(layer, n):
                turned_hi(Pos(T_MEM[layer] + n), mem_hi[layer][:, 2 * n:2 * n + 2],
                          tr[(T_MEM[layer] + n) % 2][:, :].rearrange("p (k m) -> p k m", k=2))

            def memory_projection(layer, c):
                b, g = Pos(B_MEM[layer][c]), Pos(G_MEM[layer][c])
                if c < 2:
                    projected(b, g, mk_hi[:, c, :])
                else:
                    plain(b, g, v_tmp[:, c - 2, 0:M])

            def memory_values(layer):
                turned_hi(Pos(T_MV[layer]), mv_hi[:, :, :], tr[T_MV[layer] % 2][:, :].rearrange("p (m c) -> p m c", m=MT))

            def exponentials(s, u):
                n = keys(s, u) * P
                act.wait_ge(max_done, s.at(u + 1, 8))
                act.activation(probs[:, u % 2, 0:n], sc[u % 2][:, 0:n], ACT.Exp, bias=neg_max[:, u:u + 1],
                               accum_out=row_sum[:, u:u + 1]).then_inc(exp_done, 1)

            def turned_probs(s, u):
                n, here, t = keys(s, u), slice(u % TT * P, (u % TT + 1) * P), tr_index(s, u)
                turned_hi(t, p_buffers(s)[0][:, u // TT, 0:n, here],
                          tr[t.slot][:, 0:n * P].rearrange("p (j t) -> p j t", j=n))

            def attended(s, head):
                rows = slice(head * HALF, (head + 1) * HALF)
                act.wait_ge(pv_done, s.at(head + 1, 2))
                act.copy(mix_hi[rows, bass.ds(step_tile(s), 1), :], pv[head][rows, :].rearrange("p (a t) -> p a t", a=1))\
                    .then_inc(mix_hi_ready, 1)

            def step_projection(s, b, g, c):
                if s.base < STEP_B:
                    plain(b, g, u_t[:, g.base - G_AU, :])
                elif c < 2:
                    j = (g.base - G_FOX) // 3 % 2
                    projected(b, g, (q_hi, k_hi)[c][:, j, :], SCALE if c == 0 else 1.0)
                else:
                    plain(b, g, v_tmp[:, g.slot, :])

            def pair_step(s, b=None, g=None, values=None, late=None):
                for u in range(8):
                    if b is not None and u in (0, 3, 6):
                        prepare(b.plus(u // 3 + 1))
                    if late is not None and u == 1:
                        prepare(late)
                    if u >= 2:
                        turned_probs(s, u - 2)
                    exponentials(s, u)
                    if b is not None and u in (2, 5):
                        step_projection(s, b.plus(u // 3), g.plus(u // 3), u // 3)
                attended(s, 0)
                turned_probs(s, 6)
                turned_probs(s, 7)
                if b is not None:
                    step_projection(s, b.plus(2), g.plus(2), 2)
                attended(s, 1)
                if values is not None:
                    act.wait_ge(vt_done, values.at(1))
                    act.copy(v_hi[:, values.slot], pv[0][:, :].rearrange("p (t c) -> p t c", t=TT)).then_inc(vt_hi, 1)

            def squares(n, j, g):
                if j.base < 2:
                    act.wait_ge(shifted, 2 * n + j.base + 1)
                else:
                    act.wait_ge(proj_free[g.slot], g.half(2))
                    wait(act, sq_added, j.at((KT - 1) * n - 1))
                act.activation(square[:, j.slot, :], x32_tile(j), ACT.Square).then_inc(sq_ready, 1)

            def shift_source(n, g):
                act.wait_ge(proj_free[g % 2], g // 2 + 1)
                act.copy(shift_in[:, :], x32[:, 0]).then_inc(shift_ready, 1)

            def root(n):
                act.wait_ge(ln_step, 5 * n + 3)
                act.activation(ln_sqrt[:, :], ln_var[:, :], ACT.Sqrt, bias=eps[:, 0:1]).then_inc(ln_root, 1)

            def finish(n, tiles):
                for k in tiles:
                    act.wait_ge(fin_moved, KT * n + k + 1)
                    act.activation(x32[:, k], x32[:, k], ACT.Identity, bias=par[:, 32 + KT * n + k:33 + KT * n + k],
                                   scale=par[:, KT * n + k:KT * n + k + 1]).then_inc(fin_ready, 1)
                    act.wait_ge(fin_ready, KT * n + k + 1)
                    act.copy(x_hi[:, k], x32[:, k]).then_inc(x_hi_ready, 1)

            def turned_result(j):
                act.wait_ge(tr_done, j.at(T_OUT + 1))
                act.copy(y_nat[:, :, bass.ds(j.at(0, P), P)], tr[j.slot][:, :].rearrange("p (t c) -> p t c", t=TT))\
                    .then_inc(tr_free, 1)

            def feed_forward(layer):
                for half in range(2):
                    def up(tile):
                        b, g = tile.plus(B_UP[layer][half]), tile.plus(G_UP[layer][half])
                        h = tile.plus((2 * layer + half) * FT)
                        if half or tile.trip is not None:
                            prepare(b.plus(1))
                        elif tile.base == 0:
                            prepare(b.plus(2))
                        wait(act, relu_sq, h.at(-1))
                        plain(b, g, relu[:, tile.slot, :], ACT.Relu)
                        act.wait_ge(proj_free[g.slot], g.half(2))
                        act.activation(h_hi[:, bass.ds(tile.at(), 1), :], relu[:, tile.slot:tile.slot + 1, :],
                                       ACT.Square).then_inc(h_hi_ready, 1)
                    up(Pos(0))
                    up(Pos(1))
                    with act.Fori(0, FT // 2 - 1) as i:
                        up(Pos(2, i, 2))
                        up(Pos(3, i, 2))
                    b, n = B_DN[layer][half], 2 * layer + 1
                    if not half:
                        with act.Fori(0, KT) as i:
                            for c in range(2):
                                prepare(Pos(b + c + 1, i, 2))
                        continue
                    if layer:
                        for c in range(2):
                            prepare(Pos(b + c + 1))
                        with act.Fori(0, KT // 2 - 1) as i:
                            for j in range(2):
                                for c in range(2):
                                    prepare(Pos(b + 3 + 2 * j + c, i, 4))
                                turned_result(Pos(j, i, 2))
                        prepare(Pos(b + 2 * KT - 1))
                        turned_result(Pos(KT - 2))
                        turned_result(Pos(KT - 1))
                        continue
                    for c in range(4):
                        prepare(Pos(b + c + 1))
                    g = G_DN[layer][half]
                    shift_source(n, g)
                    for j in range(2):
                        squares(n, Pos(j), Pos(g + j))
                    with act.Fori(0, 2) as i:
                        for j in range(2):
                            for c in range(2):
                                prepare(Pos(b + 4 + 2 * j + c + 1, i, 4))
                            squares(n, Pos(2 + j, i, 2), Pos(g + 2 + j, i, 2))
                    for j in range(6, KT):
                        for c in range(2):
                            prepare(Pos(b + 2 * j + c + 1))
                        squares(n, Pos(j), Pos(g + j))
                    if layer == 0:
                        prepare(Pos(B_MEM[1][3]))
                    root(n)
                    if layer == 0:
                        memory_projection(1, 2)
                        prepare(Pos(B_BQ))
                    finish(n, range(2))
                    if layer == 0:
                        memory_projection(1, 3)
                        prepare(Pos(B_BQ + 1))
                    finish(n, range(2, KT))

            def out_projection(layer):
                g = G_WO[layer]
                for j in range(KT):
                    if j:
                        prepare(Pos(B_WO[layer] + j + 1))
                    if j == 1:
                        shift_source(2 * layer, g)
                    if j == 2:
                        squares(2 * layer, Pos(0), Pos(g))
                        squares(2 * layer, Pos(1), Pos(g + 1))
                    if j > 1:
                        squares(2 * layer, Pos(j), Pos(g + j))
                    if layer == 0 and 2 <= j < 6:
                        memory_hi(1, j - 2)

            act.dma_start(mem_nat[:, :, :], mem[0].rearrange("(m p) d -> p m d", p=P)).then_inc(mem_landed, 16)
            act.dma_start(x_nat[:, :, :], x[0].rearrange("(t p) d -> p t d", p=P)).then_inc(x_landed, 16)
            act.dma_start(par_raw[0:32, :], ln_g.rearrange("l i (k p) -> (l i k) p", p=P)).then_inc(par_landed, 16)
            act.dma_start(par_raw[32:64, :], ln_b.rearrange("l i (k p) -> (l i k) p", p=P)).then_inc(par_landed, 16)
            act.dma_start(ws_raw[:, :, :], a_w_s[0].rearrange("h t s -> t h s")).then_inc(ws_landed, 16)
            act.dma_start(g_all[:, :], a_sgu_ln_g.broadcast_to([P, DMIX])).then_inc(sgu_landed, 16)
            act.dma_start(b_all[:, :], a_sgu_ln_b.broadcast_to([P, DMIX])).then_inc(sgu_landed, 16)
            for head in range(2):
                own = a_b_s.rearrange("a (j e) t -> a e j t", e=2)[:, head].broadcast_to([HALF, PAIRS, P])
                act.dma_start(bs_all[head * HALF:(head + 1) * HALF, :, :], own).then_inc(sgu_landed, 16)
            act.dma_start(wf_raw[:, :, :], kv_w[:, 2 * DMIX:].rearrange("(k p) n -> p k n", p=P)).then_inc(wf_landed, 16)
            act.dma_start(bf_row[:, :], kv_b_f.rearrange("(a n) -> a n", a=1).broadcast_to([P, HEADS])).then_inc(wf_landed, 16)

            act.wait_ge(const_ready, 3)
            act.copy(ident_r[:, :], ident[:, :])
            act.copy(causal_r[:, :], causal[:, :])
            act.copy(tri_r[:, :], tri_f[:, :]).then_inc(const_r, 1)
            prepare(Pos(0))
            for n in range(4):
                memory_hi(0, n)
            for c in range(4):
                prepare(Pos(c + 1))
                memory_projection(0, c)
            memory_values(0)
            for n in range(3):
                turned_hi(Pos(T_WS + n), ws_hi[:, 4 * n:4 * n + 4], tr[(T_WS + n) % 2][:, :].rearrange("p (h t) -> p h t", h=4))
            for k in range(KT):
                act.wait_ge(tr_free, T_X + k + 1)
                act.copy(x_hi[:, k], x32[:, k]).then_inc(x_hi_ready, 1)
            with act.Fori(0, PAIRS // 2) as i:
                for c in range(2):
                    b, g = Pos(B_AV + c, i, 2), Pos(G_AV + c, i, 2)
                    prepare(b.plus(1))
                    plain(b, g, v_tmp[:, g.slot, :], ACT.Gelu_apprx_tanh)
            for c in range(MEMPAIRS):
                prepare(Pos(B_AQ + c + 1))
                projected(Pos(B_AQ + c), Pos(G_AQ + c), qm_hi[:, c, :], SCALE)
            act.wait_ge(bn_step, 3 * TT)
            act.activation(sgu_root[:, :], sgu_mv[:, :, 1], ACT.Sqrt, bias=eps[:, 0:1]).then_inc(bn_root, 1)
            for s in range(2):
                pair_step(Pos(STEP_A + s), Pos(B_AU + 3 * s), Pos(G_AU + 3 * s))
            act.wait_ge(zg_ready, TT)
            for j in range(PAIRS + 1):
                if j == 0:
                    prepare(Pos(B_WO[0] + 1))
                if j < PAIRS:
                    wait(act, sgu_done, 2 * (j - 1))
                    act.copy(z_hi[:, j % 2], z_nat[:, :, j * P:(j + 1) * P]).then_inc(z_hi_ready, 1)
                    if j == 0:
                        for g in (G_WO[0] - 2, G_WO[0] - 1):
                            act.wait_ge(proj_free[g % 2], g // 2 + 1)
                    act.activation(u_t[:, j, :], u_t[:, j, :], ACT.Gelu_apprx_tanh).then_inc(u_ready, 1)
                for c in range(2):
                    if j:
                        act.wait_ge(sgu_gated, 2 * (j - 1) + c + 1)
                        act.copy(mix_hi[:, j - 1, c * 2 * P:(c + 1) * 2 * P], gated[:, c]).then_inc(sgu_hi, 1)
            act.wait_ge(sgu_ready, 2 * PAIRS)
            act.dma_start(mem2_nat[:, :, :], mem[0].rearrange("(m p) d -> p m d", p=P)).then_inc(mem_landed, 16)
            out_projection(0)
            prepare(Pos(27))
            root(0)
            memory_projection(1, 0)
            prepare(Pos(28))
            finish(0, range(2))
            memory_projection(1, 1)
            prepare(Pos(29))
            finish(0, range(2, KT))
            feed_forward(0)

            memory_values(1)
            for c in range(MEMPAIRS):
                if c:
                    prepare(Pos(B_BQ + c + 1))
                projected(Pos(B_BQ + c), Pos(G_BQ + c), qm_hi[:, c, :], SCALE)
            act.wait_ge(f_step, 2)
            act.activation(f_exp[:, :, :], f_abs[:, :, :], ACT.Exp).then_inc(f_act, 1)
            act.wait_ge(f_act, 1)
            act.activation(f_ln[:, :, :], f_exp[:, :, :], ACT.Ln, bias=1.0).then_inc(f_act, 1)
            act.wait_ge(f_step, 6)
            for r in range(0, P, 32):
                last = act.copy(lf_hi[:, :, r:r + HEADS], f_sp[:, :, :])
            last.then_inc(f_act, 1)
            pair_step(Pos(STEP_B), Pos(B_FOX), Pos(G_FOX), values=Pos(0))
            act.wait_ge(cum_done, 1)
            act.copy(cum[:, :], pv[1][:, :]).then_inc(f_act, 1)
            with act.Fori(0, 2) as i:
                for j in range(2):
                    pair_step(Pos(STEP_FOX + j, i, 2), Pos(B_FOX + 3 * (j + 1), i, 6),
                              Pos(G_FOX + 3 * (j + 1), i, 6), values=Pos(j + 1, i, 2))
            pair_step(Pos(7), Pos(B_FOX + 15), Pos(G_FOX + 15), values=Pos(5))
            pair_step(Pos(8), late=Pos(B_WO[1] + 1))
            pair_step(Pos(STEP_LAST))
            out_projection(1)
            root(2)
            prepare(Pos(B_UP[1][0] + 1))
            act.dma_start(g_out[:, :], ln_g[1, 1:2, :].broadcast_to([P, D])).then_inc(out_landed, 16)
            act.dma_start(b_out[:, :], ln_b[1, 1:2, :].broadcast_to([P, D])).then_inc(out_landed, 16)
            finish(2, range(KT))
            feed_forward(1)
            act.wait_ge(y_step, 1)
            act.activation(y_root[:, :], y_mv[:, :, 1], ACT.Sqrt, bias=eps[:, 0:1]).then_inc(y_rooted, 1)
            act.wait_ge(y_step, 3)
            for c in range(2):
                part = y_nat[:, TT - 1, c * D // 2:(c + 1) * D // 2]
                act.activation(part, part, ACT.Identity, bias=y_move[:, TT - 1:TT], scale=y_rstd[:, TT - 1:TT])\
                    .then_inc(y_scaled, 1)

        @block.vector
        def _(dve):
            def rest(target, whole, hi):
                return dve.tensor_tensor(target, whole, hi.bitcast(F32), ALU.subtract)

            def prepare(b):
                if b.trip is None and b.base >= B_DN[1][1] + 2 * KT:
                    return
                dve.wait_ge(w_hi_ready, b.at(1))
                rest(w_lo[:, b.slot], w_raw[:, b.slot], w_hi[:, b.slot]).then_inc(w_split, 1)

            def turned_lo(t, h, target, hi, source=None):
                dve.wait_ge(tr_hi, h.at(1))
                rest(target, tr[t.slot][:, :] if source is None else source, hi).then_inc(tr_free, 1)

            def projected(g, q, target, hi, scale=1.0):
                dve.wait_ge(qk_hi, q.at(1))
                source = proj[g.slot][:, 0:target.shape[-1]]
                if scale == 1.0:
                    rest(target, source, hi).then_inc(proj_free[g.slot], 1)
                else:
                    dve.scalar_tensor_tensor(out=target, in0=source, scalar=scale, in1=hi.bitcast(F32),
                                             op0=ALU.mult, op1=ALU.subtract).then_inc(proj_free[g.slot], 1)

            def memory_lo(layer, n):
                pair = slice(2 * n, 2 * n + 2)
                turned_lo(Pos(T_MEM[layer] + n), Pos(H_MEM[layer] + n), mem_lo[layer][:, pair], mem_hi[layer][:, pair],
                          tr[(T_MEM[layer] + n) % 2][:, :].rearrange("p (k m) -> p k m", k=2))

            def memory_keys(layer, c):
                projected(Pos(G_MEM[layer][c]), Pos(Q_MEM[layer] + c), mk_lo[:, c, :], mk_hi[:, c, :])

            def memory_values(layer):
                turned_lo(Pos(T_MV[layer]), Pos(H_MV[layer]), mv_lo[:, :, :], mv_hi[:, :, :],
                          tr[T_MV[layer] % 2][:, :].rearrange("p (m c) -> p m c", m=MT))

            def row_max(s, u):
                dve.wait_ge(sc_done, s.at(u + 1, 8))
                dve.tensor_reduce(neg_max[:, u:u + 1], sc[u % 2][:, 0:keys(s, u) * P], AX.X, ALU.max,
                                  negate=True).then_inc(max_done, 1)

            def normalize(s, u):
                own = probs[:, u % 2, 0:keys(s, u) * P]
                dve.wait_ge(exp_done, s.at(u + 1, 8))
                dve.reciprocal(inv_sum[:, u:u + 1], row_sum[:, u:u + 1]).then_inc(inv_done, 1)
                dve.wait_ge(inv_done, s.at(u + 1, 8))
                dve.tensor_scalar(own, own, inv_sum[:, u:u + 1], None, ALU.mult).then_inc(probs_ready, 1)

            def turned_probs(s, u):
                n, here, t = keys(s, u), slice(u % TT * P, (u % TT + 1) * P), tr_index(s, u)
                hi, lo = p_buffers(s)
                turned_lo(t, hi_index(s, u), lo[:, u // TT, 0:n, here], hi[:, u // TT, 0:n, here],
                          tr[t.slot][:, 0:n * P].rearrange("p (j t) -> p j t", j=n))

            def attended(s, head):
                rows = slice(head * HALF, (head + 1) * HALF)
                tile = bass.ds(step_tile(s), 1)
                dve.wait_ge(mix_hi_ready, s.at(head + 1, 2))
                rest(mix_lo[rows, tile, :], pv[head][rows, :].rearrange("p (a t) -> p a t", a=1),
                     mix_hi[rows, tile, :]).then_inc(mix_ready, 1)

            def gate_stats(n):
                if n == 0:
                    dve.wait_ge(tr_free, T_AV + PAIRS)
                for c in range(2):
                    dve.bn_stats(sgu_stats[:, n, c], z_nat[:, n, c * (DMIX // 2):(c + 1) * (DMIX // 2)]).then_inc(bn_step, 1)
                dve.wait_ge(bn_step, 3 * n + 2)
                dve.bn_aggr(sgu_mv[:, n], sgu_stats[:, n]).then_inc(bn_step, 1)

            def gate_norm(n):
                if n == 0:
                    dve.wait_ge(bn_root, 1)
                    dve.reciprocal(sgu_rstd[:, :], sgu_root[:, :]).then_inc(bn_step, 1)
                    dve.wait_ge(bn_step, 3 * TT + 1)
                dve.tensor_scalar(z_nat[:, n], z_nat[:, n], sgu_mv[:, n, 0:1], sgu_rstd[:, n:n + 1],
                                  ALU.subtract, ALU.mult).then_inc(zn_ready, 1)

            def step_projection(s, g, c, q):
                if s.base < STEP_B:
                    if s.base == STEP_A and c < 2:
                        gate_norm(2 * c)
                        gate_norm(2 * c + 1)
                elif c < 2:
                    j = (g.base - G_FOX) // 3 % 2
                    projected(g, q.plus(c), (q_lo, k_lo)[c][:, j, :], (q_hi, k_hi)[c][:, j, :], SCALE if c == 0 else 1.0)

            def cum_rows(pair):
                dve.wait_ge(f_step, 8)
                dve.tensor_scalar(cum_row[:, :], cum[:, :].bitcast(F32), head_rows[:, bass.ds(pair.at(), 1)],
                                  None, ALU.mult).then_inc(row_ready, 1)

            def pair_step(s, b=None, g=None, q=None, values=None, late=None):
                for u in range(8):
                    if b is not None and u in (0, 3, 6):
                        prepare(b.plus(u // 3 + 1))
                    if late is not None and u == 1:
                        prepare(late)
                    row_max(s, u)
                    if u >= 2:
                        turned_probs(s, u - 2)
                    normalize(s, u)
                    if b is not None and u in (2, 5):
                        step_projection(s, g.plus(u // 3), u // 3, q)
                attended(s, 0)
                turned_probs(s, 6)
                turned_probs(s, 7)
                if fox(s) and values is not None:
                    cum_rows(values)
                attended(s, 1)
                if values is not None:
                    dve.wait_ge(vt_hi, values.at(1))
                    rest(v_lo[:, values.slot], pv[0][:, :].rearrange("p (t c) -> p t c", t=TT),
                         v_hi[:, values.slot]).then_inc(vt_ready, 1)

            def residual(n, b, g, j, first=True, target=None):
                tile = x32_tile(j)
                dve.wait_ge(w_used, b.at(1))
                dve.scalar_tensor_tensor(out=tile if target is None else target, in0=tile, scalar=ALPHA if first else 1.0, in1=proj[g.slot][:, :],
                                         op0=ALU.mult, op1=ALU.add).then_inc(proj_free[g.slot], 1)

            def shift_tiles(n, g):
                for j in range(2):
                    dve.wait_ge(proj_free[j], g // 2 + 1)
                    dve.tensor_tensor(x32[:, j], x32[:, j], shift[:, :], ALU.subtract).then_inc(shifted, 1)

            def shifted_residual(n, b, g, j, first=True):
                tile = x32_tile(j)
                if first:
                    dve.scalar_tensor_tensor(out=tile, in0=tile, scalar=ALPHA, in1=shift[:, :],
                                             op0=ALU.mult, op1=ALU.subtract).then_inc(pre_shifted, 1)
                else:
                    dve.tensor_tensor(tile, tile, shift[:, :], ALU.subtract).then_inc(pre_shifted, 1)
                dve.wait_ge(pre_shifted, j.at((KT - 2) * n - 1))
                dve.wait_ge(w_used, b.at(1))
                dve.tensor_tensor(tile, tile, proj[g.slot][:, :], ALU.add).then_inc(proj_free[g.slot], 1)

            def take_shift(n):
                dve.wait_ge(shift_done, n + 1)
                dve.tensor_scalar(shift[:, :], sc[0][:, :], 1.0 / P, None, ALU.mult).then_inc(shift_out, 1)
                dve.wait_ge(shift_out, n + 1)

            def moments(n):
                dve.wait_ge(stat_done, 2 * n + 1)
                dve.tensor_scalar(ln_mean[:, :], sc[0][:, 0:TT], 1.0 / D, None, ALU.mult).then_inc(ln_step, 1)
                dve.wait_ge(ln_step, 5 * n + 1)
                dve.tensor_tensor(ln_var[:, :], ln_mean[:, :], ln_mean[:, :], ALU.mult).then_inc(ln_step, 1)
                dve.wait_ge(ln_step, 5 * n + 2)
                dve.wait_ge(stat_done, 2 * n + 2)
                dve.scalar_tensor_tensor(out=ln_var[:, :], in0=sc[1][:, 0:TT], scalar=1.0 / D, in1=ln_var[:, :],
                                         op0=ALU.mult, op1=ALU.subtract).then_inc(ln_step, 1)
                dve.wait_ge(ln_root, n + 1)
                dve.reciprocal(ln_rstd[:, :], ln_sqrt[:, :]).then_inc(ln_step, 1)
                dve.wait_ge(ln_step, 5 * n + 4)
                dve.tensor_tensor(ln_move[:, :], ln_mean[:, :], ln_rstd[:, :], ALU.mult).then_inc(ln_step, 1)
                square_of = ident[:, :].rearrange("p (a c) -> p a c", a=1).broadcast_to([P, TT, P])
                for q, column in enumerate((ln_rstd, ln_move)):
                    if q:
                        dve.wait_ge(ln_step, 5 * n + 5)
                    dve.tensor_tensor(spread[:, q], square_of,
                                      column[:, :].rearrange("p (t a) -> p t a", a=1).broadcast_to([P, TT, P]),
                                      ALU.mult).then_inc(spread_ready, 1)

            def finish(n, tiles):
                for k in tiles:
                    dve.wait_ge(spread_done, 2 * n + 1)
                    dve.tensor_tensor(x32[:, k], x32[:, k], sc[0][:, :], ALU.mult).then_inc(fin_scaled, 1)
                    dve.wait_ge(spread_done, 2 * n + 2)
                    dve.wait_ge(fin_scaled, KT * n + k + 1)
                    dve.tensor_tensor(x32[:, k], x32[:, k], sc[1][:, :], ALU.subtract).then_inc(fin_moved, 1)

            def result_stats(j):
                dve.wait_ge(tr_free, j.at(T_OUT + 1))
                for t in range(TT):
                    last = dve.bn_stats(y_stats[:, t, bass.ds(j.at(), 1), :].rearrange("p a s -> p (a s)"),
                                        y_nat[:, t, bass.ds(j.at(0, P), P)])
                last.then_inc(y_counted, 1)

            def feed_forward(layer):
                for half in range(2):
                    def up(tile):
                        b, g = tile.plus(B_UP[layer][half]), tile.plus(G_UP[layer][half])
                        h = tile.plus((2 * layer + half) * FT)
                        if half or tile.trip is not None:
                            prepare(b.plus(1))
                        elif tile.base == 0:
                            prepare(b.plus(2))
                        dve.wait_ge(proj_free[g.slot], g.half(2))
                        raw, here = h_raw[:, tile.slot:tile.slot + 1, :], bass.ds(tile.at(), 1)
                        wide = relu[:, tile.slot:tile.slot + 1, :]
                        dve.tensor_tensor(raw, wide, wide, ALU.mult).then_inc(relu_sq, 1)
                        dve.wait_ge(relu_sq, h.at(1))
                        dve.wait_ge(h_hi_ready, h.at(1))
                        rest(h_lo[:, here, :], raw, h_hi[:, here, :]).then_inc(h_ready, 1)
                    up(Pos(0))
                    up(Pos(1))
                    with dve.Fori(0, FT // 2 - 1) as i:
                        up(Pos(2, i, 2))
                        up(Pos(3, i, 2))
                    b, g, n = B_DN[layer][half], G_DN[layer][half], 2 * layer + 1
                    if not half:
                        with dve.Fori(0, KT // 2) as i:
                            for j in range(2):
                                for c in range(2):
                                    prepare(Pos(b + 2 * j + c + 1, i, 4))
                                residual(n, Pos(b + 2 * j + 1, i, 4), Pos(g + j, i, 2), Pos(j, i, 2))
                        continue
                    if layer:
                        for c in range(2):
                            prepare(Pos(b + c + 1))
                        residual(n, Pos(b + 1), Pos(g), Pos(0), False, y_in[:, 0, :])
                        with dve.Fori(0, KT // 2 - 1) as i:
                            for j in range(2):
                                for c in range(2):
                                    prepare(Pos(b + 3 + 2 * j + c, i, 4))
                                residual(n, Pos(b + 3 + 2 * j, i, 4), Pos(g + 1 + j, i, 2), Pos(1 + j, i, 2), False,
                                         y_in[:, 1 - j, :])
                                result_stats(Pos(j, i, 2))
                        prepare(Pos(b + 2 * KT - 1))
                        residual(n, Pos(b + 2 * KT - 1), Pos(g + KT - 1), Pos(KT - 1), False, y_in[:, 1, :])
                        result_stats(Pos(KT - 2))
                        result_stats(Pos(KT - 1))
                        continue
                    for j in range(2):
                        for c in range(2):
                            prepare(Pos(b + 2 * j + c + 1))
                        residual(n, Pos(b + 2 * j + 1), Pos(g + j), Pos(j), False)
                    take_shift(n)
                    shift_tiles(n, g)
                    with dve.Fori(0, KT // 2 - 2) as i:
                        for j in range(2, 4):
                            for c in range(2):
                                prepare(Pos(b + 2 * j + c + 1, i, 4))
                            shifted_residual(n, Pos(b + 2 * j + 1, i, 4), Pos(g + j, i, 2), Pos(j, i, 2), False)
                    for j in range(6, KT):
                        for c in range(2):
                            prepare(Pos(b + 2 * j + c + 1))
                        shifted_residual(n, Pos(b + 2 * j + 1), Pos(g + j), Pos(j), False)

            def out_projection(layer):
                b, g, n = B_WO[layer], G_WO[layer], 2 * layer
                for j in range(KT):
                    if j:
                        prepare(Pos(b + j + 1))
                    if j == 2:
                        take_shift(n)
                        shift_tiles(n, g)
                    if j < 2:
                        residual(n, Pos(b + j), Pos(g + j), Pos(j))
                    else:
                        shifted_residual(n, Pos(b + j), Pos(g + j), Pos(j))
                    if layer == 0 and 2 <= j < 6:
                        memory_lo(1, j - 2)

            dve.memset(ones_f[:, :], 1.0).then_inc(const_r, 1)
            dve.memset(ones_r[:, :].bitcast(F32), 1.0).then_inc(const_r, 1)
            prepare(Pos(0))
            for n in range(4):
                memory_lo(0, n)
            for c in range(4):
                prepare(Pos(c + 1))
                if c < 2:
                    memory_keys(0, c)
            memory_values(0)
            dve.wait_ge(tr_done, T_PAR + 1)
            dve.tensor_copy(par[:, :], tr[T_PAR % 2][:, 0:64]).then_inc(tr_free, 1)
            for n in range(3):
                four = slice(4 * n, 4 * n + 4)
                turned_lo(Pos(T_WS + n), Pos(H_WS + n), ws_lo[:, four], ws_hi[:, four],
                          tr[(T_WS + n) % 2][:, :].rearrange("p (h t) -> p h t", h=4))
            for k in range(KT + 1):
                if k < KT:
                    dve.wait_ge(tr_done, T_X + k + 1)
                    dve.tensor_copy(x32[:, k], tr[(T_X + k) % 2][:, :]).then_inc(tr_free, 1)
                if k:
                    dve.wait_ge(x_hi_ready, k)
                    rest(x_lo[:, k - 1], x32[:, k - 1], x_hi[:, k - 1]).then_inc(x_ready, 1)
            with dve.Fori(0, PAIRS // 2) as i:
                for c in range(2):
                    prepare(Pos(B_AV + c + 1, i, 2))
                for c in range(2):
                    t = Pos(T_AV + c, i, 2)
                    dve.wait_ge(tr_done, t.at(1))
                    dve.tensor_copy(z_nat[:, :, bass.ds(i * (2 * P) + c * P, P)],
                                    tr[t.slot][:, :].rearrange("p (t c) -> p t c", t=TT)).then_inc(tr_free, 1)
            for c in range(MEMPAIRS):
                prepare(Pos(B_AQ + c + 1))
                projected(Pos(G_AQ + c), Pos(Q_AQ + c), qm_lo[:, c, :], qm_hi[:, c, :], SCALE)
                gate_stats(2 * c)
                gate_stats(2 * c + 1)
            for s in range(2):
                pair_step(Pos(STEP_A + s), Pos(B_AU + 3 * s), Pos(G_AU + 3 * s))
            dve.wait_ge(sgu_landed, 64)
            for j in range(PAIRS + 1):
                if j == 0:
                    prepare(Pos(B_WO[0] + 1))
                if j < PAIRS:
                    dve.wait_ge(z_hi_ready, j + 1)
                    rest(z_lo[:, j % 2], z_nat[:, :, j * P:(j + 1) * P], z_hi[:, j % 2]).then_inc(z_ready, 1)
                for c in range(2):
                    if j:
                        cols = slice(c * 2 * P, (c + 1) * 2 * P)
                        dve.wait_ge(sgu_hi, 2 * (j - 1) + c + 1)
                        rest(mix_lo[:, j - 1, cols], gated[:, c], mix_hi[:, j - 1, cols]).then_inc(sgu_ready, 1)
                for c in range(2):
                    if j == PAIRS:
                        break
                    dve.wait_ge(sgu_done, 2 * j + c + 1)
                    wait(dve, sgu_ready, 2 * (j - 1) + c + 1)
                    mixed = sc[c][:, :].rearrange("p (n h t) -> p n h t", n=2, h=2)
                    for head in range(2):
                        rows = slice(head * HALF, (head + 1) * HALF)
                        last = dve.tensor_tensor(gated[rows, c].rearrange("p (n t) -> p n t", n=2), mixed[rows, :, head],
                                                 bs_all[rows, j:j + 1, :].broadcast_to([HALF, 2, P]), ALU.add)
                    last.then_inc(sgu_added, 1)
            out_projection(0)
            prepare(Pos(27))
            moments(0)
            memory_keys(1, 0)
            prepare(Pos(28))
            finish(0, range(2))
            memory_keys(1, 1)
            prepare(Pos(29))
            finish(0, range(2, KT))
            feed_forward(0)
            prepare(Pos(B_MEM[1][3]))
            moments(1)
            prepare(Pos(B_BQ))
            finish(1, range(2))
            prepare(Pos(B_BQ + 1))
            finish(1, range(2, KT))

            memory_values(1)
            for c in range(MEMPAIRS):
                if c:
                    prepare(Pos(B_BQ + c + 1))
                projected(Pos(G_BQ + c), Pos(Q_BQ + c), qm_lo[:, c, :], qm_hi[:, c, :], SCALE)
            dve.wait_ge(f_done, 1)
            dve.tensor_copy(f_turned[0:HEADS, :], pv[1][0:HEADS, :]).then_inc(f_out, 1)
            dve.wait_ge(f_done, 2)
            dve.tensor_tensor(f_log[:, :, :], pv[1][:, 0:TT * HEADS].rearrange("p (t h) -> p t h", t=TT),
                              bf_row[:, :].rearrange("p (a h) -> p a h", a=1).broadcast_to([P, TT, HEADS]), ALU.add).then_inc(f_step, 1)
            dve.wait_ge(f_step, 1)
            dve.scalar_tensor_tensor(out=f_abs[:, :, :], in0=f_log[:, :, :], scalar=-1.0, in1=f_log[:, :, :],
                                     op0=ALU.mult, op1=ALU.min).then_inc(f_step, 1)
            dve.tensor_scalar(f_neg[:, :, :], f_log[:, :, :], -1.0, 0.0, ALU.mult, ALU.max).then_inc(f_step, 1)
            dve.memset(lf_hi[:, :, :].bitcast(F32), 0.0).then_inc(f_step, 1)
            dve.memset(lf_lo[:, :, :].bitcast(F32), 0.0).then_inc(f_step, 1)
            dve.wait_ge(f_step, 3)
            dve.wait_ge(f_act, 2)
            dve.tensor_tensor(f_sp[:, :, :], f_ln[:, :, :], f_neg[:, :, :], ALU.add).then_inc(f_step, 1)
            dve.wait_ge(f_step, 6)
            dve.wait_ge(f_act, 3)
            for r in range(0, P, 32):
                last = rest(lf_lo[:, :, r:r + HEADS], f_sp[:, :, :], lf_hi[:, :, r:r + HEADS])
            last.then_inc(f_step, 1)
            pair_step(Pos(STEP_B), Pos(B_FOX), Pos(G_FOX), Pos(Q_FOX), values=Pos(0))
            dve.wait_ge(f_act, 4)
            for r in (32, 96):
                last = rest(cum[r:r + 32, :], pv[1][r:r + 32, :], cum[r:r + 32, :])
            last.then_inc(f_step, 1)
            cum_rows(Pos(0))
            with dve.Fori(0, 2) as i:
                for j in range(2):
                    pair_step(Pos(STEP_FOX + j, i, 2), Pos(B_FOX + 3 * (j + 1), i, 6), Pos(G_FOX + 3 * (j + 1), i, 6),
                              Pos(Q_FOX + 2 * (j + 1), i, 4), values=Pos(j + 1, i, 2))
            pair_step(Pos(7), Pos(B_FOX + 15), Pos(G_FOX + 15), Pos(Q_FOX + 10), values=Pos(5))
            pair_step(Pos(8), late=Pos(B_WO[1] + 1))
            pair_step(Pos(STEP_LAST))
            out_projection(1)
            moments(2)
            prepare(Pos(B_UP[1][0] + 1))
            finish(2, range(KT))
            feed_forward(1)
            dve.wait_ge(y_counted, KT)
            for t in range(TT):
                last = dve.bn_aggr(y_mv[:, t], y_stats[:, t])
            last.then_inc(y_step, 1)
            dve.wait_ge(y_step, 1)
            dve.wait_ge(out_landed, 32)

            def centre(t, c):
                part = slice(c * D // 2, (c + 1) * D // 2)
                dve.scalar_tensor_tensor(out=y_nat[:, t, part], in0=y_nat[:, t, part], scalar=y_mv[:, t, 0:1],
                                         in1=g_out[:, part], op0=ALU.subtract, op1=ALU.mult).then_inc(y_centred, 1)
            centre(0, 0)
            dve.wait_ge(y_rooted, 1)
            dve.reciprocal(y_rstd[:, :], y_root[:, :]).then_inc(y_step, 1)
            dve.wait_ge(y_step, 2)
            dve.scalar_tensor_tensor(out=y_move[:, :], in0=y_mv[:, :, 0], scalar=-1.0, in1=y_rstd[:, :],
                                     op0=ALU.mult, op1=ALU.mult).then_inc(y_step, 1)
            parts = [(t, c) for t in range(TT - 1) for c in range(2)]
            for n, (t, c) in enumerate(parts):
                if n + 1 < len(parts):
                    centre(*parts[n + 1])
                part = slice(c * D // 2, (c + 1) * D // 2)
                dve.wait_ge(y_centred, n + 1)
                dve.scalar_tensor_tensor(out=y_nat[:, t, part], in0=y_nat[:, t, part], scalar=y_rstd[:, t:t + 1],
                                         in1=b_out[:, part], op0=ALU.mult, op1=ALU.add).then_inc(y_done, 1)

        @block.gpsimd
        def _(pool):
            steps = [0]

            def behind(instruction):
                steps[0] += 1
                instruction.then_inc(pool_step, 1)
                pool.wait_ge(pool_step, steps[0])

            pool.memset(eps[:, :], LN_EPS)
            behind(pool.memset(ident[:, :], 0.0))
            pool.affine_select(out=ident[:, :], in_=ident[:, :], compare_op=ALU.not_equal, fill=1.0, base=0,
                               pattern=[[-1, P]], channel_multiplier=1).then_inc(const_ready, 1)
            behind(pool.memset(causal[:, :], 0.0))
            pool.affine_select(out=causal[:, :], in_=causal[:, :], compare_op=ALU.is_ge, fill=MASKED, base=0,
                               pattern=[[-1, P]], channel_multiplier=1).then_inc(const_ready, 1)
            behind(pool.memset(tri_f[:, :], 1.0))
            pool.affine_select(out=tri_f[:, :], in_=tri_f[:, :], compare_op=ALU.is_ge, fill=0.0, base=0,
                               pattern=[[1, T]], channel_multiplier=-1).then_inc(const_ready, 1)
            pool.wait_ge(ws_landed, 16)
            pool.affine_select(out=ws_raw[:, :, :], in_=ws_raw[:, :, :], compare_op=ALU.is_ge, fill=0.0, base=0,
                               pattern=[[0, HEADS], [-1, P]], channel_multiplier=1).then_inc(ws_masked, 1)
            behind(pool.memset(head_rows[:, :], 0.0))
            for n, row in enumerate((0, 32, 65, 97)):
                last = pool.affine_select(out=head_rows[:, :], in_=head_rows[:, :], compare_op=ALU.not_equal, fill=1.0,
                                          base=-row, pattern=[[-2, PAIRS]], channel_multiplier=1)
                if n < 3:
                    behind(last)
            last.then_inc(const_ready, 1)
            pool.wait_ge(wf_landed, 32)
            pool.tensor_copy(wf_hi[:, :, :], wf_raw[:, :, :]).then_inc(wf_hi_ready, 1)
            pool.wait_ge(wf_hi_ready, 1)
            pool.tensor_tensor(wf_lo[:, :, :], wf_raw[:, :, :], wf_hi[:, :, :].bitcast(F32), ALU.subtract).then_inc(wf_ready, 1)

            pool.wait_ge(sgu_landed, 64)
            for n in range(TT):
                pool.wait_ge(zn_ready, n + 1)
                pool.tensor_tensor(z_nat[:, n], z_nat[:, n], g_all[:, :], ALU.mult).then_inc(zg_step, 1)
                pool.wait_ge(zg_step, n + 1)
                pool.tensor_tensor(z_nat[:, n], z_nat[:, n], b_all[:, :], ALU.add).then_inc(zg_ready, 1)
            for j in range(PAIRS):
                for c in range(2):
                    pool.wait_ge(sgu_added, 2 * j + c + 1)
                    pool.wait_ge(u_ready, j + 1)
                    pool.tensor_tensor(gated[:, c], gated[:, c], u_t[:, j, c * 2 * P:(c + 1) * 2 * P], ALU.mult)\
                        .then_inc(sgu_gated, 1)

            def add_tile(n, j, g, first=False):
                own = (KT - 1) * n
                if j.base < 2 and j.trip is None:
                    pool.wait_ge(shifted, 2 * n + j.base + 1)
                else:
                    pool.wait_ge(proj_free[g.slot], g.half(2))
                for source, added, sums in ((x32_tile(j), sum_added, total), (square[:, j.slot, :], sq_added, total_sq)):
                    if sums is total_sq:
                        pool.wait_ge(sq_ready, j.at(KT * n + 1))
                    if first:
                        pool.tensor_copy(sums[:, :], source).then_inc(added, 1)
                    else:
                        wait(pool, added, j.at(own))
                        pool.tensor_tensor(sums[:, :], sums[:, :], source, ALU.add).then_inc(added, 1)

            def layer_norm(n):
                g = G_DN[n // 2][1] if n % 2 else G_WO[n // 2]
                add_tile(n, Pos(0), Pos(g), True)
                add_tile(n, Pos(1), Pos(g + 1))
                with pool.Fori(0, 2) as i:
                    for j in range(2, 4):
                        add_tile(n, Pos(j, i, 2), Pos(g + j, i, 2))
                add_tile(n, Pos(6), Pos(g + 6))
                for k in range(KT):
                    pool.wait_ge(x_hi_ready, KT * (n + 1) + k + 1)
                    pool.tensor_tensor(x_lo[:, k], x32[:, k], x_hi[:, k].bitcast(F32), ALU.subtract).then_inc(x_ready, 1)

            for n in range(3):
                layer_norm(n)
            pool.wait_ge(out_landed, 32)
            for c in range(2):
                part = slice(c * D // 2, (c + 1) * D // 2)
                own = y_nat[:, TT - 1, part]
                pool.wait_ge(y_scaled, c + 1)
                pool.tensor_tensor(own, own, g_out[:, part], ALU.mult).then_inc(y_gained, 1)
                pool.wait_ge(y_gained, c + 1)
                pool.tensor_tensor(own, own, b_out[:, part], ALU.add).then_inc(y_last, 1)


_INS = ["x", "mem", "a_w_in", "a_sgu_ln_g", "a_sgu_ln_b", "a_w_s", "a_b_s", "kv_w", "kv_b_f", "b_w_q",
        "mem_w_kv", "w_o", "ln_g", "ln_b", "w_up", "w_down"]


def kernel(**inputs):
    import numpy as np
    import concourse.bacc as bacc
    from concourse.bass_utils import run_bass_kernel_spmd

    nc = bacc.Bacc("TRN2", target_bir_lowering=False, num_devices=1)
    arrays, args = {}, []
    for name in _INS:
        a = np.ascontiguousarray(inputs[name])
        arrays[f"in_{name}"] = a
        args.append(nc.dram_tensor(f"in_{name}", a.shape, mybir.dt.from_np(a.dtype), kind="ExternalInput").ap())
    out = nc.dram_tensor("out_y", inputs["x"].shape, F32, kind="ExternalOutput").ap()
    trunk_kernel(nc, *args, out)
    result = run_bass_kernel_spmd(nc, [arrays], core_ids=[0])
    return result.results[0]["out_y"]
```

```python
from contextlib import ExitStack

import concourse.bass as bass
from concourse import mybir
from concourse.alu_op_type import AluOpType as ALU

ACT = mybir.ActivationFunctionType
AX = mybir.AxisListType
F32 = mybir.dt.float32
F32R = mybir.dt.float32r

P = 128
HALF = P // 2
MASKED = -1.0e37
LN_EPS = 1e-5


class Pos:

    def __init__(self, base, trip=None, step=0):
        self.base, self.trip, self.step = base, trip, step

    def at(self, off=0, mul=1):
        n = self.base * mul + off
        return n if self.trip is None else self.trip * (self.step * mul) + n

    def half(self, off=0):
        n = (self.base + off) // 2
        return n if self.trip is None else self.trip * (self.step // 2) + n

    def plus(self, off):
        return Pos(self.base + off, self.trip, self.step)

    def times(self, mul, off=0):
        return Pos(self.base * mul + off, self.trip, self.step * mul)

    @property
    def slot(self):
        return self.base % 2


def wait(engine, semaphore, value):
    if not (isinstance(value, int) and value <= 0):
        engine.wait_ge(semaphore, value)


def trunk_kernel(nc, x, mem, a_w_in, a_sgu_ln_g, a_sgu_ln_b, a_w_s, a_b_s, kv_w, kv_b_f, b_w_q,
                 mem_w_kv, w_o, ln_g, ln_b, w_up, w_down, out):
    _, T, D = x.shape
    M = mem.shape[1]
    KT = D // P
    TT = T // P
    MT = M // P
    HEADS = a_w_s.shape[1]
    PAIRS = HEADS // 2
    DMIX = HEADS * HALF
    MEMPAIRS = (D - DMIX) // P
    FF = w_up.shape[2]
    FT = FF // P // 2
    SCALE = float(HALF) ** -0.5
    ALPHA = float(2 * w_up.shape[0]) ** 0.25
    assert (T, D, M, HEADS, FF) == (512, 1024, 256, 12, 4096) and a_w_s.shape[2] == P

    B_MEM = [[0, 1, 2, 3], [26, 27, 92, 93]]
    G_MEM = [[0, 1, 2, 3], [26, 27, 76, 77]]
    B_AV = G_AV = 4
    B_AQ = G_AQ = 10
    B_AU = G_AU = 12
    B_WO, G_WO = [18, 114], [18, 98]
    B_UP = [[28, 60], [122, 154]]
    G_UP = [[28, 52], [106, 130]]
    B_DN = [[44, 76], [138, 170]]
    G_DN = [[44, 68], [122, 146]]
    B_BQ, G_BQ = 94, 78
    B_FOX, G_FOX = 96, 80

    STEP_A, STEP_B, STEP_FOX, STEP_LAST = 0, 2, 3, 9
    T_MEM, T_X, T_MV, T_AV, T_PAR, T_WS = [0, 39], 4, [12, 43], 13, 19, 20
    T_STEP = [23, 28]
    T_OUT = 108
    H_MEM, H_MV, H_WS = [0, 24], [4, 28], 5
    H_STEP = [8, 13]
    Q_MEM, Q_AQ, Q_BQ, Q_FOX = [0, 4], 2, 6, 8

    ctx = ExitStack()
    with ctx:
        def psum(name):
            return ctx.enter_context(nc.psum_tensor(name, [P, 512], F32))

        def sem(name):
            return ctx.enter_context(nc.semaphore(name))

        base = [(nc.sbuf_base + 63) // 64 * 64]

        def put(name, shape, dtype, offset=None):
            size = 4
            for n in shape[1:]:
                size *= n
            if offset is None:
                offset = base[0]
                base[0] += (size + 63) // 64 * 64
            assert offset + size <= nc.sbuf_usable_end, (name, offset + size)
            return nc.alloc_sbuf_tensor_at(name, shape, dtype, offset=offset)

        K1 = 1024
        X0 = base[0]
        x_hi = put("x_hi", [P, KT, T], F32R)
        x_lo = put("x_lo", [P, KT, T], F32R)
        w_hi = put("w_hi", [P, 2, KT, P], F32R)
        w_lo = put("w_lo", [P, 2, KT, P], F32R)
        x32 = put("x32", [P, KT, T], F32)
        w_raw = put("w_raw", [P, 2, KT, P], F32)
        mk_hi = put("mk_hi", [P, MEMPAIRS, M], F32R)
        mk_lo = put("mk_lo", [P, MEMPAIRS, M], F32R)
        mv_hi = put("mv_hi", [P, MT, MEMPAIRS * P], F32R)
        mv_lo = put("mv_lo", [P, MT, MEMPAIRS * P], F32R)
        ident = put("ident", [P, P], F32)
        ident_r = put("ident_r", [P, P], F32R)
        ones_r = put("ones_r", [P, P], F32R)
        ones_f = put("ones_f", [P, P], F32)
        causal = put("causal", [P, P], F32)
        causal_r = put("causal_r", [P, P], F32R)
        tri_r = put("tri_r", [P, T], F32R)
        head_rows = put("head_rows", [P, PAIRS], F32)
        eps = put("eps", [P, 1], F32)
        par_raw = put("par_raw", [64, P], F32)
        par = put("par", [P, 64], F32)
        neg_max = put("neg_max", [P, 8], F32)
        row_sum = put("row_sum", [P, 8], F32)
        inv_sum = put("inv_sum", [P, 8], F32)
        sgu_stats = put("sgu_stats", [P, TT, 2, 6], F32)
        sgu_mv = put("sgu_mv", [P, TT, 2], F32)
        sgu_root = put("sgu_root", [P, TT], F32)
        sgu_rstd = put("sgu_rstd", [P, TT], F32)
        wf_raw = put("wf_raw", [P, KT, HEADS], F32)
        wf_hi = put("wf_hi", [P, KT, HEADS], F32R)
        wf_lo = put("wf_lo", [P, KT, HEADS], F32R)
        bf_row = put("bf_row", [P, HEADS], F32)
        v_tmp = put("v_tmp", [P, 2, T], F32)
        probs = put("probs", [P, 2, T], F32)
        top = base[0]

        mix_hi = put("mix_hi", [P, KT, T], F32R, top)
        mix_lo = put("mix_lo", [P, KT, T], F32R, top + 16 * K1)
        qm_hi = put("qm_hi", [P, MEMPAIRS, T], F32R, top + 32 * K1)
        qm_lo = put("qm_lo", [P, MEMPAIRS, T], F32R, top + 36 * K1)
        A0 = top + 40 * K1
        u_t = put("u_t", [P, PAIRS, T], F32, A0)
        z_nat = put("z_nat", [P, TT, DMIX], F32, A0 + 12 * K1)
        pa_hi = put("pa_hi", [P, 2, MT, T], F32R, A0 + 24 * K1)
        pa_lo = put("pa_lo", [P, 2, MT, T], F32R, A0 + 32 * K1)
        z_hi = put("z_hi", [P, 2, TT, P], F32R, A0 + 40 * K1)
        z_lo = put("z_lo", [P, 2, TT, P], F32R, A0 + 44 * K1)
        gate_even = put("gate_even", [P, 2, 2 * P], F32, A0 + 48 * K1)
        ws_hi = put("ws_hi", [P, HEADS, P], F32R, A0 + 50 * K1)
        ws_lo = put("ws_lo", [P, HEADS, P], F32R, A0 + 56 * K1)
        bs_all = put("bs_all", [P, PAIRS, P], F32, A0 + 62 * K1)
        g_all = put("g_all", [P, DMIX], F32, A0 + 65 * K1)
        b_all = put("b_all", [P, DMIX], F32, A0 + 68 * K1)
        memt_hi = put("memt_hi", [P, KT, M], F32R, top)
        memt_lo = put("memt_lo", [P, KT, M], F32R, top + 8 * K1)
        mem_nat = put("mem_nat", [P, MT, D], F32, top + 16 * K1)
        ws_raw = put("ws_raw", [P, HEADS, P], F32, top + 24 * K1)
        x_nat = put("x_nat", [P, TT, D], F32, top + 30 * K1)
        tri_f = put("tri_f", [P, T], F32, A0 + 12 * K1)
        q_hi = put("q_hi", [P, 2, T], F32R, A0)
        q_lo = put("q_lo", [P, 2, T], F32R, A0 + 4 * K1)
        k_hi = put("k_hi", [P, 2, T], F32R, A0 + 8 * K1)
        k_lo = put("k_lo", [P, 2, T], F32R, A0 + 12 * K1)
        v_hi = put("v_hi", [P, 2, TT, P], F32R, A0 + 16 * K1)
        v_lo = put("v_lo", [P, 2, TT, P], F32R, A0 + 20 * K1)
        pb_hi = put("pb_hi", [P, 2, TT, T], F32R, A0 + 24 * K1)
        pb_lo = put("pb_lo", [P, 2, TT, T], F32R, A0 + 40 * K1)
        cum = put("cum", [P, T], F32R, A0 + 56 * K1)
        cum_row = put("cum_row", [P, T], F32R, A0 + 58 * K1)
        f_turned = put("f_turned", [P, T], F32, A0 + 58 * K1)
        lf_hi = put("lf_hi", [P, TT, P], F32R, A0 + 62 * K1)
        lf_lo = put("lf_lo", [P, TT, P], F32R, A0 + 64 * K1)
        f_log = put("f_log", [P, TT, HEADS], F32, A0 + 66 * K1)
        f_abs = put("f_abs", [P, TT, HEADS], F32, A0 + 66 * K1 + 256)
        f_neg = put("f_neg", [P, TT, HEADS], F32, A0 + 66 * K1 + 512)
        f_exp = put("f_exp", [P, TT, HEADS], F32, A0 + 66 * K1 + 768)
        f_ln = put("f_ln", [P, TT, HEADS], F32, A0 + 67 * K1)
        f_sp = put("f_sp", [P, TT, HEADS], F32, A0 + 67 * K1 + 256)
        h_hi = put("h_hi", [P, FT, T], F32R, top)
        h_lo = put("h_lo", [P, FT, T], F32R, top + 32 * K1)
        L0 = top + 64 * K1
        shift = put("shift", [P, T], F32, L0)
        shift_in = put("shift_in", [P, T], F32R, L0 + 2 * K1)
        total = put("total", [P, T], F32, L0 + 4 * K1)
        total_sq = put("total_sq", [P, T], F32, L0 + 6 * K1)
        square = put("square", [P, 2, T], F32, L0 + 8 * K1)
        ln_mean = put("ln_mean", [P, TT], F32, L0 + 16 * K1)
        ln_var = put("ln_var", [P, TT], F32, L0 + 16 * K1 + 64)
        ln_sqrt = put("ln_sqrt", [P, TT], F32, L0 + 16 * K1 + 128)
        ln_rstd = put("ln_rstd", [P, TT], F32, L0 + 16 * K1 + 192)
        ln_move = put("ln_move", [P, TT], F32, L0 + 16 * K1 + 256)
        relu = put("relu", [P, 2, T], F32, L0 + 24 * K1)
        h_raw = put("h_raw", [P, 2, T], F32, L0 + 28 * K1)
        mem2_nat = put("mem2_nat", [P, MT, D], F32, L0 + 24 * K1)
        memt2_hi = put("memt2_hi", [P, KT, M], F32R, L0 + 32 * K1)
        memt2_lo = put("memt2_lo", [P, KT, M], F32R, L0 + 40 * K1)
        y_nat = put("y_nat", [P, TT, D], F32, X0)
        g_out = put("g_out", [P, D], F32, L0 + 32 * K1)
        b_out = put("b_out", [P, D], F32, L0 + 36 * K1)
        y_stats = put("y_stats", [P, TT, KT, 6], F32, L0 + 40 * K1)
        y_in = put("y_in", [P, 2, T], F32, L0 + 44 * K1)
        y_mv = put("y_mv", [P, TT, 2], F32, L0 + 41 * K1)
        y_root = put("y_root", [P, TT], F32, L0 + 41 * K1 + 64)
        y_rstd = put("y_rstd", [P, TT], F32, L0 + 41 * K1 + 128)
        y_move = put("y_move", [P, TT], F32, L0 + 41 * K1 + 192)
        mem_in = [mem_nat, mem2_nat]
        mem_hi, mem_lo = [memt_hi, memt2_hi], [memt_lo, memt2_lo]

        proj = [psum("proj0"), psum("proj1")]
        sc = [psum("sc0"), psum("sc1")]
        tr = [psum("tr0"), psum("tr1")]
        pv = [psum("pv0"), psum("pv1")]

        w_landed = [sem("w_landed0"), sem("w_landed1")]
        w_hi_ready, w_split = sem("w_hi_ready"), sem("w_split")
        w_used = sem("w_used")
        proj_free = [sem("proj_free0"), sem("proj_free1")]
        qk_hi = sem("qk_hi")
        tr_done, tr_hi, tr_free = sem("tr_done"), sem("tr_hi"), sem("tr_free")
        x_hi_ready, x_ready = sem("x_hi_ready"), sem("x_ready")
        mem_landed, x_landed = ([sem(f"{name}_landed{c}") for c in range(2)] for name in ("mem", "x"))
        mem2_landed, ws_landed = sem("mem2_landed"), sem("ws_landed")
        par_landed, sgu_landed, wf_landed = sem("par_landed"), sem("sgu_landed"), sem("wf_landed")
        const_ready, const_r, ws_masked = sem("const_ready"), sem("const_r"), sem("ws_masked")
        pool_step = sem("pool_step")
        bn_step, zn_ready, zg_ready = sem("bn_step"), sem("zn_ready"), sem("zg_ready")
        zg_step = sem("zg_step")
        z_hi_ready, z_ready = sem("z_hi_ready"), sem("z_ready")
        sgu_done, sgu_added, sgu_gated = sem("sgu_done"), sem("sgu_added"), sem("sgu_gated")
        sgu_hi, sgu_ready = sem("sgu_hi"), sem("sgu_ready")
        sc_done, max_done, exp_done = sem("sc_done"), sem("max_done"), sem("exp_done")
        inv_done, probs_ready = sem("inv_done"), sem("probs_ready")
        pv_done, mix_hi_ready, mix_ready = sem("pv_done"), sem("mix_hi_ready"), sem("mix_ready")
        vt_done, vt_hi, vt_ready = sem("vt_done"), sem("vt_hi"), sem("vt_ready")
        row_ready = sem("row_ready")
        wf_hi_ready, wf_ready = sem("wf_hi_ready"), sem("wf_ready")
        f_done, f_out, lf_zeroed, f_step, f_act, cum_done = sem("f_done"), sem("f_out"), sem("lf_zeroed"), sem("f_step"), sem("f_act"), sem("cum_done")
        relu_sq, h_hi_ready, h_ready = sem("relu_sq"), sem("h_hi_ready"), sem("h_ready")
        shift_ready, shift_done, shifted = sem("shift_ready"), sem("shift_done"), sem("shifted")
        shift_out, pre_shifted = sem("shift_out"), sem("pre_shifted")
        sq_ready, sum_added, sq_added = sem("sq_ready"), sem("sum_added"), sem("sq_added")
        stat_done, spread_done = sem("stat_done"), sem("spread_done")
        ln_step, ln_root = sem("ln_step"), sem("ln_root")
        bn_root, u_ready = sem("bn_root"), sem("u_ready")
        fin_scaled, fin_moved, fin_ready = sem("fin_scaled"), sem("fin_moved"), sem("fin_ready")
        y_counted, y_step, y_rooted = sem("y_counted"), sem("y_step"), sem("y_rooted")
        y_centred, y_scaled, y_gained = sem("y_centred"), sem("y_scaled"), sem("y_gained")
        y_done, y_last, y_stored = sem("y_done"), sem("y_last"), sem("y_stored")
        out_landed = sem("out_landed")

        block = ctx.enter_context(nc.Block())

        def x32_tile(j):
            if j.trip is None:
                return x32[:, j.base, :]
            return x32[:, bass.ds(j.at(), 1), :].rearrange("p a t -> p (a t)")

        def gated(j, c):
            return v_tmp[:, c, 0:2 * P] if j % 2 else gate_even[:, c]

        def tr_index(s, u):
            return s.times(8, T_STEP[s.base >= STEP_B] + u)

        def hi_index(s, u):
            return s.times(8, H_STEP[s.base >= STEP_B] + u)

        def fox(s):
            return STEP_FOX <= s.base < STEP_LAST

        def step_kind(s):
            return s.plus(-STEP_FOX) if fox(s) else Pos({0: 0, 1: 1, STEP_B: 0, STEP_LAST: 1}[s.base])

        def step_tile(s):
            return step_kind(s).at() if fox(s) else PAIRS + step_kind(s).at()

        def keys(s, u):
            return u % TT + 1 if fox(s) else MT

        def p_buffers(s):
            return (pb_hi, pb_lo) if s.base >= STEP_B else (pa_hi, pa_lo)

        @block.sync
        def _(sp):
            def load(b, source):
                wait(sp, w_split, b.at(-1))
                sp.dma_start(w_raw[:, b.slot], source).then_inc(w_landed[b.slot], 16)

            def cols(w, c, r=0):
                return w[r:r + D, bass.ds(c, P)].rearrange("(k p) n -> p k n", p=P)

            def memory_weights(layer, parts):
                for c in parts:
                    load(Pos(B_MEM[layer][c]), cols(mem_w_kv[layer], c * P))

            def feed_forward(layer):
                for half in range(2):
                    with sp.Fori(0, FT // 2) as i:
                        for c in range(2):
                            load(Pos(B_UP[layer][half] + c, i, 2),
                                 cols(w_up[layer], i * (2 * P) + (half * FT + c) * P))
                    with sp.Fori(0, KT) as i:
                        for c in range(2):
                            load(Pos(B_DN[layer][half] + c, i, 2),
                                 cols(w_down[layer], i * P, (half * 2 + c) * D))

            memory_weights(0, range(4))
            with sp.Fori(0, PAIRS // 2) as i:
                for c in range(2):
                    load(Pos(B_AV + c, i, 2), cols(a_w_in[0], i * (2 * P) + DMIX + c * P))
            for c in range(MEMPAIRS):
                load(Pos(B_AQ + c), cols(a_w_in[0], 2 * DMIX + c * P))
            with sp.Fori(0, PAIRS // 2) as i:
                for c in range(2):
                    load(Pos(B_AU + c, i, 2), cols(a_w_in[0], i * (2 * P) + c * P))
            with sp.Fori(0, KT // 2) as i:
                for c in range(2):
                    load(Pos(B_WO[0] + c, i, 2), cols(w_o[0], i * (2 * P) + c * P))
            memory_weights(1, range(2))
            feed_forward(0)
            memory_weights(1, range(2, 4))
            for c in range(MEMPAIRS):
                load(Pos(B_BQ + c), cols(b_w_q[0], DMIX + c * P))
            with sp.Fori(0, PAIRS // 2) as i:
                for j in range(2):
                    load(Pos(B_FOX + 3 * j, i, 6), cols(b_w_q[0], i * (2 * P) + j * P))
                    load(Pos(B_FOX + 3 * j + 1, i, 6), cols(kv_w, i * (2 * P) + j * P))
                    load(Pos(B_FOX + 3 * j + 2, i, 6), cols(kv_w, i * (2 * P) + DMIX + j * P))
            with sp.Fori(0, KT // 2) as i:
                for c in range(2):
                    load(Pos(B_WO[1] + c, i, 2), cols(w_o[1], i * (2 * P) + c * P))
            feed_forward(1)
            rows = out[0].rearrange("(t p) d -> p t d", p=P)
            for t in range(TT - 1):
                for c in range(2):
                    half = slice(c * D // 2, (c + 1) * D // 2)
                    sp.wait_ge(y_done, 2 * t + c + 1)
                    sp.dma_start(rows[:, t, half], y_nat[:, t, half]).then_inc(y_stored, 16)
            sp.wait_ge(y_stored, 32 * TT)

        @block.tensor
        def _(pe):
            def products(target, terms, start=True, stop=True):
                for n, (lhs, rhs) in enumerate(terms):
                    last = pe.matmul(target, lhs, rhs, start=start and n == 0,
                                     stop=stop and n == len(terms) - 1)
                return last

            def block_terms(b, k, hi, lo):
                return [(w_hi[:, b.slot, k], hi), (w_hi[:, b.slot, k], lo), (w_lo[:, b.slot, k], hi)]

            def project(b, g, hi, lo, columns=T, order=range(KT), ready=None, parts=(0, KT),
                        start=True, stop=True):
                bank = proj[g.slot]
                for n in range(*parts):
                    k = order[n]
                    if n == 0:
                        pe.wait_ge(w_split, b.at(1))
                        if start:
                            wait(pe, proj_free[g.slot], g.half())
                    if ready:
                        ready(n)
                    last = products(bank[:, 0:columns], block_terms(b, k, hi[:, k], lo[:, k]),
                                    start and n == 0, stop and n == KT - 1)
                if parts[1] == KT:
                    last.then_inc(w_used, 1)

            def transposes(t, pieces):
                wait(pe, tr_free, t.at(-1))
                at = 0
                for piece in pieces:
                    rows, n = piece.shape[0], piece.shape[-1]
                    last = pe.transpose(tr[t.slot][0:n, at:at + rows], piece, ident[0:rows, 0:rows])
                    at += rows
                last.then_inc(tr_done, 1)

            def memory_transposes(layer, n):
                pe.wait_ge(mem2_landed if layer else mem_landed[n // 2], 16)
                transposes(Pos(T_MEM[layer] + n), [mem_in[layer][:, m, k * P:(k + 1) * P]
                                                   for k in (2 * n, 2 * n + 1) for m in range(MT)])

            def memory_projection(layer, c, parts=(0, KT)):
                def ready(k):
                    if k % 2 == 0:
                        pe.wait_ge(tr_free, T_MEM[layer] + k // 2 + 1)
                project(Pos(B_MEM[layer][c]), Pos(G_MEM[layer][c]), mem_hi[layer], mem_lo[layer], M, parts=parts,
                        ready=ready if c == 0 else None)

            def memory_values(layer):
                for c in range(2, 4):
                    g = Pos(G_MEM[layer][c])
                    pe.wait_ge(proj_free[g.slot], g.half(2))
                transposes(Pos(T_MV[layer]), [v_tmp[:, c, m * P:(m + 1) * P] for m in range(MT) for c in range(2)])

            def scores(s, u):
                head, i, n = u // TT, u % TT, keys(s, u) * P
                rows = slice(head * HALF, (head + 1) * HALF)
                here = slice(i * P, (i + 1) * P)
                wait(pe, exp_done, s.at(u - 1, 8))
                bank = sc[u % 2]
                if fox(s):
                    c = step_kind(s).slot
                    if u == 0:
                        g = step_kind(s).times(3, G_FOX)
                        for q in (g, g.plus(1)):
                            pe.wait_ge(proj_free[q.slot], Pos(q.base, q.trip, q.step).half(2))
                        pe.wait_ge(row_ready, step_kind(s).at(1))
                    products(bank[:, 0:n], [(ones_r[rows, :], cum_row[rows, 0:n])], stop=False)
                    products(bank[:, here], [(ident_r[:, :], causal_r[:, :])], start=False, stop=False)
                    qh, ql, kh, kl = q_hi[rows, c, here], q_lo[rows, c, here], k_hi[rows, c, 0:n], k_lo[rows, c, 0:n]
                else:
                    c = step_kind(s).at()
                    if u == 0 and s.base in (STEP_A, STEP_B):
                        for q in range(MEMPAIRS):
                            pe.wait_ge(proj_free[q], ((G_AQ, G_BQ)[s.base == STEP_B] + q) // 2 + 1)
                    qh, ql, kh, kl = qm_hi[rows, c, here], qm_lo[rows, c, here], mk_hi[rows, c, :], mk_lo[rows, c, :]
                products(bank[:, 0:n], [(qh, kl), (ql, kh), (qh, kh)], start=not fox(s)).then_inc(sc_done, 1)

            def turn(s, u):
                pe.wait_ge(probs_ready, s.at(u + 1, 8))
                transposes(tr_index(s, u), [probs[:, u % 2, j * P:(j + 1) * P] for j in range(keys(s, u))])

            def attend(s, head):
                pe.wait_ge(tr_free, tr_index(s, head * TT + TT - 1).at(1))
                wait(pe, mix_ready, s.at(head - 1, 2))
                if s.base == STEP_B and head == 1:
                    pe.wait_ge(f_step, 1)
                hi, lo = p_buffers(s)
                c = step_kind(s).slot
                if fox(s) and head == 0:
                    pe.wait_ge(vt_ready, step_kind(s).at(1))
                tiles = TT if fox(s) else MT
                for j in range(tiles):
                    seen = slice(j * P if fox(s) else 0, T)
                    if fox(s):
                        vh, vl = v_hi[:, c, j], v_lo[:, c, j]
                    else:
                        vh, vl = mv_hi[:, j, c * P:(c + 1) * P], mv_lo[:, j, c * P:(c + 1) * P]
                    ph, pl = hi[:, head, j, seen], lo[:, head, j, seen]
                    last = products(pv[head][:, seen], [(vh, ph), (vh, pl), (vl, ph)], j == 0, j == tiles - 1)
                last.then_inc(pv_done, 1)

            def turn_values(s, j):
                g = j.times(3, G_FOX + 2)
                pe.wait_ge(proj_free[g.slot], g.half(2))
                if s is not None:
                    pe.wait_ge(mix_ready, s.at(1, 2))
                for t in range(TT):
                    last = pe.transpose(pv[0][:, t * P:(t + 1) * P], v_tmp[:, g.slot, t * P:(t + 1) * P], ident[:, :])
                last.then_inc(vt_done, 1)

            def pair_step(s, b=None, g=None, values=None, extra=None, early=0, after=None):
                at = [0, 5, 7] if s.base in (STEP_A, STEP_B) else [0, 3, 6]
                at += [8, 11, 14, 16, 18, 19, 21, 24]

                def filler(n):
                    if b is not None:
                        c = at[n] // KT
                        project(b.plus(c), g.plus(c), x_hi, x_lo, parts=(at[n] - c * KT, at[n + 1] - c * KT))
                    elif extra and n in extra:
                        out_start(1, *extra[n])
                for u in range(8):
                    filler(u)
                    if u >= 2:
                        turn(s, u - 2)
                    if u >= early:
                        scores(s, u)
                attend(s, 0)
                turn(s, 6)
                filler(8)
                if after:
                    scores(after, 0)
                turn(s, 7)
                if s.base == STEP_B:
                    cumulate()
                filler(9)
                if after:
                    scores(after, 1)
                attend(s, 1)
                if values is not None:
                    turn_values(s, values)

            def project_two(b, g, n0):
                pe.wait_ge(w_split, b.at(1))
                wait(pe, proj_free[g.slot], g.half())
                bank, slot = proj[g.slot], b.slot
                for k in range(KT + 3):
                    if k < KT:
                        pe.wait_ge(x_hi_ready, n0 + k + 1)
                        products(bank[:, :], [(w_hi[:, slot, k], x_hi[:, k]), (w_lo[:, slot, k], x_hi[:, k])], k == 0, False)
                    if 0 < k <= KT:
                        pe.wait_ge(x_ready, n0 + k)
                        last = products(bank[:, :], [(w_hi[:, slot, k - 1], x_lo[:, k - 1])], False, k == KT)
                        if k == KT:
                            last.then_inc(w_used, 1)
                    if k >= 3:
                        project(b.plus(1), g.plus(1), x_hi, x_lo, parts=(k - 3, k - 2))

            out_order = [[6, 7, 0, 1, 2, 3, 4, 5], [6, 0, 1, 2, 3, 4, 5, 7]]

            def out_start(layer, c, n):
                def ready(n):
                    if layer:
                        pe.wait_ge(mix_ready, 2 * (STEP_B + n) + 2)
                    elif n < 2:
                        pe.wait_ge(mix_ready, 2 * n + 2)
                    else:
                        pe.wait_ge(sgu_ready, 2 * (n - 1))
                project(Pos(B_WO[layer] + c), Pos(G_WO[layer] + c), mix_hi, mix_lo, order=out_order[layer],
                        ready=ready, parts=(n, n + 1))

            def out_projection(layer):
                b, g = Pos(B_WO[layer]), Pos(G_WO[layer])
                for j in range(2, KT):
                    if j == KT - 1:
                        project(b.plus(j), g.plus(j), mix_hi, mix_lo, order=out_order[layer], parts=(0, 6))
                        layer_sums(2 * layer, g.base + j, True)
                        project(b.plus(j), g.plus(j), mix_hi, mix_lo, order=out_order[layer], parts=(6, KT))
                    elif j == 2:
                        project(b.plus(j), g.plus(j), mix_hi, mix_lo, order=out_order[layer], parts=(0, 5))
                        shift_sum(2 * layer)
                        project(b.plus(j), g.plus(j), mix_hi, mix_lo, order=out_order[layer], parts=(5, KT))
                    else:
                        project(b.plus(j), g.plus(j), mix_hi, mix_lo, order=out_order[layer])
                    if layer == 0 and j < 6:
                        memory_transposes(1, j - 2)

            def shift_sum(n):
                pe.wait_ge(shift_ready, n + 1)
                products(sc[0][:, :], [(ones_r[:, :], shift_in[:, :])]).then_inc(shift_done, 1)

            def layer_sums(n, g, early):
                for bank, added, sums, done, count, last_tile in (
                        (sc[0], sum_added, total, proj_free[g % 2], g // 2 + 1, x32[:, KT - 1]),
                        (sc[1], sq_added, total_sq, sq_ready, KT * (n + 1), square[:, 1])):
                    if early:
                        pe.wait_ge(added, (KT - 2) * (n + 1))
                    else:
                        pe.wait_ge(done, count)
                    part = sums if early else last_tile
                    for t in range(TT):
                        last = pe.matmul(bank[:, t:t + 1], part[:, t * P:(t + 1) * P], ones_f[:, 0:1],
                                         start=early and t == 0, stop=not early, skip_group_check=True)
                    if not early:
                        last.then_inc(stat_done, 1)

            def layer_spread(n):
                for q, column in enumerate((ln_rstd, ln_move)):
                    pe.wait_ge(ln_step, 5 * n + 4 + q)
                    for t in range(TT):
                        last = pe.transpose(sc[q][:, t * P:(t + 1) * P], column[:, t:t + 1].broadcast_to([P, P]), ident[:, :])
                    last.then_inc(spread_done, 1)

            def turn_result(j, g):
                pe.wait_ge(proj_free[g.slot], g.half(2))
                transposes(j.plus(T_OUT), [y_in[:, j.slot, t * P:(t + 1) * P] for t in range(TT)])

            def feed_forward(layer):
                for half in range(2):
                    b, g = Pos(B_UP[layer][half]), Pos(G_UP[layer][half])
                    if half:
                        for c in range(2):
                            project(b.plus(c), g.plus(c), x_hi, x_lo)
                    else:
                        project_two(b, g, KT * (2 * layer + 1))
                    with pe.Fori(0, FT // 2 - 1) as i:
                        for c in range(2, 4):
                            project(Pos(b.base + c, i, 2), Pos(g.base + c, i, 2), x_hi, x_lo)
                    b, g = B_DN[layer][half], G_DN[layer][half]
                    h0 = (2 * layer + half) * FT

                    def down(b, g, ready=False, between=None):
                        for c in range(2):
                            if c and between:
                                between()
                            project(b.plus(c), g, h_hi[:, c * KT:(c + 1) * KT], h_lo[:, c * KT:(c + 1) * KT],
                                    ready=(lambda n: pe.wait_ge(h_ready, h0 + c * KT + n + 1)) if ready else None,
                                    start=c == 0, stop=c == 1)
                    if half and layer:
                        down(Pos(b), Pos(g), True)
                        down(Pos(b + 2), Pos(g + 1), between=lambda: turn_result(Pos(0), Pos(g)))
                        with pe.Fori(0, KT // 2 - 1) as i:
                            for j in range(2, 4):
                                down(Pos(b + 2 * j, i, 4), Pos(g + j, i, 2),
                                     between=lambda: turn_result(Pos(j - 1, i, 2), Pos(g + j - 1, i, 2)))
                        turn_result(Pos(KT - 1), Pos(g + KT - 1))
                        continue
                    for j in range(2):
                        down(Pos(b + 2 * j), Pos(g + j), j == 0)
                    if half:
                        shift_sum(2 * layer + 1)
                    with pe.Fori(0, KT // 2 - 1 - half) as i:
                        for j in range(2):
                            down(Pos(b + 4 + 2 * j, i, 4), Pos(g + 2 + j, i, 2))
                    if half:
                        j = KT - 1
                        down(Pos(b + 2 * j - 2), Pos(g + j - 1))
                        project(Pos(b + 2 * j), Pos(g + j), h_hi[:, 0:KT], h_lo[:, 0:KT], stop=False)
                        layer_sums(2 * layer + 1, g + j, True)
                        project(Pos(b + 2 * j + 1), Pos(g + j), h_hi[:, KT:2 * KT], h_lo[:, KT:2 * KT], start=False)

            def spatial_gate():
                pe.wait_ge(exp_done, 16)
                for j in range(PAIRS):
                    pe.wait_ge(z_ready, j + 1)
                    both = slice(2 * j, 2 * j + 2)
                    for c in range(2):
                        wait(pe, sgu_added, 2 * (j - 1) + c + 1)
                        for n in range(2):
                            zh, zl = z_hi[:, j % 2, 2 * c + n], z_lo[:, j % 2, 2 * c + n]
                            last = products(sc[c][:, n * 2 * P:(n + 1) * 2 * P],
                                            [(zh, ws_hi[:, both]), (zh, ws_lo[:, both]), (zl, ws_hi[:, both])])
                        last.then_inc(sgu_done, 1)
                    out_start(0, 0, j)
                    if j >= 2:
                        out_start(0, 1, j - 2)

            def forget_gate():
                pe.wait_ge(wf_ready, 1)
                terms = []
                for k in range(KT):
                    terms += [(wf_hi[:, k], x_hi[:, k]), (wf_hi[:, k], x_lo[:, k]), (wf_lo[:, k], x_hi[:, k])]
                products(pv[1][0:HEADS, :], terms).then_inc(f_done, 1)

            def turn_forget_gate():
                pe.wait_ge(f_out, 1)
                for t in range(TT):
                    last = pe.transpose(pv[1][:, t * HEADS:(t + 1) * HEADS], f_turned[0:HEADS, t * P:(t + 1) * P],
                                        ident[0:HEADS, 0:HEADS])
                last.then_inc(f_done, 1)

            def cumulate():
                pe.wait_ge(f_act, 3)
                pe.wait_ge(f_step, 5)
                pe.wait_ge(exp_done, 8 * STEP_B + 7)
                for t in range(TT):
                    span = tri_r[:, 0:T - t * P]
                    last = products(sc[0][:, t * P:T], [(lf_hi[:, t], span), (lf_lo[:, t], span)],
                                    t == 0, t == TT - 1)
                last.then_inc(cum_done, 1)

            pe.wait_ge(const_ready, 1)
            for n in range(4):
                memory_transposes(0, n)
            for c in range(4):
                memory_projection(0, c)
                for k in (2 * c, 2 * c + 1):
                    pe.wait_ge(x_landed[k // (KT // 2)], 16)
                    transposes(Pos(T_X + k), [x_nat[:, t, k * P:(k + 1) * P] for t in range(TT)])
            memory_values(0)

            def turn_v(t, g):
                pe.wait_ge(proj_free[g.slot], g.half(2))
                transposes(t, [v_tmp[:, g.slot, t * P:(t + 1) * P] for t in range(TT)])
            project(Pos(B_AV), Pos(G_AV), x_hi, x_lo, ready=lambda k: pe.wait_ge(x_ready, k + 1))
            with pe.Fori(0, PAIRS // 2 - 1) as i:
                for c in range(2):
                    project(Pos(B_AV + 1 + c, i, 2), Pos(G_AV + 1 + c, i, 2), x_hi, x_lo)
                    turn_v(Pos(T_AV + c, i, 2), Pos(G_AV + c, i, 2))
            for c in range(PAIRS - 1, PAIRS + 1):
                project(Pos(B_AV + c), Pos(G_AV + c), x_hi, x_lo)
                turn_v(Pos(T_AV + c - 1), Pos(G_AV + c - 1))
            pe.wait_ge(par_landed, 32)
            transposes(Pos(T_PAR), [par_raw[:, :]])
            pe.wait_ge(ws_masked, 1)
            for n in range(4):
                project(Pos(B_AQ + 1), Pos(G_AQ + 1), x_hi, x_lo, parts=(2 * n, 2 * n + 2))
                if n < 3:
                    transposes(Pos(T_WS + n), [ws_raw[:, h] for h in range(4 * n, 4 * n + 4)])
            for s in range(2):
                pair_step(Pos(STEP_A + s), Pos(B_AU + 3 * s), Pos(G_AU + 3 * s))
            spatial_gate()
            for c, n in ((0, 6), (1, 4), (0, 7), (1, 5), (1, 6), (1, 7)):
                out_start(0, c, n)
            out_projection(0)
            layer_sums(0, G_WO[0] + KT - 1, False)
            memory_projection(1, 0, (0, 5))
            layer_spread(0)
            memory_projection(1, 0, (5, KT))
            memory_projection(1, 1)
            feed_forward(0)
            memory_projection(1, 2, (0, 4))
            layer_sums(1, G_DN[0][1] + KT - 1, False)
            memory_projection(1, 2, (4, KT))
            layer_spread(1)
            memory_projection(1, 3)

            project_two(Pos(B_BQ), Pos(G_BQ), 2 * KT)
            forget_gate()
            memory_values(1)
            turn_forget_gate()
            pair_step(Pos(STEP_B), Pos(B_FOX), Pos(G_FOX), values=Pos(0))
            with pe.Fori(0, 2) as i:
                for j in range(2):
                    pair_step(Pos(STEP_FOX + j, i, 2), Pos(B_FOX + 3 * (j + 1), i, 6),
                              Pos(G_FOX + 3 * (j + 1), i, 6), values=Pos(j + 1, i, 2))
            pair_step(Pos(7), Pos(B_FOX + 15), Pos(G_FOX + 15), values=Pos(5))
            pair_step(Pos(8), extra={0: (0, 0), 1: (0, 1), 3: (1, 0), 5: (0, 2), 9: (1, 1)}, after=Pos(STEP_LAST))
            pair_step(Pos(STEP_LAST), extra={0: (1, 2), 2: (0, 3), 4: (1, 3), 6: (0, 4), 8: (0, 5)}, early=2)
            for c, n in ((0, 6), (1, 4), (0, 7), (1, 5), (1, 6), (1, 7)):
                out_start(1, c, n)
            out_projection(1)
            layer_sums(2, G_WO[1] + KT - 1, False)
            layer_spread(2)
            feed_forward(1)

        @block.scalar
        def _(act):
            def prepare(b):
                if b.trip is None and b.base >= B_DN[1][1] + 2 * KT:
                    return
                act.wait_ge(w_landed[b.slot], b.half(2) * 16)
                wait(act, w_used, b.at(-1))
                act.copy(w_hi[:, b.slot], w_raw[:, b.slot]).then_inc(w_hi_ready, 1)

            def turned_hi(t, target, source=None):
                act.wait_ge(tr_done, t.at(1))
                act.copy(target, tr[t.slot][:, :] if source is None else source).then_inc(tr_hi, 1)

            def projected(b, g, target, scale=1.0):
                act.wait_ge(w_used, b.at(1))
                act.activation(target, proj[g.slot][:, 0:target.shape[-1]], ACT.Copy, scale=scale).then_inc(qk_hi, 1)

            def plain(b, g, target, function=ACT.Copy):
                act.wait_ge(w_used, b.at(1))
                act.activation(target, proj[g.slot][:, 0:target.shape[-1]], function).then_inc(proj_free[g.slot], 1)

            def memory_hi(layer, n):
                turned_hi(Pos(T_MEM[layer] + n), mem_hi[layer][:, 2 * n:2 * n + 2],
                          tr[(T_MEM[layer] + n) % 2][:, :].rearrange("p (k m) -> p k m", k=2))

            def memory_projection(layer, c):
                b, g = Pos(B_MEM[layer][c]), Pos(G_MEM[layer][c])
                if c < 2:
                    projected(b, g, mk_hi[:, c, :])
                else:
                    plain(b, g, v_tmp[:, c - 2, 0:M])

            def memory_values(layer):
                turned_hi(Pos(T_MV[layer]), mv_hi[:, :, :], tr[T_MV[layer] % 2][:, :].rearrange("p (m c) -> p m c", m=MT))

            def exponentials(s, u):
                n = keys(s, u) * P
                act.wait_ge(max_done, s.at(u + 1, 8))
                act.activation(probs[:, u % 2, 0:n], sc[u % 2][:, 0:n], ACT.Exp, bias=neg_max[:, u:u + 1],
                               accum_out=row_sum[:, u:u + 1]).then_inc(exp_done, 1)

            def turned_probs(s, u):
                n, here, t = keys(s, u), slice(u % TT * P, (u % TT + 1) * P), tr_index(s, u)
                turned_hi(t, p_buffers(s)[0][:, u // TT, 0:n, here],
                          tr[t.slot][:, 0:n * P].rearrange("p (j t) -> p j t", j=n))

            def attended(s, head):
                rows = slice(head * HALF, (head + 1) * HALF)
                act.wait_ge(pv_done, s.at(head + 1, 2))
                act.copy(mix_hi[rows, bass.ds(step_tile(s), 1), :], pv[head][rows, :].rearrange("p (a t) -> p a t", a=1))\
                    .then_inc(mix_hi_ready, 1)

            def step_projection(s, b, g, c):
                if s.base < STEP_B:
                    plain(b, g, u_t[:, g.base - G_AU, :])
                elif c < 2:
                    j = (g.base - G_FOX) // 3 % 2
                    projected(b, g, (q_hi, k_hi)[c][:, j, :], SCALE if c == 0 else 1.0)
                else:
                    plain(b, g, v_tmp[:, g.slot, :])

            def pair_step(s, b=None, g=None, values=None, late=None):
                for u in range(8):
                    if b is not None and u in (0, 3, 6):
                        prepare(b.plus(u // 3 + 1))
                    if late is not None and u == 1:
                        prepare(late)
                    if u >= 2:
                        turned_probs(s, u - 2)
                    exponentials(s, u)
                    if b is not None and u in (2, 5):
                        step_projection(s, b.plus(u // 3), g.plus(u // 3), u // 3)
                attended(s, 0)
                turned_probs(s, 6)
                turned_probs(s, 7)
                if b is not None:
                    step_projection(s, b.plus(2), g.plus(2), 2)
                attended(s, 1)
                if values is not None:
                    act.wait_ge(vt_done, values.at(1))
                    act.copy(v_hi[:, values.slot], pv[0][:, :].rearrange("p (t c) -> p t c", t=TT)).then_inc(vt_hi, 1)

            def squares(n, j, g):
                if j.base < 2:
                    act.wait_ge(shifted, 2 * n + j.base + 1)
                else:
                    act.wait_ge(proj_free[g.slot], g.half(2))
                    wait(act, sq_added, j.at((KT - 2) * n - 1))
                act.activation(square[:, j.slot, :], x32_tile(j), ACT.Square).then_inc(sq_ready, 1)

            def shift_source(n, g):
                act.wait_ge(proj_free[g % 2], g // 2 + 1)
                act.copy(shift_in[:, :], x32[:, 0]).then_inc(shift_ready, 1)

            def root(n):
                act.wait_ge(ln_step, 5 * n + 3)
                act.activation(ln_sqrt[:, :], ln_var[:, :], ACT.Sqrt, bias=eps[:, 0:1]).then_inc(ln_root, 1)

            def finish(n, tiles):
                for k in tiles:
                    act.wait_ge(fin_moved, KT * n + k + 1)
                    gain = dict(bias=par[:, 32 + KT * n + k:33 + KT * n + k], scale=par[:, KT * n + k:KT * n + k + 1])
                    if k == 0:
                        act.activation(x_hi[:, k], x32[:, k], ACT.Identity, **gain).then_inc(x_hi_ready, 1)
                        act.wait_ge(x_hi_ready, KT * (n + 1) + k + 1)
                        act.activation(x32[:, k], x32[:, k], ACT.Identity, **gain).then_inc(fin_ready, 1)
                    else:
                        act.activation(x32[:, k], x32[:, k], ACT.Identity, **gain).then_inc(fin_ready, 1)
                        act.wait_ge(fin_ready, KT * n + k + 1)
                        act.copy(x_hi[:, k], x32[:, k]).then_inc(x_hi_ready, 1)

            def turned_result(j):
                act.wait_ge(tr_done, j.at(T_OUT + 1))
                act.copy(y_nat[:, :, bass.ds(j.at(0, P), P)], tr[j.slot][:, :].rearrange("p (t c) -> p t c", t=TT))\
                    .then_inc(tr_free, 1)

            def feed_forward(layer):
                for half in range(2):
                    def up(tile):
                        b, g = tile.plus(B_UP[layer][half]), tile.plus(G_UP[layer][half])
                        h = tile.plus((2 * layer + half) * FT)
                        if half or tile.trip is not None:
                            prepare(b.plus(1))
                        elif tile.base == 0:
                            prepare(b.plus(2))
                        wait(act, relu_sq, h.at(-1))
                        plain(b, g, relu[:, tile.slot, :], ACT.Relu)
                        act.wait_ge(proj_free[g.slot], g.half(2))
                        act.activation(h_hi[:, bass.ds(tile.at(), 1), :], relu[:, tile.slot:tile.slot + 1, :],
                                       ACT.Square).then_inc(h_hi_ready, 1)
                    up(Pos(0))
                    up(Pos(1))
                    with act.Fori(0, FT // 2 - 1) as i:
                        up(Pos(2, i, 2))
                        up(Pos(3, i, 2))
                    b, n = B_DN[layer][half], 2 * layer + 1
                    if not half:
                        with act.Fori(0, KT) as i:
                            for c in range(2):
                                prepare(Pos(b + c + 1, i, 2))
                        continue
                    if layer:
                        for c in range(2):
                            prepare(Pos(b + c + 1))
                        with act.Fori(0, KT // 2 - 1) as i:
                            for j in range(2):
                                for c in range(2):
                                    prepare(Pos(b + 3 + 2 * j + c, i, 4))
                                turned_result(Pos(j, i, 2))
                        prepare(Pos(b + 2 * KT - 1))
                        turned_result(Pos(KT - 2))
                        turned_result(Pos(KT - 1))
                        continue
                    for c in range(4):
                        prepare(Pos(b + c + 1))
                    g = G_DN[layer][half]
                    shift_source(n, g)
                    for j in range(2):
                        squares(n, Pos(j), Pos(g + j))
                    with act.Fori(0, 2) as i:
                        for j in range(2):
                            for c in range(2):
                                prepare(Pos(b + 4 + 2 * j + c + 1, i, 4))
                            squares(n, Pos(2 + j, i, 2), Pos(g + 2 + j, i, 2))
                    for j in range(6, KT):
                        for c in range(2):
                            prepare(Pos(b + 2 * j + c + 1))
                        squares(n, Pos(j), Pos(g + j))
                    if layer == 0:
                        prepare(Pos(B_MEM[1][3]))
                    root(n)
                    if layer == 0:
                        memory_projection(1, 2)
                        prepare(Pos(B_BQ))
                    finish(n, range(2))
                    if layer == 0:
                        memory_projection(1, 3)
                        prepare(Pos(B_BQ + 1))
                    finish(n, range(2, KT))

            def out_projection(layer):
                b, g = B_WO[layer], G_WO[layer]
                prepare(Pos(b + 2))
                shift_source(2 * layer, g)
                prepare(Pos(b + 3))
                for j in range(KT):
                    if 2 <= j < KT - 1:
                        prepare(Pos(b + j + 2))
                    squares(2 * layer, Pos(j), Pos(g + j))
                    if layer == 0 and 2 <= j < 6:
                        memory_hi(1, j - 2)

            for c in range(2):
                half = slice(c * D // 2, (c + 1) * D // 2)
                act.dma_start(mem_nat[:, :, half], mem[0].rearrange("(m p) d -> p m d", p=P)[:, :, half]).then_inc(mem_landed[c], 16)
            for c in range(2):
                half = slice(c * D // 2, (c + 1) * D // 2)
                act.dma_start(x_nat[:, :, half], x[0].rearrange("(t p) d -> p t d", p=P)[:, :, half]).then_inc(x_landed[c], 16)

            def gate_input(j):
                g = j.plus(G_AV)
                plain(j.plus(B_AV), g, v_tmp[:, g.slot, :], ACT.Gelu_apprx_tanh)

            prepare(Pos(0))
            for n in range(4):
                memory_hi(0, n)
            for c in range(4):
                prepare(Pos(c + 1))
                if c == 0:
                    act.dma_start(par_raw[0:32, :], ln_g.rearrange("l i (k p) -> (l i k) p", p=P)).then_inc(par_landed, 16)
                    act.dma_start(par_raw[32:64, :], ln_b.rearrange("l i (k p) -> (l i k) p", p=P)).then_inc(par_landed, 16)
                    act.dma_start(ws_raw[:, :, :], a_w_s[0].rearrange("h t s -> t h s")).then_inc(ws_landed, 16)
                memory_projection(0, c)
                for k in (2 * c, 2 * c + 1):
                    act.wait_ge(tr_free, T_X + k + 1)
                    act.copy(x_hi[:, k], x32[:, k]).then_inc(x_hi_ready, 1)
            memory_values(0)
            prepare(Pos(B_AV + 1))
            act.dma_start(g_all[:, :], a_sgu_ln_g.broadcast_to([P, DMIX])).then_inc(sgu_landed, 16)
            act.dma_start(b_all[:, :], a_sgu_ln_b.broadcast_to([P, DMIX])).then_inc(sgu_landed, 16)
            for head in range(2):
                own = a_b_s.rearrange("a (j e) t -> a e j t", e=2)[:, head].broadcast_to([HALF, PAIRS, P])
                act.dma_start(bs_all[head * HALF:(head + 1) * HALF, :, :], own).then_inc(sgu_landed, 16)
            act.dma_start(wf_raw[:, :, :], kv_w[:, 2 * DMIX:].rearrange("(k p) n -> p k n", p=P)).then_inc(wf_landed, 16)
            act.dma_start(bf_row[:, :], kv_b_f.rearrange("(a n) -> a n", a=1).broadcast_to([P, HEADS])).then_inc(wf_landed, 16)
            act.wait_ge(const_ready, 3)
            act.copy(ident_r[:, :], ident[:, :])
            act.copy(causal_r[:, :], causal[:, :])
            act.copy(tri_r[:, :], tri_f[:, :]).then_inc(const_r, 1)
            gate_input(Pos(0))
            with act.Fori(0, PAIRS // 2 - 1) as i:
                for c in range(2):
                    prepare(Pos(B_AV + c + 2, i, 2))
                    gate_input(Pos(c + 1, i, 2))
            prepare(Pos(B_AV + PAIRS))
            gate_input(Pos(PAIRS - 1))
            for c in range(MEMPAIRS):
                prepare(Pos(B_AQ + c + 1))
                if c == 1:
                    for n in range(3):
                        turned_hi(Pos(T_WS + n), ws_hi[:, 4 * n:4 * n + 4],
                                  tr[(T_WS + n) % 2][:, :].rearrange("p (h t) -> p h t", h=4))
                projected(Pos(B_AQ + c), Pos(G_AQ + c), qm_hi[:, c, :], SCALE)
            act.wait_ge(bn_step, 3 * TT)
            act.activation(sgu_root[:, :], sgu_mv[:, :, 1], ACT.Sqrt, bias=eps[:, 0:1]).then_inc(bn_root, 1)
            pair_step(Pos(STEP_A), Pos(B_AU), Pos(G_AU))
            act.wait_ge(zg_ready, TT)
            for j in range(2):
                act.copy(z_hi[:, j % 2], z_nat[:, :, j * P:(j + 1) * P]).then_inc(z_hi_ready, 1)
            pair_step(Pos(STEP_A + 1), Pos(B_AU + 3), Pos(G_AU + 3))
            for j in range(PAIRS + 1):
                if j == 2:
                    prepare(Pos(B_WO[0] + 1))
                if j < PAIRS:
                    if j == 0:
                        for g in (G_WO[0] - 2, G_WO[0] - 1):
                            act.wait_ge(proj_free[g % 2], g // 2 + 1)
                    act.activation(u_t[:, j, :], u_t[:, j, :], ACT.Gelu_apprx_tanh).then_inc(u_ready, 1)
                if 0 < j < PAIRS - 1:
                    act.wait_ge(sgu_done, 2 * j)
                    act.copy(z_hi[:, (j + 1) % 2], z_nat[:, :, (j + 1) * P:(j + 2) * P]).then_inc(z_hi_ready, 1)
                for c in range(2):
                    if j:
                        act.wait_ge(sgu_gated, 2 * (j - 1) + c + 1)
                        act.copy(mix_hi[:, j - 1, c * 2 * P:(c + 1) * 2 * P], gated(j - 1, c)).then_inc(sgu_hi, 1)
            act.wait_ge(sgu_ready, 2 * PAIRS)
            act.dma_start(mem2_nat[:, :, :], mem[0].rearrange("(m p) d -> p m d", p=P)).then_inc(mem2_landed, 16)
            out_projection(0)
            prepare(Pos(27))
            root(0)
            memory_projection(1, 0)
            prepare(Pos(28))
            finish(0, range(2))
            memory_projection(1, 1)
            prepare(Pos(29))
            finish(0, range(2, KT))
            feed_forward(0)

            for c in range(MEMPAIRS):
                if c:
                    prepare(Pos(B_BQ + c + 1))
                projected(Pos(B_BQ + c), Pos(G_BQ + c), qm_hi[:, c, :], SCALE)
            memory_values(1)
            act.wait_ge(f_step, 2)
            act.activation(f_exp[:, :, :], f_abs[:, :, :], ACT.Exp).then_inc(f_act, 1)
            act.wait_ge(f_act, 1)
            act.activation(f_ln[:, :, :], f_exp[:, :, :], ACT.Ln, bias=1.0).then_inc(f_act, 1)
            act.wait_ge(f_step, 4)
            act.wait_ge(lf_zeroed, 2)
            for r in range(0, P, 32):
                last = act.copy(lf_hi[:, :, r:r + HEADS], f_sp[:, :, :])
            last.then_inc(f_act, 1)
            pair_step(Pos(STEP_B), Pos(B_FOX), Pos(G_FOX), values=Pos(0))
            act.wait_ge(cum_done, 1)
            act.copy(cum[:, :], sc[0][:, :]).then_inc(f_act, 1)
            with act.Fori(0, 2) as i:
                for j in range(2):
                    pair_step(Pos(STEP_FOX + j, i, 2), Pos(B_FOX + 3 * (j + 1), i, 6),
                              Pos(G_FOX + 3 * (j + 1), i, 6), values=Pos(j + 1, i, 2))
            pair_step(Pos(7), Pos(B_FOX + 15), Pos(G_FOX + 15), values=Pos(5))
            pair_step(Pos(8), late=Pos(B_WO[1] + 1))
            pair_step(Pos(STEP_LAST))
            out_projection(1)
            root(2)
            prepare(Pos(B_UP[1][0] + 1))
            act.dma_start(g_out[:, :], ln_g[1, 1:2, :].broadcast_to([P, D])).then_inc(out_landed, 16)
            act.dma_start(b_out[:, :], ln_b[1, 1:2, :].broadcast_to([P, D])).then_inc(out_landed, 16)
            finish(2, range(KT))
            feed_forward(1)
            act.wait_ge(y_step, 1)
            act.activation(y_root[:, :], y_mv[:, :, 1], ACT.Sqrt, bias=eps[:, 0:1]).then_inc(y_rooted, 1)
            act.wait_ge(y_step, 3)
            for c in range(2):
                part = y_nat[:, TT - 1, c * D // 2:(c + 1) * D // 2]
                act.activation(part, part, ACT.Identity, bias=y_move[:, TT - 1:TT], scale=y_rstd[:, TT - 1:TT])\
                    .then_inc(y_scaled, 1)
            for c in range(2):
                half = slice(c * D // 2, (c + 1) * D // 2)
                act.wait_ge(y_last, c + 1)
                act.dma_start(out[0, (TT - 1) * P:TT * P, half], y_nat[:, TT - 1, half]).then_inc(y_stored, 16)

        @block.vector
        def _(dve):
            def rest(target, whole, hi):
                return dve.tensor_tensor(target, whole, hi.bitcast(F32), ALU.subtract)

            def prepare(b):
                if b.trip is None and b.base >= B_DN[1][1] + 2 * KT:
                    return
                dve.wait_ge(w_hi_ready, b.at(1))
                rest(w_lo[:, b.slot], w_raw[:, b.slot], w_hi[:, b.slot]).then_inc(w_split, 1)

            def turned_lo(t, h, target, hi, source=None):
                dve.wait_ge(tr_hi, h.at(1))
                rest(target, tr[t.slot][:, :] if source is None else source, hi).then_inc(tr_free, 1)

            def projected(g, q, target, hi, scale=1.0):
                dve.wait_ge(qk_hi, q.at(1))
                source = proj[g.slot][:, 0:target.shape[-1]]
                if scale == 1.0:
                    rest(target, source, hi).then_inc(proj_free[g.slot], 1)
                else:
                    dve.scalar_tensor_tensor(out=target, in0=source, scalar=scale, in1=hi.bitcast(F32),
                                             op0=ALU.mult, op1=ALU.subtract).then_inc(proj_free[g.slot], 1)

            def memory_lo(layer, n):
                pair = slice(2 * n, 2 * n + 2)
                turned_lo(Pos(T_MEM[layer] + n), Pos(H_MEM[layer] + n), mem_lo[layer][:, pair], mem_hi[layer][:, pair],
                          tr[(T_MEM[layer] + n) % 2][:, :].rearrange("p (k m) -> p k m", k=2))

            def memory_keys(layer, c):
                projected(Pos(G_MEM[layer][c]), Pos(Q_MEM[layer] + c), mk_lo[:, c, :], mk_hi[:, c, :])

            def memory_values(layer):
                turned_lo(Pos(T_MV[layer]), Pos(H_MV[layer]), mv_lo[:, :, :], mv_hi[:, :, :],
                          tr[T_MV[layer] % 2][:, :].rearrange("p (m c) -> p m c", m=MT))

            def row_max(s, u):
                dve.wait_ge(sc_done, s.at(u + 1, 8))
                dve.tensor_reduce(neg_max[:, u:u + 1], sc[u % 2][:, 0:keys(s, u) * P], AX.X, ALU.max,
                                  negate=True).then_inc(max_done, 1)

            def normalize(s, u):
                own = probs[:, u % 2, 0:keys(s, u) * P]
                dve.wait_ge(exp_done, s.at(u + 1, 8))
                dve.reciprocal(inv_sum[:, u:u + 1], row_sum[:, u:u + 1]).then_inc(inv_done, 1)
                dve.wait_ge(inv_done, s.at(u + 1, 8))
                dve.tensor_scalar(own, own, inv_sum[:, u:u + 1], None, ALU.mult).then_inc(probs_ready, 1)

            def turned_probs(s, u):
                n, here, t = keys(s, u), slice(u % TT * P, (u % TT + 1) * P), tr_index(s, u)
                hi, lo = p_buffers(s)
                turned_lo(t, hi_index(s, u), lo[:, u // TT, 0:n, here], hi[:, u // TT, 0:n, here],
                          tr[t.slot][:, 0:n * P].rearrange("p (j t) -> p j t", j=n))

            def attended(s, head):
                rows = slice(head * HALF, (head + 1) * HALF)
                tile = bass.ds(step_tile(s), 1)
                dve.wait_ge(mix_hi_ready, s.at(head + 1, 2))
                rest(mix_lo[rows, tile, :], pv[head][rows, :].rearrange("p (a t) -> p a t", a=1),
                     mix_hi[rows, tile, :]).then_inc(mix_ready, 1)

            def gate_stats(n):
                if n == 0:
                    dve.wait_ge(tr_free, T_AV + PAIRS)
                for c in range(2):
                    dve.bn_stats(sgu_stats[:, n, c], z_nat[:, n, c * (DMIX // 2):(c + 1) * (DMIX // 2)]).then_inc(bn_step, 1)
                dve.wait_ge(bn_step, 3 * n + 2)
                dve.bn_aggr(sgu_mv[:, n], sgu_stats[:, n]).then_inc(bn_step, 1)

            def gate_norm(n):
                if n == 0:
                    dve.wait_ge(bn_root, 1)
                    dve.reciprocal(sgu_rstd[:, :], sgu_root[:, :]).then_inc(bn_step, 1)
                    dve.wait_ge(bn_step, 3 * TT + 1)
                dve.tensor_scalar(z_nat[:, n], z_nat[:, n], sgu_mv[:, n, 0:1], sgu_rstd[:, n:n + 1],
                                  ALU.subtract, ALU.mult).then_inc(zn_ready, 1)

            def step_projection(s, g, c, q):
                if s.base >= STEP_B and c < 2:
                    j = (g.base - G_FOX) // 3 % 2
                    projected(g, q.plus(c), (q_lo, k_lo)[c][:, j, :], (q_hi, k_hi)[c][:, j, :], SCALE if c == 0 else 1.0)

            def cum_rows(pair):
                dve.wait_ge(f_step, 6)
                dve.tensor_scalar(cum_row[:, :], cum[:, :].bitcast(F32), head_rows[:, bass.ds(pair.at(), 1)],
                                  None, ALU.mult).then_inc(row_ready, 1)

            def pair_step(s, b=None, g=None, q=None, values=None, late=None):
                for u in range(8):
                    row_max(s, u)
                    if b is not None and u in (0, 3, 6):
                        prepare(b.plus(u // 3 + 1))
                    if late is not None and u == 1:
                        prepare(late)
                    if u >= 2:
                        turned_probs(s, u - 2)
                    normalize(s, u)
                    if s.base == STEP_A and 1 <= u <= TT:
                        gate_norm(u - 1)
                    if b is not None and u in (2, 5):
                        step_projection(s, g.plus(u // 3), u // 3, q)
                attended(s, 0)
                turned_probs(s, 6)
                turned_probs(s, 7)
                if fox(s) and values is not None:
                    cum_rows(values)
                attended(s, 1)
                if values is not None:
                    dve.wait_ge(vt_hi, values.at(1))
                    rest(v_lo[:, values.slot], pv[0][:, :].rearrange("p (t c) -> p t c", t=TT),
                         v_hi[:, values.slot]).then_inc(vt_ready, 1)

            def residual(n, b, g, j, first=True, target=None):
                tile = x32_tile(j)
                dve.wait_ge(w_used, b.at(1))
                dve.scalar_tensor_tensor(out=tile if target is None else target, in0=tile, scalar=ALPHA if first else 1.0, in1=proj[g.slot][:, :],
                                         op0=ALU.mult, op1=ALU.add).then_inc(proj_free[g.slot], 1)

            def shift_tiles(n, g):
                for j in range(2):
                    dve.wait_ge(proj_free[j], g // 2 + 1)
                    dve.tensor_tensor(x32[:, j], x32[:, j], shift[:, :], ALU.subtract).then_inc(shifted, 1)

            def shifted_residual(n, b, g, j, first=True):
                tile = x32_tile(j)
                if first:
                    dve.scalar_tensor_tensor(out=tile, in0=tile, scalar=ALPHA, in1=shift[:, :],
                                             op0=ALU.mult, op1=ALU.subtract).then_inc(pre_shifted, 1)
                else:
                    dve.tensor_tensor(tile, tile, shift[:, :], ALU.subtract).then_inc(pre_shifted, 1)
                dve.wait_ge(pre_shifted, j.at((KT - 2) * n - 1))
                dve.wait_ge(w_used, b.at(1))
                dve.tensor_tensor(tile, tile, proj[g.slot][:, :], ALU.add).then_inc(proj_free[g.slot], 1)

            def take_shift(n):
                dve.wait_ge(shift_done, n + 1)
                dve.tensor_scalar(shift[:, :], sc[0][:, :], 1.0 / P, None, ALU.mult).then_inc(shift_out, 1)
                dve.wait_ge(shift_out, n + 1)

            def moments(n):
                dve.wait_ge(stat_done, 2 * n + 1)
                dve.tensor_scalar(ln_mean[:, :], sc[0][:, 0:TT], 1.0 / D, None, ALU.mult).then_inc(ln_step, 1)
                dve.wait_ge(ln_step, 5 * n + 1)
                dve.tensor_tensor(ln_var[:, :], ln_mean[:, :], ln_mean[:, :], ALU.mult).then_inc(ln_step, 1)
                dve.wait_ge(ln_step, 5 * n + 2)
                dve.wait_ge(stat_done, 2 * n + 2)
                dve.scalar_tensor_tensor(out=ln_var[:, :], in0=sc[1][:, 0:TT], scalar=1.0 / D, in1=ln_var[:, :],
                                         op0=ALU.mult, op1=ALU.subtract).then_inc(ln_step, 1)
                dve.wait_ge(ln_root, n + 1)
                dve.reciprocal(ln_rstd[:, :], ln_sqrt[:, :]).then_inc(ln_step, 1)
                dve.wait_ge(ln_step, 5 * n + 4)
                dve.tensor_tensor(ln_move[:, :], ln_mean[:, :], ln_rstd[:, :], ALU.mult).then_inc(ln_step, 1)

            def finish(n, between={}):
                def move(k):
                    dve.wait_ge(spread_done, 2 * n + 2)
                    dve.wait_ge(fin_scaled, KT * n + k + 1)
                    dve.tensor_tensor(x32[:, k], x32[:, k], sc[1][:, :], ALU.subtract).then_inc(fin_moved, 1)
                dve.wait_ge(spread_done, 2 * n + 1)
                for k in range(KT):
                    dve.tensor_tensor(x32[:, k], x32[:, k], sc[0][:, :], ALU.mult).then_inc(fin_scaled, 1)
                    if k != 1:
                        move(max(k - 1, 0))
                    for other in between.get(k, ()):
                        other()
                move(KT - 1)

            def result_stats(j):
                dve.wait_ge(tr_free, j.at(T_OUT + 1))
                for t in range(TT):
                    last = dve.bn_stats(y_stats[:, t, bass.ds(j.at(), 1), :].rearrange("p a s -> p (a s)"),
                                        y_nat[:, t, bass.ds(j.at(0, P), P)])
                last.then_inc(y_counted, 1)

            def feed_forward(layer):
                for half in range(2):
                    def up(tile):
                        b, g = tile.plus(B_UP[layer][half]), tile.plus(G_UP[layer][half])
                        h = tile.plus((2 * layer + half) * FT)
                        if half or tile.trip is not None:
                            prepare(b.plus(1))
                        elif tile.base == 0:
                            prepare(b.plus(2))
                        dve.wait_ge(proj_free[g.slot], g.half(2))
                        raw, here = h_raw[:, tile.slot:tile.slot + 1, :], bass.ds(tile.at(), 1)
                        wide = relu[:, tile.slot:tile.slot + 1, :]
                        dve.tensor_tensor(raw, wide, wide, ALU.mult).then_inc(relu_sq, 1)
                        dve.wait_ge(relu_sq, h.at(1))
                        dve.wait_ge(h_hi_ready, h.at(1))
                        rest(h_lo[:, here, :], raw, h_hi[:, here, :]).then_inc(h_ready, 1)
                    up(Pos(0))
                    up(Pos(1))
                    with dve.Fori(0, FT // 2 - 1) as i:
                        up(Pos(2, i, 2))
                        up(Pos(3, i, 2))
                    b, g, n = B_DN[layer][half], G_DN[layer][half], 2 * layer + 1
                    if not half:
                        with dve.Fori(0, KT // 2) as i:
                            for j in range(2):
                                for c in range(2):
                                    prepare(Pos(b + 2 * j + c + 1, i, 4))
                                residual(n, Pos(b + 2 * j + 1, i, 4), Pos(g + j, i, 2), Pos(j, i, 2))
                        continue
                    if layer:
                        for c in range(2):
                            prepare(Pos(b + c + 1))
                        residual(n, Pos(b + 1), Pos(g), Pos(0), False, y_in[:, 0, :])
                        with dve.Fori(0, KT // 2 - 1) as i:
                            for j in range(2):
                                for c in range(2):
                                    prepare(Pos(b + 3 + 2 * j + c, i, 4))
                                residual(n, Pos(b + 3 + 2 * j, i, 4), Pos(g + 1 + j, i, 2), Pos(1 + j, i, 2), False,
                                         y_in[:, 1 - j, :])
                                result_stats(Pos(j, i, 2))
                        prepare(Pos(b + 2 * KT - 1))
                        result_stats(Pos(KT - 2))
                        residual(n, Pos(b + 2 * KT - 1), Pos(g + KT - 1), Pos(KT - 1), False, y_in[:, 1, :])
                        result_stats(Pos(KT - 1))
                        continue
                    for j in range(2):
                        for c in range(2):
                            prepare(Pos(b + 2 * j + c + 1))
                        residual(n, Pos(b + 2 * j + 1), Pos(g + j), Pos(j), False)
                    take_shift(n)
                    shift_tiles(n, g)
                    with dve.Fori(0, KT // 2 - 2) as i:
                        for j in range(2, 4):
                            for c in range(2):
                                prepare(Pos(b + 2 * j + c + 1, i, 4))
                            shifted_residual(n, Pos(b + 2 * j + 1, i, 4), Pos(g + j, i, 2), Pos(j, i, 2), False)
                    for j in range(6, KT):
                        for c in range(2):
                            prepare(Pos(b + 2 * j + c + 1))
                        shifted_residual(n, Pos(b + 2 * j + 1), Pos(g + j), Pos(j), False)

            def out_projection(layer):
                b, g, n = B_WO[layer], G_WO[layer], 2 * layer
                for j in range(KT):
                    if j == 2:
                        take_shift(n)
                        shift_tiles(n, g)
                    if j < 2:
                        residual(n, Pos(b + j), Pos(g + j), Pos(j))
                    else:
                        shifted_residual(n, Pos(b + j), Pos(g + j), Pos(j))
                    if j < KT - 1:
                        prepare(Pos(b + j + 2))
                    if layer == 0 and 2 <= j < 6:
                        memory_lo(1, j - 2)

            dve.memset(ones_f[:, :], 1.0).then_inc(const_r, 1)
            dve.memset(ones_r[:, :].bitcast(F32), 1.0).then_inc(const_r, 1)
            prepare(Pos(0))
            for n in range(4):
                memory_lo(0, n)
            for c in range(4):
                prepare(Pos(c + 1))
                if c < 2:
                    memory_keys(0, c)
                for k in (2 * c, 2 * c + 1):
                    dve.wait_ge(tr_done, T_X + k + 1)
                    dve.tensor_copy(x32[:, k], tr[(T_X + k) % 2][:, :]).then_inc(tr_free, 1)
            memory_values(0)
            def natural_v(j):
                dve.wait_ge(tr_done, j.at(T_AV + 1))
                dve.tensor_copy(z_nat[:, :, bass.ds(j.at(0, P), P)],
                                tr[(T_AV + j.base) % 2][:, :].rearrange("p (t c) -> p t c", t=TT)).then_inc(tr_free, 1)

            prepare(Pos(B_AV + 1))
            with dve.Fori(0, PAIRS // 2 - 1) as i:
                for c in range(2):
                    prepare(Pos(B_AV + c + 2, i, 2))
                    natural_v(Pos(c, i, 2))
            prepare(Pos(B_AV + PAIRS))
            natural_v(Pos(PAIRS - 2))
            for c in range(MEMPAIRS):
                prepare(Pos(B_AQ + c + 1))
                if c == 1:
                    for n in range(3):
                        four = slice(4 * n, 4 * n + 4)
                        turned_lo(Pos(T_WS + n), Pos(H_WS + n), ws_lo[:, four], ws_hi[:, four],
                                  tr[(T_WS + n) % 2][:, :].rearrange("p (h t) -> p h t", h=4))
                projected(Pos(G_AQ + c), Pos(Q_AQ + c), qm_lo[:, c, :], qm_hi[:, c, :], SCALE)
                if c == 0:
                    natural_v(Pos(PAIRS - 1))
                    dve.wait_ge(tr_done, T_PAR + 1)
                    dve.tensor_copy(par[:, :], tr[T_PAR % 2][:, 0:64]).then_inc(tr_free, 1)
                gate_stats(2 * c)
                gate_stats(2 * c + 1)
            def gate_lo(j):
                dve.wait_ge(z_hi_ready, j + 1)
                rest(z_lo[:, j % 2], z_nat[:, :, j * P:(j + 1) * P], z_hi[:, j % 2]).then_inc(z_ready, 1)

            pair_step(Pos(STEP_A), Pos(B_AU), Pos(G_AU))
            gate_lo(0)
            gate_lo(1)
            pair_step(Pos(STEP_A + 1), Pos(B_AU + 3), Pos(G_AU + 3))
            dve.wait_ge(sgu_landed, 64)
            for j in range(PAIRS + 1):
                if j == 2:
                    prepare(Pos(B_WO[0] + 1))
                for c in range(2):
                    if j == PAIRS:
                        break
                    dve.wait_ge(sgu_done, 2 * j + c + 1)
                    wait(dve, sgu_ready, 2 * (j - 2) + c + 1)
                    mixed = sc[c][:, :].rearrange("p (n h t) -> p n h t", n=2, h=2)
                    for head in range(2):
                        rows = slice(head * HALF, (head + 1) * HALF)
                        last = dve.tensor_tensor(gated(j, c)[rows].rearrange("p (n t) -> p n t", n=2), mixed[rows, :, head],
                                                 bs_all[rows, j:j + 1, :].broadcast_to([HALF, 2, P]), ALU.add)
                    last.then_inc(sgu_added, 1)
                if 0 < j < PAIRS - 1:
                    gate_lo(j + 1)
                for c in range(2):
                    if j:
                        cols = slice(c * 2 * P, (c + 1) * 2 * P)
                        dve.wait_ge(sgu_hi, 2 * (j - 1) + c + 1)
                        rest(mix_lo[:, j - 1, cols], gated(j - 1, c), mix_hi[:, j - 1, cols]).then_inc(sgu_ready, 1)
            out_projection(0)
            prepare(Pos(27))
            moments(0)
            finish(0, {3: (lambda: memory_keys(1, 0), lambda: prepare(Pos(28))),
                       5: (lambda: memory_keys(1, 1), lambda: prepare(Pos(29)))})
            feed_forward(0)
            prepare(Pos(B_MEM[1][3]))
            moments(1)
            finish(1, {2: (lambda: prepare(Pos(B_BQ)),), 5: (lambda: prepare(Pos(B_BQ + 1)),)})

            for c in range(MEMPAIRS):
                if c:
                    prepare(Pos(B_BQ + c + 1))
                projected(Pos(G_BQ + c), Pos(Q_BQ + c), qm_lo[:, c, :], qm_hi[:, c, :], SCALE)
            dve.wait_ge(f_done, 1)
            dve.tensor_copy(f_turned[0:HEADS, :], pv[1][0:HEADS, :]).then_inc(f_out, 1)
            memory_values(1)
            dve.wait_ge(f_done, 2)
            dve.tensor_tensor(f_log[:, :, :], pv[1][:, 0:TT * HEADS].rearrange("p (t h) -> p t h", t=TT),
                              bf_row[:, :].rearrange("p (a h) -> p a h", a=1).broadcast_to([P, TT, HEADS]), ALU.add).then_inc(f_step, 1)
            dve.wait_ge(f_step, 1)
            dve.scalar_tensor_tensor(out=f_abs[:, :, :], in0=f_log[:, :, :], scalar=-1.0, in1=f_log[:, :, :],
                                     op0=ALU.mult, op1=ALU.min).then_inc(f_step, 1)
            dve.tensor_scalar(f_neg[:, :, :], f_log[:, :, :], -1.0, 0.0, ALU.mult, ALU.max).then_inc(f_step, 1)
            dve.wait_ge(f_step, 3)
            dve.wait_ge(f_act, 2)
            dve.tensor_tensor(f_sp[:, :, :], f_ln[:, :, :], f_neg[:, :, :], ALU.add).then_inc(f_step, 1)
            dve.wait_ge(f_step, 4)
            dve.wait_ge(lf_zeroed, 2)
            dve.wait_ge(f_act, 3)
            for r in range(0, P, 32):
                last = rest(lf_lo[:, :, r:r + HEADS], f_sp[:, :, :], lf_hi[:, :, r:r + HEADS])
            last.then_inc(f_step, 1)
            pair_step(Pos(STEP_B), Pos(B_FOX), Pos(G_FOX), Pos(Q_FOX), values=Pos(0))
            dve.wait_ge(f_act, 4)
            for r in (32, 96):
                last = rest(cum[r:r + 32, :], sc[0][r:r + 32, :], cum[r:r + 32, :])
            last.then_inc(f_step, 1)
            cum_rows(Pos(0))
            with dve.Fori(0, 2) as i:
                for j in range(2):
                    pair_step(Pos(STEP_FOX + j, i, 2), Pos(B_FOX + 3 * (j + 1), i, 6), Pos(G_FOX + 3 * (j + 1), i, 6),
                              Pos(Q_FOX + 2 * (j + 1), i, 4), values=Pos(j + 1, i, 2))
            pair_step(Pos(7), Pos(B_FOX + 15), Pos(G_FOX + 15), Pos(Q_FOX + 10), values=Pos(5))
            pair_step(Pos(8), late=Pos(B_WO[1] + 1))
            pair_step(Pos(STEP_LAST))
            out_projection(1)
            moments(2)
            finish(2, {4: (lambda: prepare(Pos(B_UP[1][0] + 1)),)})
            feed_forward(1)
            dve.wait_ge(y_counted, KT)
            for t in range(TT):
                last = dve.bn_aggr(y_mv[:, t], y_stats[:, t])
            last.then_inc(y_step, 1)
            dve.wait_ge(y_step, 1)
            dve.wait_ge(out_landed, 32)

            def centre(t, c):
                part = slice(c * D // 2, (c + 1) * D // 2)
                dve.scalar_tensor_tensor(out=y_nat[:, t, part], in0=y_nat[:, t, part], scalar=y_mv[:, t, 0:1],
                                         in1=g_out[:, part], op0=ALU.subtract, op1=ALU.mult).then_inc(y_centred, 1)
            centre(0, 0)
            dve.wait_ge(y_rooted, 1)
            dve.reciprocal(y_rstd[:, :], y_root[:, :]).then_inc(y_step, 1)
            dve.wait_ge(y_step, 2)
            dve.scalar_tensor_tensor(out=y_move[:, :], in0=y_mv[:, :, 0], scalar=-1.0, in1=y_rstd[:, :],
                                     op0=ALU.mult, op1=ALU.mult).then_inc(y_step, 1)
            parts = [(t, c) for t in range(TT - 1) for c in range(2)]
            for n, (t, c) in enumerate(parts):
                if n + 1 < len(parts):
                    centre(*parts[n + 1])
                part = slice(c * D // 2, (c + 1) * D // 2)
                dve.wait_ge(y_centred, n + 1)
                dve.scalar_tensor_tensor(out=y_nat[:, t, part], in0=y_nat[:, t, part], scalar=y_rstd[:, t:t + 1],
                                         in1=b_out[:, part], op0=ALU.mult, op1=ALU.add).then_inc(y_done, 1)

        @block.gpsimd
        def _(pool):
            steps = [0]

            def behind(instruction):
                steps[0] += 1
                instruction.then_inc(pool_step, 1)
                pool.wait_ge(pool_step, steps[0])

            def trunk_lo(n, k):
                pool.wait_ge(x_hi_ready, KT * n + k + 1)
                if n:
                    pool.wait_ge(fin_ready, KT * (n - 1) + k + 1)
                pool.tensor_tensor(x_lo[:, k], x32[:, k], x_hi[:, k].bitcast(F32), ALU.subtract).then_inc(x_ready, 1)

            pool.memset(eps[:, :], LN_EPS)
            behind(pool.memset(ident[:, :], 0.0))
            pool.affine_select(out=ident[:, :], in_=ident[:, :], compare_op=ALU.not_equal, fill=1.0, base=0,
                               pattern=[[-1, P]], channel_multiplier=1).then_inc(const_ready, 1)
            behind(pool.memset(causal[:, :], 0.0))
            pool.affine_select(out=causal[:, :], in_=causal[:, :], compare_op=ALU.is_ge, fill=MASKED, base=0,
                               pattern=[[-1, P]], channel_multiplier=1).then_inc(const_ready, 1)
            behind(pool.memset(tri_f[:, :], 1.0))
            pool.affine_select(out=tri_f[:, :], in_=tri_f[:, :], compare_op=ALU.is_ge, fill=0.0, base=0,
                               pattern=[[1, T]], channel_multiplier=-1).then_inc(const_ready, 1)
            for k in range(KT):
                trunk_lo(0, k)
            pool.wait_ge(ws_landed, 16)
            pool.affine_select(out=ws_raw[:, :, :], in_=ws_raw[:, :, :], compare_op=ALU.is_ge, fill=0.0, base=0,
                               pattern=[[0, HEADS], [-1, P]], channel_multiplier=1).then_inc(ws_masked, 1)
            behind(pool.memset(head_rows[:, :], 0.0))
            for n, row in enumerate((0, 32, 65, 97)):
                last = pool.affine_select(out=head_rows[:, :], in_=head_rows[:, :], compare_op=ALU.not_equal, fill=1.0,
                                          base=-row, pattern=[[-2, PAIRS]], channel_multiplier=1)
                if n < 3:
                    behind(last)
            last.then_inc(const_ready, 1)
            pool.wait_ge(wf_landed, 32)
            pool.tensor_copy(wf_hi[:, :, :], wf_raw[:, :, :]).then_inc(wf_hi_ready, 1)
            pool.wait_ge(wf_hi_ready, 1)
            pool.tensor_tensor(wf_lo[:, :, :], wf_raw[:, :, :], wf_hi[:, :, :].bitcast(F32), ALU.subtract).then_inc(wf_ready, 1)

            pool.wait_ge(sgu_landed, 64)
            for n in range(TT):
                pool.wait_ge(zn_ready, n + 1)
                pool.tensor_tensor(z_nat[:, n], z_nat[:, n], g_all[:, :], ALU.mult).then_inc(zg_step, 1)
                pool.wait_ge(zg_step, n + 1)
                pool.tensor_tensor(z_nat[:, n], z_nat[:, n], b_all[:, :], ALU.add).then_inc(zg_ready, 1)
            for j in range(PAIRS):
                for c in range(2):
                    pool.wait_ge(sgu_added, 2 * j + c + 1)
                    pool.wait_ge(u_ready, j + 1)
                    pool.tensor_tensor(gated(j, c), gated(j, c), u_t[:, j, c * 2 * P:(c + 1) * 2 * P], ALU.mult)\
                        .then_inc(sgu_gated, 1)

            def tile_there(n, j, g):
                if j.base < 2 and j.trip is None:
                    pool.wait_ge(shifted, 2 * n + j.base + 1)
                else:
                    pool.wait_ge(proj_free[g.slot], g.half(2))

            def add_tile(n, j, g):
                own = (KT - 2) * n
                first = j.base == 1
                tile_there(n, j, g)
                for source, added, sums, other in ((x32_tile(j), sum_added, total, x32[:, 0]),
                                                   (square[:, j.slot, :], sq_added, total_sq, square[:, 0])):
                    if sums is total_sq:
                        pool.wait_ge(sq_ready, j.at(KT * n + 1))
                    if not first:
                        pool.wait_ge(added, j.at(own - 1))
                    pool.tensor_tensor(sums[:, :], other if first else sums[:, :], source, ALU.add).then_inc(added, 1)

            def layer_norm(n):
                g = G_DN[n // 2][1] if n % 2 else G_WO[n // 2]
                tile_there(n, Pos(0), Pos(g))
                add_tile(n, Pos(1), Pos(g + 1))
                with pool.Fori(0, 2) as i:
                    for j in range(2, 4):
                        add_tile(n, Pos(j, i, 2), Pos(g + j, i, 2))
                add_tile(n, Pos(6), Pos(g + 6))
                for k in range(KT):
                    trunk_lo(n + 1, k)
                if n == 1:
                    for part in (lf_hi, lf_lo):
                        pool.memset(part[:, :, :].bitcast(F32), 0.0).then_inc(lf_zeroed, 1)

            for n in range(3):
                layer_norm(n)
            pool.wait_ge(out_landed, 32)
            for c in range(2):
                part = slice(c * D // 2, (c + 1) * D // 2)
                own = y_nat[:, TT - 1, part]
                pool.wait_ge(y_scaled, c + 1)
                pool.tensor_tensor(own, own, g_out[:, part], ALU.mult).then_inc(y_gained, 1)
                pool.wait_ge(y_gained, c + 1)
                pool.tensor_tensor(own, own, b_out[:, part], ALU.add).then_inc(y_last, 1)


_INS = ["x", "mem", "a_w_in", "a_sgu_ln_g", "a_sgu_ln_b", "a_w_s", "a_b_s", "kv_w", "kv_b_f", "b_w_q",
        "mem_w_kv", "w_o", "ln_g", "ln_b", "w_up", "w_down"]


def kernel(**inputs):
    import numpy as np
    import concourse.bacc as bacc
    from concourse.bass_utils import run_bass_kernel_spmd

    nc = bacc.Bacc("TRN2", target_bir_lowering=False, num_devices=1)
    arrays, args = {}, []
    for name in _INS:
        a = np.ascontiguousarray(inputs[name])
        arrays[f"in_{name}"] = a
        args.append(nc.dram_tensor(f"in_{name}", a.shape, mybir.dt.from_np(a.dtype), kind="ExternalInput").ap())
    out = nc.dram_tensor("out_y", inputs["x"].shape, F32, kind="ExternalOutput").ap()
    trunk_kernel(nc, *args, out)
    result = run_bass_kernel_spmd(nc, [arrays], core_ids=[0])
    return result.results[0]["out_y"]
```
